# Optimizing a Trainium2 kernel written in Bass

```python
import math
import jax, jax.numpy as jnp
from jax import lax
import numpy as np

D_MODEL = 1024
BATCH = 1
SEQ = 256
DEPTH = 1

POOL_WINDOWS = (2, 4, 8, 16)
N_POOL_GROUPS = len(POOL_WINDOWS)
POOL_WIDTH = D_MODEL // 2
POOL_GROUP = POOL_WIDTH // N_POOL_GROUPS
N_HEADS = 4
HEAD_DIM = D_MODEL // 16
V_HEAD_DIM = 2 * HEAD_DIM
QK_WIDTH = N_HEADS * 2 * HEAD_DIM
ATTN_WIDTH = N_HEADS * V_HEAD_DIM
Q_BLOCK = 128
OFF_POOL = 0
OFF_Q = OFF_POOL + POOL_WIDTH
OFF_K = OFF_Q + QK_WIDTH
OFF_V = OFF_K + QK_WIDTH
OFF_GP = OFF_V + ATTN_WIDTH
OFF_GA = OFF_GP + D_MODEL
IN_WIDTH = OFF_GA + D_MODEL
N_GROUPS = 4
EXPERTS_PER_GROUP = 8
N_EXPERTS = N_GROUPS * EXPERTS_PER_GROUP
TOP_K = 2
D_EXPERT = D_MODEL // 2
ROW_BLOCK = 512
EPS = 1e-6


def rmsnorm(x, g):
    xf = x.astype(jnp.float32)
    y = xf * lax.rsqrt(jnp.mean(xf * xf, axis=-1, keepdims=True) + EPS)
    return (y * g.astype(jnp.float32)).astype(x.dtype)

def lambda_init(layer):
    return 0.8 - 0.6 * math.exp(-0.3 * layer)

def alibi_slopes():
    return jnp.asarray([2.0 ** (-8.0 * (h + 1) / N_HEADS) for h in range(N_HEADS)], jnp.float32)

def pool_mixer(u, w_grp, scale):
    B, S, C = u.shape
    uf = u.astype(jnp.float32)
    c0 = jnp.concatenate([jnp.zeros((B, 1, C), jnp.float32), jnp.cumsum(uf, axis=1)], axis=1)
    t = jnp.arange(S)
    outs = []
    for g, w in enumerate(POOL_WINDOWS):
        sl = slice(g * POOL_GROUP, (g + 1) * POOL_GROUP)
        cg = c0[:, :, sl]
        upper = cg[:, 1:]
        lower = jnp.pad(cg[:, :S + 1 - w], ((0, 0), (w - 1, 0), (0, 0)))
        cnt = jnp.minimum(t + 1, w).astype(jnp.float32)[None, :, None]
        outs.append((upper - lower) / cnt - uf[:, :, sl])
    d = jnp.stack(outs, axis=2).astype(u.dtype)
    y = jnp.einsum('bsgc,gcd->bsgd', d, w_grp).reshape(B, S, POOL_WIDTH)
    return y * scale

def diff_attention(q, k, v, q_g, k_g, lam, subln_g, lam_init):
    B, S = q.shape[0], q.shape[1]
    qf = rmsnorm(q.astype(jnp.float32), q_g) * (HEAD_DIM ** -0.5)
    kf = rmsnorm(k.astype(jnp.float32), k_g)
    slopes = alibi_slopes()
    nb = S // Q_BLOCK
    kpos = jnp.arange(S)
    qb = qf.reshape(B, nb, Q_BLOCK, N_HEADS, 2, HEAD_DIM).transpose(1, 0, 2, 3, 4, 5)

    def block(args):
        qblk, i = args
        qpos = i * Q_BLOCK + jnp.arange(Q_BLOCK)
        dist = (qpos[:, None] - kpos[None, :]).astype(jnp.float32)
        bias = jnp.where(dist[None] >= 0, -slopes[:, None, None] * dist[None], -jnp.inf)
        s = jnp.einsum('bqhmd,bkhmd->bhmqk', qblk, kf) + bias[None, :, None]
        p = jax.nn.softmax(s, axis=-1)
        a = p[:, :, 0] - lam * p[:, :, 1]
        return jnp.einsum('bhqk,bkhe->bqhe', a.astype(v.dtype), v)

    o = lax.map(block, (qb, jnp.arange(nb)))
    o = o.transpose(1, 0, 2, 3, 4).reshape(B, S, N_HEADS, V_HEAD_DIM)
    o = rmsnorm(o, subln_g) * (1.0 - lam_init)
    return o.reshape(B, S, ATTN_WIDTH)

def hier_moe(hn, w_rg, b_rg, w_re, b_re, w_gate, w_up, w_down):
    N, D = hn.shape
    pg = jax.nn.softmax((hn @ w_rg).astype(jnp.float32) + b_rg.astype(jnp.float32), axis=-1)
    p_top, g_idx = lax.top_k(pg, 1)
    le = ((hn @ w_re).astype(jnp.float32) + b_re.astype(jnp.float32)).reshape(N, N_GROUPS, EXPERTS_PER_GROUP)
    le_sel = jnp.take_along_axis(le, g_idx[:, :, None], axis=1)[:, 0]
    pe = jax.nn.softmax(le_sel, axis=-1)
    pv, e_idx = lax.top_k(pe, TOP_K)
    wts = p_top * pv / jnp.sum(pv, axis=-1, keepdims=True)
    eid = (g_idx * EXPERTS_PER_GROUP + e_idx).reshape(-1)
    tok = jnp.repeat(jnp.arange(N, dtype=jnp.int32), TOP_K)
    wflat = wts.reshape(-1)
    M = N * TOP_K
    order = jnp.argsort(eid)
    s_eid, s_tok, s_w = eid[order], tok[order], wflat[order]
    counts = jnp.bincount(eid, length=N_EXPERTS)
    padded = (counts + ROW_BLOCK - 1) // ROW_BLOCK * ROW_BLOCK
    pend = jnp.cumsum(padded)
    pstart = pend - padded
    start = jnp.cumsum(counts) - counts
    dest = pstart[s_eid] + jnp.arange(M) - start[s_eid]
    n_blocks = -(-M // ROW_BLOCK) + N_EXPERTS
    P = n_blocks * ROW_BLOCK
    slot_tok = jnp.zeros((P,), jnp.int32).at[dest].set(s_tok)
    slot_w = jnp.zeros((P,), jnp.float32).at[dest].set(s_w)
    block_eid = jnp.minimum(jnp.searchsorted(pend, jnp.arange(n_blocks) * ROW_BLOCK, side='right'), N_EXPERTS - 1)

    def expert_block(args):
        toks, wb, e = args
        xb = hn[toks]
        hdn = jax.nn.silu(xb @ w_gate[e]) * (xb @ w_up[e])
        return (hdn @ w_down[e]) * wb[:, None].astype(hn.dtype)

    yb = lax.map(expert_block, (slot_tok.reshape(n_blocks, ROW_BLOCK), slot_w.reshape(n_blocks, ROW_BLOCK), block_eid))
    return jnp.zeros((N, D), hn.dtype).at[slot_tok].add(yb.reshape(P, D))

def first_inputs(seed: int = 0) -> dict:
    key = jax.random.key(seed)
    ks = jax.random.split(key, 24)
    f32 = jnp.float32
    nrm = lambda k, shape, fan: jax.random.normal(k, shape, f32) * (fan ** -0.5)
    gain = lambda k, shape: 1.0 + 0.02 * jax.random.normal(k, shape, f32)
    L = DEPTH
    return {
        "x": jax.random.normal(ks[0], (BATCH, SEQ, D_MODEL), f32),
        "norm1_g": gain(ks[1], (L, D_MODEL)),
        "w_in": nrm(ks[2], (L, D_MODEL, IN_WIDTH), D_MODEL),
        "pool_w": nrm(ks[3], (L, N_POOL_GROUPS, POOL_GROUP, POOL_GROUP), POOL_GROUP),
        "pool_scale": gain(ks[4], (L, POOL_WIDTH)),
        "w_pool_up": nrm(ks[5], (L, POOL_WIDTH, D_MODEL), POOL_WIDTH),
        "q_norm_g": gain(ks[6], (L, HEAD_DIM)),
        "k_norm_g": gain(ks[7], (L, HEAD_DIM)),
        "lambda_q1": 0.1 * jax.random.normal(ks[8], (L, HEAD_DIM), f32),
        "lambda_k1": 0.1 * jax.random.normal(ks[9], (L, HEAD_DIM), f32),
        "lambda_q2": 0.1 * jax.random.normal(ks[10], (L, HEAD_DIM), f32),
        "lambda_k2": 0.1 * jax.random.normal(ks[11], (L, HEAD_DIM), f32),
        "subln_g": gain(ks[12], (L, V_HEAD_DIM)),
        "w_attn_up": nrm(ks[13], (L, ATTN_WIDTH, D_MODEL), ATTN_WIDTH),
        "w_out": nrm(ks[14], (L, D_MODEL, D_MODEL), D_MODEL),
        "norm2_g": gain(ks[15], (L, D_MODEL)),
        "w_router_group": nrm(ks[16], (L, D_MODEL, N_GROUPS), D_MODEL),
        "b_router_group": 0.01 * jax.random.normal(ks[17], (L, N_GROUPS), f32),
        "w_router_expert": nrm(ks[18], (L, D_MODEL, N_EXPERTS), D_MODEL),
        "b_router_expert": 0.01 * jax.random.normal(ks[19], (L, N_EXPERTS), f32),
        "w_expert_gate": nrm(ks[20], (L, N_EXPERTS, D_MODEL, D_EXPERT), D_MODEL),
        "w_expert_up": nrm(ks[21], (L, N_EXPERTS, D_MODEL, D_EXPERT), D_MODEL),
        "w_expert_down": nrm(ks[22], (L, N_EXPERTS, D_EXPERT, D_MODEL), D_EXPERT),
    }

def first_block(x, norm1_g, w_in, pool_w, pool_scale, w_pool_up, q_norm_g, k_norm_g, lambda_q1, lambda_k1,
              lambda_q2, lambda_k2, subln_g, w_attn_up, w_out, norm2_g, w_router_group, b_router_group,
              w_router_expert, b_router_expert, w_expert_gate, w_expert_up, w_expert_down):
    B, S, D = x.shape
    for l in range(DEPTH):
        lam_init = lambda_init(l)
        h = rmsnorm(x, norm1_g[l])
        proj = h @ w_in[l]
        u = proj[..., OFF_POOL:OFF_Q]
        q = proj[..., OFF_Q:OFF_K].reshape(B, S, N_HEADS, 2, HEAD_DIM)
        k = proj[..., OFF_K:OFF_V].reshape(B, S, N_HEADS, 2, HEAD_DIM)
        v = proj[..., OFF_V:OFF_GP].reshape(B, S, N_HEADS, V_HEAD_DIM)
        gate_p = jax.nn.sigmoid(proj[..., OFF_GP:OFF_GA])
        gate_a = jax.nn.sigmoid(proj[..., OFF_GA:IN_WIDTH])
        pool_out = pool_mixer(u, pool_w[l], pool_scale[l]) @ w_pool_up[l]
        lam = (jnp.exp(jnp.sum(lambda_q1[l].astype(jnp.float32) * lambda_k1[l].astype(jnp.float32)))
               - jnp.exp(jnp.sum(lambda_q2[l].astype(jnp.float32) * lambda_k2[l].astype(jnp.float32))) + lam_init)
        attn_out = diff_attention(q, k, v, q_norm_g[l], k_norm_g[l], lam, subln_g[l], lam_init) @ w_attn_up[l]
        x = x + (gate_p * pool_out + gate_a * attn_out) @ w_out[l]
        hn = rmsnorm(x, norm2_g[l]).reshape(B * S, D)
        x = x + hier_moe(hn, w_router_group[l], b_router_group[l], w_router_expert[l], b_router_expert[l],
                         w_expert_gate[l], w_expert_up[l], w_expert_down[l]).reshape(B, S, D)
    return x


DEPTH_2 = 2

NUM_MIXERS = 4
RMS_EPS = 1e-6
ROPE_THETA = 500000.0
ATTN_BLOCK = 128

SSM_D_INNER = 2 * D_MODEL
SSM_HEAD_DIM = 64
SSM_N_HEADS = SSM_D_INNER // SSM_HEAD_DIM
SSM_D_STATE = 128
SSM_N_GROUPS = 8
SSM_CONV = 4
SSM_CHUNK = 128
SSM_BC_DIM = SSM_N_GROUPS * SSM_D_STATE
SSM_CONV_DIM = SSM_D_INNER + 2 * SSM_BC_DIM
SSM_IN_COLS = SSM_D_INNER + SSM_CONV_DIM + SSM_N_HEADS
SSM_DT_MIN = 0.001
SSM_DT_MAX = 0.1

MLA_N_HEADS = 16
MLA_Q_LORA = 3 * D_MODEL // 8
MLA_KV_LORA = D_MODEL // 4
MLA_NOPE_DIM = 128
MLA_ROPE_DIM = 64
MLA_V_DIM = 128
MLA_QK_DIM = MLA_NOPE_DIM + MLA_ROPE_DIM
MLA_WIDTH = MLA_N_HEADS * MLA_V_DIM
MLA_IN_COLS = MLA_Q_LORA + MLA_KV_LORA + MLA_ROPE_DIM + MLA_WIDTH

FOX_N_HEADS = 16
FOX_HEAD_DIM = 128
FOX_WIDTH = FOX_N_HEADS * FOX_HEAD_DIM
FOX_IN_COLS = 3 * FOX_WIDTH + FOX_N_HEADS + FOX_WIDTH
FOX_F_BIAS_MEAN = 3.0

DIL_CONFIGS = ((128, 1), (512, 4), (2048, 16))
DIL_N_HEADS = 8
DIL_HEAD_DIM = 128
DIL_WIDTH = DIL_N_HEADS * DIL_HEAD_DIM
DIL_ROPE_DIM = DIL_HEAD_DIM // 4
DIL_IN_COLS = 3 * len(DIL_CONFIGS) * DIL_WIDTH + DIL_WIDTH

N_SSM_LAYERS = (DEPTH_2 + 3) // NUM_MIXERS
N_MLA_LAYERS = (DEPTH_2 + 2) // NUM_MIXERS
N_FOX_LAYERS = (DEPTH_2 + 1) // NUM_MIXERS
N_DIL_LAYERS = DEPTH_2 // NUM_MIXERS


def rms_norm(x, w):
    xf = x.astype(jnp.float32)
    return (xf * lax.rsqrt(jnp.mean(xf * xf, axis=-1, keepdims=True) + RMS_EPS)).astype(x.dtype) * w

def rope(x, positions):
    half = x.shape[-1] // 2
    inv_freq = ROPE_THETA ** (-jnp.arange(half, dtype=jnp.float32) / half)
    ang = positions.astype(jnp.float32)[:, None] * inv_freq[None, :]
    cos = jnp.cos(ang)[None, :, None, :]
    sin = jnp.sin(ang)[None, :, None, :]
    x1 = x[..., :half].astype(jnp.float32)
    x2 = x[..., half:].astype(jnp.float32)
    return jnp.concatenate([x1 * cos - x2 * sin, x2 * cos + x1 * sin], axis=-1).astype(x.dtype)

def partial_rope(x, positions):
    return jnp.concatenate([rope(x[..., :DIL_ROPE_DIM], positions), x[..., DIL_ROPE_DIM:]], axis=-1)

def causal_depthwise_conv(x, w, b):
    k = w.shape[0]
    y = lax.conv_general_dilated(x, w[:, None, :], window_strides=(1,), padding=[(k - 1, 0)],
                                 dimension_numbers=('NWC', 'WIO', 'NWC'), feature_group_count=x.shape[-1])
    return y + b

def gated_group_rms_norm(y, z, w, groups):
    g = y * jax.nn.silu(z.astype(jnp.float32))
    shp = g.shape
    gg = g.reshape(shp[:-1] + (groups, shp[-1] // groups))
    gg = gg * lax.rsqrt(jnp.mean(gg * gg, axis=-1, keepdims=True) + RMS_EPS)
    return gg.reshape(shp) * w

def ssd_chunked(xdt, a, b_in, c_out):
    bsz, seq, heads, p = xdt.shape
    g, n = b_in.shape[2], b_in.shape[3]
    r = heads // g
    t = SSM_CHUNK
    nc = seq // t
    xc = xdt.reshape(bsz, nc, t, g, r, p)
    bc = b_in.reshape(bsz, nc, t, g, n)
    cc = c_out.reshape(bsz, nc, t, g, n)
    a_cum = jnp.cumsum(a.reshape(bsz, nc, t, g, r).transpose(0, 3, 4, 1, 2), axis=-1)
    causal = jnp.tril(jnp.ones((t, t), dtype=bool))
    seg = a_cum[..., :, None] - a_cum[..., None, :]
    decay_in = jnp.exp(jnp.where(causal, seg, -jnp.inf))
    cb = jnp.einsum('bctgn,bcsgn->bgcts', cc, bc)
    y_diag = jnp.einsum('bgcts,bgrcts,bcsgrp->bctgrp', cb, decay_in, xc)
    decay_to_end = jnp.exp(a_cum[..., -1:] - a_cum)
    chunk_states = jnp.einsum('bctgn,bgrct,bctgrp->bcgrpn', bc, decay_to_end, xc)
    chunk_decay = jnp.exp(a_cum[..., -1])

    def carry_state(state, inp):
        st, dec = inp
        return state * dec[..., None, None] + st, state

    init = jnp.zeros_like(chunk_states[:, 0])
    _, entering = lax.scan(carry_state, init,
                           (chunk_states.swapaxes(0, 1), chunk_decay.transpose(3, 0, 1, 2)))
    entering = entering.swapaxes(0, 1)
    y_off = jnp.einsum('bctgn,bcgrpn,bgrct->bctgrp', cc, entering, jnp.exp(a_cum))
    return (y_diag + y_off).reshape(bsz, seq, heads, p)

def causal_block_attention(q, k, v, scale, log_forget_cum=None):
    bsz, seq, heads, dk = q.shape
    nb = seq // ATTN_BLOCK
    key_pos = jnp.arange(seq)
    q_blocks = q.reshape(bsz, nb, ATTN_BLOCK, heads, dk).swapaxes(0, 1)
    block_ids = jnp.arange(nb)
    use_decay = log_forget_cum is not None
    if use_decay:
        c_k = log_forget_cum.astype(jnp.float32).transpose(0, 2, 1)
        c_blocks = c_k.reshape(bsz, heads, nb, ATTN_BLOCK).transpose(2, 0, 1, 3)
        xs = (q_blocks, block_ids, c_blocks)
    else:
        xs = (q_blocks, block_ids)

    def attend(args):
        qb, bi = args[0], args[1]
        s = jnp.einsum('bqhd,bkhd->bhqk', qb, k).astype(jnp.float32) * scale
        if use_decay:
            s = s + args[2][..., :, None] - c_k[:, :, None, :]
        q_pos = bi * ATTN_BLOCK + jnp.arange(ATTN_BLOCK)
        s = jnp.where(key_pos[None, :] <= q_pos[:, None], s, -jnp.inf)
        p = jax.nn.softmax(s, axis=-1)
        return jnp.einsum('bhqk,bkhd->bqhd', p.astype(v.dtype), v)

    out = lax.map(attend, xs)
    return out.swapaxes(0, 1).reshape(bsz, seq, heads, v.shape[-1])

def dilated_band_attention(q, k, v, dilation, span):
    bsz, seq, heads, dh = q.shape
    length = seq // dilation
    nseq = bsz * dilation

    def to_residue(u):
        return u.reshape(bsz, length, dilation, heads, dh).transpose(0, 2, 1, 3, 4).reshape(nseq, length, heads, dh)

    blk = min(span, length)
    nb = -(-length // blk)
    padded = nb * blk
    padw = ((0, 0), (0, padded - length), (0, 0), (0, 0))
    qs = jnp.pad(to_residue(q), padw).reshape(nseq, nb, blk, heads, dh)
    ks = jnp.pad(to_residue(k), padw).reshape(nseq, nb, blk, heads, dh)
    vs = jnp.pad(to_residue(v), padw).reshape(nseq, nb, blk, heads, dh)

    def with_prev(u):
        prev = jnp.pad(u, ((0, 0), (1, 0), (0, 0), (0, 0), (0, 0)))[:, :nb]
        return jnp.concatenate([prev, u], axis=2)

    kw, vw = with_prev(ks), with_prev(vs)
    s = jnp.einsum('nbqhd,nbkhd->nbhqk', qs, kw).astype(jnp.float32) * (dh ** -0.5)
    q_idx = jnp.arange(blk)[:, None] + blk
    k_idx = jnp.arange(2 * blk)[None, :]
    dist = q_idx - k_idx
    key_abs = (jnp.arange(nb) * blk - blk)[:, None] + jnp.arange(2 * blk)[None, :]
    valid = ((dist >= 0) & (dist <= span))[None, :, :] & (key_abs >= 0)[:, None, :]
    s = jnp.where(valid[None, :, None, :, :], s, -jnp.inf)
    m = jnp.max(s, axis=-1, keepdims=True)
    p = jnp.exp(s - m)
    den = jnp.sum(p, axis=-1)
    o = jnp.einsum('nbhqk,nbkhd->nbqhd', p, vw.astype(jnp.float32)) / den.transpose(0, 1, 3, 2)[..., None]
    lse = (m[..., 0] + jnp.log(den)).transpose(0, 1, 3, 2)
    o = o.reshape(nseq, padded, heads, dh)[:, :length]
    lse = lse.reshape(nseq, padded, heads)[:, :length]
    o = o.reshape(bsz, dilation, length, heads, dh).transpose(0, 2, 1, 3, 4).reshape(bsz, seq, heads, dh)
    lse = lse.reshape(bsz, dilation, length, heads).transpose(0, 2, 1, 3).reshape(bsz, seq, heads)
    return o, lse

def ssd_mixer(u, in_w, conv_w, conv_b, dt_bias, a_log, d_skip, norm_w, out_w):
    bsz, seq, _ = u.shape
    proj = u @ in_w
    z = proj[..., :SSM_D_INNER]
    xbc = proj[..., SSM_D_INNER:SSM_D_INNER + SSM_CONV_DIM]
    dt_raw = proj[..., SSM_D_INNER + SSM_CONV_DIM:]
    xbc = jax.nn.silu(causal_depthwise_conv(xbc, conv_w, conv_b)).astype(jnp.float32)
    xs = xbc[..., :SSM_D_INNER].reshape(bsz, seq, SSM_N_HEADS, SSM_HEAD_DIM)
    b_in = xbc[..., SSM_D_INNER:SSM_D_INNER + SSM_BC_DIM].reshape(bsz, seq, SSM_N_GROUPS, SSM_D_STATE)
    c_out = xbc[..., SSM_D_INNER + SSM_BC_DIM:].reshape(bsz, seq, SSM_N_GROUPS, SSM_D_STATE)
    dt = jax.nn.softplus(dt_raw.astype(jnp.float32) + dt_bias.astype(jnp.float32))
    a = dt * (-jnp.exp(a_log.astype(jnp.float32)))
    y = ssd_chunked(xs * dt[..., None], a, b_in, c_out)
    y = y + d_skip.astype(jnp.float32)[:, None] * xs
    y = gated_group_rms_norm(y.reshape(bsz, seq, SSM_D_INNER), z, norm_w, SSM_N_GROUPS)
    return y.astype(u.dtype) @ out_w

def mla_mixer(u, positions, in_w, q_norm_w, kv_norm_w, uq_w, ukv_w, out_w):
    bsz, seq, _ = u.shape
    proj = u @ in_w
    o1 = MLA_Q_LORA
    o2 = o1 + MLA_KV_LORA
    o3 = o2 + MLA_ROPE_DIM
    c_q, c_kv, k_r, z = proj[..., :o1], proj[..., o1:o2], proj[..., o2:o3], proj[..., o3:]
    q = (rms_norm(c_q, q_norm_w) @ uq_w).reshape(bsz, seq, MLA_N_HEADS, MLA_QK_DIM)
    kv = (rms_norm(c_kv, kv_norm_w) @ ukv_w).reshape(bsz, seq, MLA_N_HEADS, MLA_NOPE_DIM + MLA_V_DIM)
    q_nope, q_rope = q[..., :MLA_NOPE_DIM], rope(q[..., MLA_NOPE_DIM:], positions)
    k_nope, v = kv[..., :MLA_NOPE_DIM], kv[..., MLA_NOPE_DIM:]
    k_rope = rope(k_r[:, :, None, :], positions)
    q_full = jnp.concatenate([q_nope, q_rope], axis=-1)
    k_full = jnp.concatenate([k_nope, jnp.broadcast_to(k_rope, (bsz, seq, MLA_N_HEADS, MLA_ROPE_DIM))], axis=-1)
    o = causal_block_attention(q_full, k_full, v, MLA_QK_DIM ** -0.5)
    o = o.reshape(bsz, seq, MLA_WIDTH) * jax.nn.silu(z)
    return o @ out_w

def fox_mixer(u, in_w, f_bias, out_w):
    bsz, seq, _ = u.shape
    proj = u @ in_w
    w = FOX_WIDTH
    q = proj[..., :w].reshape(bsz, seq, FOX_N_HEADS, FOX_HEAD_DIM)
    k = proj[..., w:2 * w].reshape(bsz, seq, FOX_N_HEADS, FOX_HEAD_DIM)
    v = proj[..., 2 * w:3 * w].reshape(bsz, seq, FOX_N_HEADS, FOX_HEAD_DIM)
    f_logit = proj[..., 3 * w:3 * w + FOX_N_HEADS]
    z = proj[..., 3 * w + FOX_N_HEADS:]
    log_f = jax.nn.log_sigmoid(f_logit.astype(jnp.float32) + f_bias.astype(jnp.float32))
    c = jnp.cumsum(log_f, axis=1)
    o = causal_block_attention(q, k, v, FOX_HEAD_DIM ** -0.5, log_forget_cum=c)
    o = o.reshape(bsz, seq, FOX_WIDTH) * jax.nn.silu(z)
    return o @ out_w

def dilated_mixer(u, positions, in_w, out_w):
    bsz, seq, _ = u.shape
    proj = u @ in_w
    w = DIL_WIDTH
    outs, lses = [], []
    for gi, (window, dilation) in enumerate(DIL_CONFIGS):
        base = 3 * w * gi
        q = proj[..., base:base + w].reshape(bsz, seq, DIL_N_HEADS, DIL_HEAD_DIM)
        k = proj[..., base + w:base + 2 * w].reshape(bsz, seq, DIL_N_HEADS, DIL_HEAD_DIM)
        v = proj[..., base + 2 * w:base + 3 * w].reshape(bsz, seq, DIL_N_HEADS, DIL_HEAD_DIM)
        o, lse = dilated_band_attention(partial_rope(q, positions), partial_rope(k, positions), v,
                                        dilation, window // dilation)
        outs.append(o)
        lses.append(lse)
    mix = jax.nn.softmax(jnp.stack(lses, axis=0), axis=0)
    o = jnp.sum(mix[..., None] * jnp.stack(outs, axis=0), axis=0)
    z = proj[..., 3 * w * len(DIL_CONFIGS):]
    o = o.reshape(bsz, seq, w).astype(u.dtype) * jax.nn.silu(z)
    return o @ out_w

def second_inputs(seed: int = 0) -> dict:
    key = jax.random.key(seed)
    ks = iter(jax.random.split(key, 32))
    f32 = jnp.float32

    def dense(shape, fan_in):
        return jax.random.normal(next(ks), shape, f32) * (fan_in ** -0.5)

    def gain(shape):
        return 1.0 + 0.02 * jax.random.normal(next(ks), shape, f32)

    x = jax.random.normal(next(ks), (BATCH, SEQ, D_MODEL), f32)
    norm_w = gain((DEPTH_2, D_MODEL))
    final_norm_w = gain((D_MODEL,))
    ssm_in_w = dense((N_SSM_LAYERS, D_MODEL, SSM_IN_COLS), D_MODEL)
    ssm_conv_w = dense((N_SSM_LAYERS, SSM_CONV, SSM_CONV_DIM), SSM_CONV)
    ssm_conv_b = 0.02 * jax.random.normal(next(ks), (N_SSM_LAYERS, SSM_CONV_DIM), f32)
    dt0 = jnp.exp(jax.random.uniform(next(ks), (N_SSM_LAYERS, SSM_N_HEADS), f32,
                                     minval=np.log(SSM_DT_MIN), maxval=np.log(SSM_DT_MAX)))
    ssm_dt_bias = dt0 + jnp.log(-jnp.expm1(-dt0))
    ssm_A_log = jnp.log(jax.random.uniform(next(ks), (N_SSM_LAYERS, SSM_N_HEADS), f32, minval=1.0, maxval=16.0))
    ssm_D = gain((N_SSM_LAYERS, SSM_N_HEADS))
    ssm_norm_w = gain((N_SSM_LAYERS, SSM_D_INNER))
    ssm_out_w = dense((N_SSM_LAYERS, SSM_D_INNER, D_MODEL), SSM_D_INNER)
    mla_in_w = dense((N_MLA_LAYERS, D_MODEL, MLA_IN_COLS), D_MODEL)
    mla_q_norm_w = gain((N_MLA_LAYERS, MLA_Q_LORA))
    mla_kv_norm_w = gain((N_MLA_LAYERS, MLA_KV_LORA))
    mla_uq_w = dense((N_MLA_LAYERS, MLA_Q_LORA, MLA_N_HEADS * MLA_QK_DIM), MLA_Q_LORA)
    mla_ukv_w = dense((N_MLA_LAYERS, MLA_KV_LORA, MLA_N_HEADS * (MLA_NOPE_DIM + MLA_V_DIM)), MLA_KV_LORA)
    mla_out_w = dense((N_MLA_LAYERS, MLA_WIDTH, D_MODEL), MLA_WIDTH)
    fox_in_w = dense((N_FOX_LAYERS, D_MODEL, FOX_IN_COLS), D_MODEL)
    fox_f_bias = FOX_F_BIAS_MEAN + 0.5 * jax.random.normal(next(ks), (N_FOX_LAYERS, FOX_N_HEADS), f32)
    fox_out_w = dense((N_FOX_LAYERS, FOX_WIDTH, D_MODEL), FOX_WIDTH)
    dil_in_w = dense((N_DIL_LAYERS, D_MODEL, DIL_IN_COLS), D_MODEL)
    dil_out_w = dense((N_DIL_LAYERS, DIL_WIDTH, D_MODEL), DIL_WIDTH)
    return {'x': x, 'norm_w': norm_w, 'final_norm_w': final_norm_w,
            'ssm_in_w': ssm_in_w, 'ssm_conv_w': ssm_conv_w, 'ssm_conv_b': ssm_conv_b,
            'ssm_dt_bias': ssm_dt_bias, 'ssm_A_log': ssm_A_log, 'ssm_D': ssm_D,
            'ssm_norm_w': ssm_norm_w, 'ssm_out_w': ssm_out_w,
            'mla_in_w': mla_in_w, 'mla_q_norm_w': mla_q_norm_w, 'mla_kv_norm_w': mla_kv_norm_w,
            'mla_uq_w': mla_uq_w, 'mla_ukv_w': mla_ukv_w, 'mla_out_w': mla_out_w,
            'fox_in_w': fox_in_w, 'fox_f_bias': fox_f_bias, 'fox_out_w': fox_out_w,
            'dil_in_w': dil_in_w, 'dil_out_w': dil_out_w}

def second_block(x, norm_w, final_norm_w, ssm_in_w, ssm_conv_w, ssm_conv_b, ssm_dt_bias, ssm_A_log, ssm_D,
              ssm_norm_w, ssm_out_w, mla_in_w, mla_q_norm_w, mla_kv_norm_w, mla_uq_w, mla_ukv_w, mla_out_w,
              fox_in_w, fox_f_bias, fox_out_w, dil_in_w, dil_out_w):
    positions = jnp.arange(x.shape[1])
    h = x
    for i in range(DEPTH_2):
        kind, j = i % NUM_MIXERS, i // NUM_MIXERS
        u = rms_norm(h, norm_w[i])
        if kind == 0:
            y = ssd_mixer(u, ssm_in_w[j], ssm_conv_w[j], ssm_conv_b[j], ssm_dt_bias[j], ssm_A_log[j],
                          ssm_D[j], ssm_norm_w[j], ssm_out_w[j])
        elif kind == 1:
            y = mla_mixer(u, positions, mla_in_w[j], mla_q_norm_w[j], mla_kv_norm_w[j], mla_uq_w[j],
                          mla_ukv_w[j], mla_out_w[j])
        elif kind == 2:
            y = fox_mixer(u, fox_in_w[j], fox_f_bias[j], fox_out_w[j])
        else:
            y = dilated_mixer(u, positions, dil_in_w[j], dil_out_w[j])
        h = h + y.astype(h.dtype)
    return rms_norm(h, final_norm_w)


def setup_inputs(seed=0):
    out = dict(first_inputs(seed))
    for name, value in second_inputs(seed + 1).items():
        if name != "x":
            out[name + "_2"] = value
    return out


def reference(
    x, norm1_g, w_in, pool_w, pool_scale, w_pool_up, q_norm_g, k_norm_g, lambda_q1, lambda_k1,
    lambda_q2, lambda_k2, subln_g, w_attn_up, w_out, norm2_g, w_router_group, b_router_group,
    w_router_expert, b_router_expert, w_expert_gate, w_expert_up, w_expert_down, norm_w_2,
    final_norm_w_2, ssm_in_w_2, ssm_conv_w_2, ssm_conv_b_2, ssm_dt_bias_2, ssm_A_log_2, ssm_D_2,
    ssm_norm_w_2, ssm_out_w_2, mla_in_w_2, mla_q_norm_w_2, mla_kv_norm_w_2, mla_uq_w_2,
    mla_ukv_w_2, mla_out_w_2, fox_in_w_2, fox_f_bias_2, fox_out_w_2, dil_in_w_2, dil_out_w_2,
):
    x = first_block(
        x, norm1_g, w_in, pool_w, pool_scale, w_pool_up, q_norm_g, k_norm_g, lambda_q1,
        lambda_k1, lambda_q2, lambda_k2, subln_g, w_attn_up, w_out, norm2_g, w_router_group,
        b_router_group, w_router_expert, b_router_expert, w_expert_gate, w_expert_up,
        w_expert_down,
    )
    return second_block(
        x, norm_w_2, final_norm_w_2, ssm_in_w_2, ssm_conv_w_2, ssm_conv_b_2, ssm_dt_bias_2,
        ssm_A_log_2, ssm_D_2, ssm_norm_w_2, ssm_out_w_2, mla_in_w_2, mla_q_norm_w_2,
        mla_kv_norm_w_2, mla_uq_w_2, mla_ukv_w_2, mla_out_w_2, fox_in_w_2, fox_f_bias_2,
        fox_out_w_2, dil_in_w_2, dil_out_w_2,
    )


_drawn_inputs = setup_inputs


def setup_inputs(seed=0):
    import zlib

    import numpy as np

    out = dict(_drawn_inputs(seed))
    spreads = {}
    factors = {'q_norm_g': 3.627,
     'k_norm_g': 5.664,
     'lambda_k1': 8.0,
     'lambda_q2': 8.0,
     'subln_g': 6.114,
     'b_router_group': 5.578,
     'b_router_expert': 3.218,
     'norm_w_2': 2.897,
     'final_norm_w_2': 2.869,
     'ssm_conv_b_2': 3.236,
     'ssm_D_2': 7.093,
     'ssm_norm_w_2': 4.241,
     'mla_q_norm_w_2': 8.0,
     'mla_kv_norm_w_2': 8.0}
    for name, (base, spread) in spreads.items():
        noise = np.random.default_rng([zlib.crc32(name.encode()), seed]).standard_normal(out[name].shape)
        drawn = base * np.exp(spread * noise) if base else spread * noise
        out[name] = __import__('jax').numpy.asarray(drawn.astype(out[name].dtype))
    for name, factor in factors.items():
        out[name] = (out[name] * factor).astype(out[name].dtype)
    return out
```

```python
import math
from contextlib import ExitStack

import numpy as np
import concourse.bass as bass
from concourse import mybir

F32 = mybir.dt.float32
I32 = mybir.dt.int32
ALU = mybir.AluOpType
ACT = mybir.ActivationFunctionType
AX_X = mybir.AxisListType.X

P = 128
T = 256
NB = T // P
D = 1024
KT = D // P
EPS = 1e-6
NEG = -1e30
LAMBDA_INIT = 0.8 - 0.6 * math.exp(-0.3 * 0)

H1, HD1 = 4, 64
POOL_WINDOWS = (2, 4, 8, 16)
UPAD = 16

NE, EPG, NG = 32, 8, 4
SLOTS = 64
PASSES = T // SLOTS
PAIRS = NE // 2

SG, SR, SP_, SN = 8, 4, 64, 128
SH = SG * SR
CONV = 4

MH = 16
MQL, MKVL, MR = 384, 256, 64
MSCALE = (128 + MR) ** -0.5

SLOT = 4096
RING = 6
CHUNKS_A = 12
CHUNKS_E = 3 * NE
CHUNKS_S = 16
CHUNKS_M = 16
CHUNKS_B = CHUNKS_S + CHUNKS_M


def constants():
    c, at, parts = {}, 0, []

    def put(name, a):
        nonlocal at
        a = np.ascontiguousarray(a, dtype=np.float32).reshape(P, -1)
        c[name] = (at, a.shape[1])
        at += a.shape[1]
        parts.append(a)

    i = np.arange(P)
    put("ident", np.eye(P))
    put("upto", i[:, None] <= i[None, :])
    put("before", i[:, None] < i[None, :])
    put("ones", np.ones((P, P)))
    put("halves", (i[:, None] // HD1) == (i[None, :] // HD1))
    put("future", np.where(i[:, None] <= i[None, :], 0.0, NEG))
    dist = np.concatenate([i[:, None] - i[None, :], i[:, None] + P - np.arange(T)[None, :]], axis=1)
    put("causal", np.where(dist >= 0, 0.0, NEG))
    slopes = [2.0 ** (-8.0 * (h + 1) / H1) for h in range(H1)]
    put("alibi", np.concatenate([np.where(dist >= 0, -s * dist, NEG) for s in slopes], axis=1))
    half = MR // 2
    inv = (500000.0 ** (-np.arange(half, dtype=np.float32) / np.float32(half))).astype(np.float32)
    ang = inv[:, None] * np.arange(T, dtype=np.float32)[None, :]
    cos, sin = np.cos(ang), np.sin(ang)
    put("rope", np.concatenate([np.tile(cos, (4, 1)), np.tile(np.concatenate([-sin, sin]), (2, 1))], axis=1))
    put("slot", np.tile(np.arange(SLOTS), (P, 1)))
    put("rev", np.tile(np.arange(NE, 0, -1), (P, 1)))
    put("count", np.tile(np.concatenate([1.0 / np.minimum(np.arange(UPAD) + 1, w) for w in POOL_WINDOWS]), (P, 1)))
    put("eps", np.full((P, 1), EPS))
    return c, np.concatenate(parts, axis=1)


PARAM_WIDTHS = dict(
    g1=KT, g2=KT, gs=KT, gm=KT, pool_scale=4, qg=1, kg=1, subln=1, lam=4 * HD1, router_b=NG + NE,
    conv_w=32 * CONV, conv_b=32, dt_b=SH, a_log=SH, d_skip=SH, ssm_g=16, cq_g=3, ckv_g=2,
    router_w=KT * (NG + NE), pool_w=4 * P, dt_w=KT * SH, final_g=D)
PARAMS, _at = {}, 0
for _n, _w in PARAM_WIDTHS.items():
    PARAMS[_n] = (_at, _w)
    _at += _w
NPARAM = _at


def program(nc, weights, params, consts, x, out, cmap, stages="1ESM"):
    NCONST = sum(w for _, w in cmap.values())
    ctx = ExitStack()
    with ctx:
        def sbuf(name, shape, dt=F32):
            return ctx.enter_context(nc.sbuf_tensor(name, shape, dt))

        ring = sbuf("ring", [P, RING, SLOT])
        con = sbuf("con", [P, NCONST])
        par = sbuf("par", [P, NPARAM])
        res = sbuf("res", [P, NB, D])
        work = sbuf("work", [P, 20300])
        small = sbuf("small", [P, 96])
        steps32 = sbuf("steps32", [1, 1], I32)
        bank = [ctx.enter_context(nc.psum_tensor(f"bank{b}", [P, 512], F32)) for b in range(8)]

        def C(name):
            o, w = cmap[name]
            return con[:, o:o + w]

        def PR(name):
            o, w = PARAMS[name]
            return par[:, o:o + w]

        def view(t, at, *shape):
            n = int(np.prod(shape))
            v = t[:, at:at + n]
            if len(shape) == 2:
                v = v.rearrange("p (a b) -> p a b", b=shape[1])
            if len(shape) == 3:
                v = v.rearrange("p (a b c) -> p a b c", b=shape[1], c=shape[2])
            return v

        def buf(at, *shape):
            return view(work, at, *shape)

        def three(ap, b):
            return ap.rearrange("p (a b) -> p a b", b=b)

        def four(ap, b, c):
            return ap.rearrange("p (a b c) -> p a b c", b=b, c=c)

        sems = {}

        def S(name):
            if name not in sems:
                sems[name] = ctx.enter_context(nc.semaphore(name))
            return sems[name]

        ident = C("ident")
        eps = C("eps")

        filled = [S(f"filled{b}") for b in range(8)]
        drained = [S(f"drained{b}") for b in range(8)]
        where, used, turn = {}, [0] * 8, [0]

        def new_tile(pe, name):
            b = turn[0] % 8
            turn[0] += 1
            used[b] += 1
            where[name] = (b, used[b])
            if used[b] > 1:
                pe.wait_ge(drained[b], used[b] - 1)
            return bank[b]

        def is_filled(ins, name):
            ins.then_inc(filled[where[name][0]], 1)

        def wait_filled(e, name):
            e.wait_ge(filled[where[name][0]], where[name][1])

        def is_drained(ins, name):
            ins.then_inc(drained[where[name][0]], 1)

        def wait_drained(e, name):
            e.wait_ge(drained[where[name][0]], where[name][1])

        def tile(name):
            return bank[where[name][0]]

        def chain(e, name):
            n = [0]

            def link(ins):
                n[0] += 1
                ins.then_inc(S(name), 1)
                e.wait_ge(S(name), n[0])
            return link

        full_a = [S(f"ring_a{s}") for s in range(RING)]
        full_b = [S(f"ring_b{s}") for s in range(RING)]
        last_use = {"a": [], "b": []}
        moe_gate, moe_up, moe_y0, moe_y1 = S("moe_gate"), S("moe_up"), S("moe_y0"), S("moe_y1")
        pairs_known = S("pairs_known")

        ss, rt, rs = small[:, 0:16], small[:, 16:32], small[:, 32:48]
        lamv, neglam = small[:, 48:52], small[:, 52:53]
        mx, sm = small[:, 56:72], small[:, 72:88]
        qg8 = small[:, 88:89]
        sg08 = small[:, 89:90]

        A_hT, A_xn = buf(0, KT, T), buf(2048, NB, D)
        A_u = buf(4096, 4, UPAD + T)
        A_qk = buf(5184, 8, T)
        A_v = buf(7232, NB, 512)
        A_sig = buf(8256, KT, 2, T)
        A_sq = buf(12352, 8, T)
        A_pl = buf(14400, 2, 4 * (UPAD + T))
        A_dT, A_yT, A_oT = buf(16576, 4, T), buf(17600, 4, T), buf(18624, 4, T)
        A_p, A_a, A_aT = buf(0, 4, 384), buf(2048, 2, 384), buf(2816, 2, 384)
        A_o = buf(12352, NB, 512)
        A_gt = buf(13376, 2, 512)
        A_mix = buf(14400, KT, T)

        E_xn, E_hnT, E_xe = buf(0, NB, D), buf(2048, KT, T), buf(4096, KT, P)
        E_S, E_SW, E_SWT = buf(5120, NB, P), buf(5376, NB, P), buf(5632, T)
        E_sg, E_hd, E_hdT = buf(5888, 512), buf(6400, 512), buf(6912, 4, P)
        E_y = buf(7424, 2, 512)
        XW = PASSES * NE + 2
        E_rank, E_w = buf(8448, NB, XW), buf(8448 + 2 * XW, NB, XW)
        E_t = 9000

        S_uT, S_xn = buf(0, KT, T), buf(2048, NB, D)
        S_BT, S_CT = buf(2048, SG, T), buf(4096, SG, T)
        S_xs, S_z = buf(6144, NB, 2048), buf(10240, NB, 2048)
        S_raw, S_cv, S_xsT = buf(14336, 3, 260), buf(15116, 3, T), buf(15884, 3, T)
        S_dt = buf(16652, 12, 64)
        S_E, S_M = buf(17420, 2, 512), buf(18444, 2, 512)
        S_xdt, S_xde = buf(19468, 2, 256), buf(19980, 256)
        S_Bt, S_st, S_yo, S_xd = buf(0, SG, P), buf(1024, 2, 256), buf(1536, 256), buf(1792, 256)
        S_yT = buf(2048, 16, T)

        M_uT, M_xn = buf(0, KT, T), buf(2048, NB, D)
        M_cq, M_ckv = buf(4096, NB, MQL), buf(4864, NB, MKVL)
        M_cqT, M_ckvT = buf(5376, 3, T), buf(6144, 2, T)
        M_kr, M_rt = buf(6656, T), buf(6912, 2, 512)
        M_z, M_kn, M_v = buf(7936, MH, T), buf(12032, MH, T), buf(16128, NB, 2048)
        M_qn, M_qr = buf(0, 4, T), buf(1024, 2, T)
        M_p, M_pT = buf(1536, 2, 384), buf(2304, 2, 384)
        F_out = buf(4096, NB, D)

        def conv_silu(j, act):
            act.wait_ge(S("conv_sum"), j + 1)
            if j < 8:
                dst = S_BT[:, j, :]
            elif j < 16:
                dst = S_CT[:, j - 8, :]
            else:
                if j >= 19:
                    wait_filled(act, f"xsT{j - 19}")
                dst = S_xsT[:, (j - 16) % 3, :]
            nc.scalar.activation(dst, S_cv[:, j % 3, :], ACT.Silu).then_inc(S("conv_out"), 1)

        def xs_out(j, dve):
            n = f"xsT{j}"
            wait_filled(dve, n)
            is_drained(nc.vector.tensor_copy(S_xs[:, :, j * P:j * P + P], three(tile(n)[:, 0:T], P)), n)

        block = ctx.enter_context(nc.Block())

        @block.tensor
        def _(pe):
            def chunk(which, n):
                sem = (full_a if which == "a" else full_b)[n % RING]
                pe.wait_ge(sem, 16 * (n // RING + 1))
                return ring[:, n % RING, :]

            def norm_T(tag, xn):
                pe.wait_ge(S(tag + "_xn"), NB)
                for i in range(KT // 2):
                    t = new_tile(pe, f"{tag}_T{i}")
                    for k in range(2):
                        for b in range(NB):
                            m = pe.transpose(t[:, k * T + b * P:k * T + b * P + P],
                                             xn[:, b, (2 * i + k) * P:(2 * i + k + 1) * P], ident)
                    is_filled(m, f"{tag}_T{i}")

            def norm_T_wait(tag):
                for i in range(KT // 2):
                    wait_drained(pe, f"{tag}_T{i}")

            def channel_tile(name, w, width, col, rhs, kts, c0=0, tl=None, last=True):
                t = tl if tl is not None else new_tile(pe, name)
                for k in range(kts):
                    m = pe.matmul(t[:, c0:c0 + T], w[:, k * width + col:k * width + col + P], rhs[:, k, :],
                                  start=(k == 0), stop=(k == kts - 1))
                if last:
                    is_filled(m, name)
                return m, t

            def token_tile(name, w, width, col, n, lhs, b, kts):
                t = new_tile(pe, name)
                for k in range(kts):
                    m = pe.matmul(t[:, 0:n], lhs[:, k, b * P:b * P + P], w[:, k * width + col:k * width + col + n],
                                  start=(k == 0), stop=(k == kts - 1))
                is_filled(m, name)
                return m

            def chunk_used(which, name=None, sem=None, count=0):
                if name is not None:
                    sem, count = filled[where[name][0]], where[name][1]
                last_use[which].append((sem, count))

            pe.wait_ge(S("loaded_con"), 16)
            if "1" in stages:
                norm_T("n1", A_xn)
                norm_T_wait("n1")
                for c in range(2):
                    w = chunk("a", c)
                    for j in range(4):
                        channel_tile(f"qk{4 * c + j}", w, 512, j * P, A_hT, KT)
                    chunk_used("a", f"qk{4 * c + 3}")
                w = chunk("a", 2)
                for b in range(NB):
                    token_tile(f"v{b}", w, 512, 0, 512, A_hT, b, KT)
                chunk_used("a", "v1")
                w = chunk("a", 3)
                for j in range(4):
                    channel_tile(f"u{j}", w, 512, j * P, A_hT, KT)
                chunk_used("a", "u3")
                for i in range(4):
                    n = f"sq{i}"
                    t = new_tile(pe, n)
                    pe.wait_ge(S("sq_ready"), i + 1)
                    is_filled(pe.matmul(t[:, :], C("halves"), A_sq[:, 2 * i:2 * i + 2, :], start=True, stop=True), n)
                for c in range(4):
                    w = chunk("a", 4 + c)
                    for j in range(4):
                        channel_tile(f"gate{4 * c + j}", w, 512, j * P, A_hT, KT)
                    chunk_used("a", f"gate{4 * c + 3}")
                for g in range(4):
                    n = f"pw{g}"
                    t = new_tile(pe, n)
                    pe.wait_ge(S("pool_d"), g + 1)
                    is_filled(pe.matmul(t[:, 0:T], PR("pool_w")[:, g * P:g * P + P], A_dT[:, g, :],
                                        start=True, stop=True), n)

                def scores(h):
                    for m_ in range(2):
                        n = f"s{h}_{m_}"
                        t = new_tile(pe, n)
                        lo = 64 * m_
                        pe.matmul(t[:, 0:384], ident, C("alibi")[:, h * 384:(h + 1) * 384], start=True, stop=False,
                                  skip_group_check=True)
                        pe.matmul(t[:, 0:P], A_qk[lo:lo + 64, h, 0:P], A_qk[lo:lo + 64, 4 + h, 0:P],
                                  start=False, stop=False, skip_group_check=True)
                        is_filled(pe.matmul(t[:, P:384], A_qk[lo:lo + 64, h, P:T], A_qk[lo:lo + 64, 4 + h, :],
                                            start=False, stop=True, skip_group_check=True), n)

                def turn_probs(h):
                    n = f"at{h}"
                    t = new_tile(pe, n)
                    pe.wait_ge(S("a_ready"), h + 1)
                    for j in range(3):
                        m = pe.transpose(t[:, j * P:j * P + P], A_a[:, h % 2, j * P:j * P + P], ident)
                    is_filled(m, n)

                def values(h):
                    n = f"o{h}"
                    t = new_tile(pe, n)
                    wait_drained(pe, f"at{h}")
                    if h == 0:
                        wait_drained(pe, "v0")
                        wait_drained(pe, "v1")
                    aT = A_aT[:, h % 2, :]
                    pe.matmul(t[:, 0:P], aT[:, 0:P], A_v[:, 0, h * P:h * P + P], start=True, stop=True)
                    pe.matmul(t[:, P:T], aT[:, P:T], A_v[:, 0, h * P:h * P + P], start=True, stop=False)
                    is_filled(pe.matmul(t[:, P:T], aT[:, T:384], A_v[:, 1, h * P:h * P + P],
                                        start=False, stop=True), n)

                pe.wait_ge(S("qk_ready"), 4)
                for h in range(H1 + 2):
                    if h < H1:
                        scores(h)
                    if 1 <= h <= H1:
                        turn_probs(h - 1)
                    if h >= 2:
                        values(h - 2)
                pe.wait_ge(S("o_norm"), NB)
                for i in range(2):
                    n = f"oT{i}"
                    t = new_tile(pe, n)
                    for k in range(2):
                        for b in range(NB):
                            m = pe.transpose(t[:, k * T + b * P:k * T + b * P + P],
                                             A_o[:, b, (2 * i + k) * P:(2 * i + k + 1) * P], ident)
                    is_filled(m, n)
                wp, wa = chunk("a", 8), chunk("a", 9)
                for g in range(4):
                    wait_drained(pe, f"pw{g}")
                for i in range(2):
                    wait_drained(pe, f"oT{i}")
                for j in range(KT):
                    n = f"up{j}"
                    _, t = channel_tile(n, wp, D, j * P, A_yT, 4, last=False)
                    channel_tile(n, wa, D, j * P, A_oT, 4, c0=T, tl=t)
                chunk_used("a", f"up{KT - 1}")
                chunk_used("a", f"up{KT - 1}")
                pe.wait_ge(S("mix_ready"), KT)
                for c in range(2):
                    w = chunk("a", 10 + c)
                    for b in range(NB):
                        token_tile(f"wo{c}_{b}", w, 512, 0, 512, A_mix, b, KT)
                    chunk_used("a", f"wo{c}_1")

            if "E" in stages:
                norm_T("n2", E_xn)
                norm_T_wait("n2")
                n = "route"
                t = new_tile(pe, n)
                NL = NG + NE
                for b in range(NB):
                    for k in range(KT):
                        m = pe.matmul(t[:, b * NL:(b + 1) * NL], E_hnT[:, k, b * P:b * P + P],
                                      PR("router_w")[:, k * NL:(k + 1) * NL], start=(k == 0), stop=(k == KT - 1))
                is_filled(m, n)
                n = "rank"
                t = new_tile(pe, n)
                pe.wait_ge(S("member_ready"), 1)
                mem = buf(E_t + 600, NB, NE)
                pe.matmul(t[:, 0:NE], C("before"), mem[:, 0, :], start=True, stop=True)
                pe.matmul(t[:, NE:2 * NE], C("ones"), mem[:, 0, :], start=True, stop=False)
                pe.matmul(t[:, NE:2 * NE], C("before"), mem[:, 1, :], start=False, stop=True)
                pe.matmul(t[:, 2 * NE:3 * NE], C("ones"), mem[:, 0, :], start=True, stop=False)
                is_filled(pe.matmul(t[:, 2 * NE:3 * NE], C("ones"), mem[:, 1, :], start=False, stop=True), n)
                for b in range(8):
                    if used[b]:
                        pe.wait_ge(drained[b], used[b])
                for b in range(NB):
                    for j in range(2):
                        m = pe.matmul(bank[2 * b + j][:, :], ident, res[:, b, j * 512:(j + 1) * 512],
                                      start=True, stop=False, skip_group_check=True)
                A, B, Cb, Dk = bank[4], bank[5], bank[6], bank[7]

                def gather(half, sem):
                    for k in range(4):
                        for b in range(NB):
                            kk = 4 * half + k
                            m = pe.matmul(A[:, k * P:k * P + P], E_xn[:, b, kk * P:kk * P + P], E_S[:, b, :],
                                          start=(b == 0), stop=(b == NB - 1))
                    m.then_inc(sem, 1)

                pe.wait_ge(S("pick_ready"), 1)
                gather(0, S("xlo_mm"))
                pe.wait_ge(S("xlo_out"), 1)
                gather(1, S("xhi_mm"))
                pe.wait_ge(pairs_known, 1)
                pairs = pe.value_load(steps32[0:1, 0:1], min_val=PAIRS, max_val=PAIRS * PASSES)
                base = CHUNKS_A // RING if "1" in stages else 0
                with pe.Fori(0, pairs) as i:
                    pe.wait_ge(S("weight_ready"), i + 1)
                    pe.wait_ge(S("xhi_out"), i + 1)
                    for b in range(NB):
                        m = pe.transpose(A[:, b * P:b * P + P], E_SW[:, b, :], ident)
                    m.then_inc(S("swt_mm"), 1)
                    for q, (t, sem) in enumerate(((B, moe_gate), (Cb, moe_up))):
                        for j in range(2):
                            pe.wait_ge(full_a[2 * q + j], i * 16 + 16 * (base + 1))
                        for k in range(KT):
                            for j in range(2):
                                m = pe.matmul(t[64 * j:64 * j + 64, :], E_xe[:, k, 64 * j:64 * j + 64],
                                              ring[:, 2 * q + j, k * 512:(k + 1) * 512],
                                              start=(k == 0), stop=(k == KT - 1))
                        m.then_inc(sem, 1)
                    pe.wait_ge(S("pick_ready"), i + 2)
                    pe.wait_ge(S("swt_out"), i + 1)
                    gather(0, S("xlo_mm"))
                    pe.wait_ge(S("hd_ready"), i + 1)
                    for k in range(4):
                        m = pe.transpose(Dk[:, k * P:k * P + P], E_hd[:, k * P:k * P + P], ident)
                    m.then_inc(S("hdt_mm"), 1)
                    pe.wait_ge(S("xlo_out"), i + 2)
                    gather(1, S("xhi_mm"))
                    pe.wait_ge(S("hdt_out"), i + 1)
                    for j in range(2):
                        pe.wait_ge(full_a[4 + j], i * 16 + 16 * (base + 1))
                    for q, (t, sem) in enumerate(((B, moe_y0), (Cb, moe_y1))):
                        for k in range(4):
                            for j in range(2):
                                m = pe.matmul(t[64 * j:64 * j + 64, :], E_hdT[:, k, 64 * j:64 * j + 64],
                                              ring[:, 4 + j, k * D + q * 512:k * D + (q + 1) * 512],
                                              start=(k == 0), stop=(k == 3))
                        m.then_inc(sem, 1)
                    for q, sem in enumerate((S("y0_out"), S("y1_out"))):
                        pe.wait_ge(sem, i + 1)
                        for b in range(NB):
                            m = pe.matmul(bank[2 * b + q][:, :], E_SWT[:, b * P:b * P + P], E_y[:, q, :],
                                          start=False, stop=False, skip_group_check=True)
                    m.then_inc(S("scattered"), 1)
                pe.wait_ge(S("moe_taken"), 4)

            def out_tiles(tag, rhsT, cb):
                for half in range(2):
                    ts = [new_tile(pe, f"{tag}{half}_{b}") for b in range(NB)]
                    for q in range(2):
                        w = chunk("b", cb)
                        cb += 1
                        for b in range(NB):
                            for k in range(KT):
                                m = pe.matmul(ts[b][:, :], rhsT[:, q * KT + k, b * P:b * P + P],
                                              w[:, k * 512:(k + 1) * 512],
                                              start=(q == 0 and k == 0), stop=(q == 1 and k == KT - 1))
                            if q == 1:
                                is_filled(m, f"{tag}{half}_{b}")
                        if q == 0:
                            m.then_inc(S(tag + "_half"), 1)
                            chunk_used("b", sem=S(tag + "_half"), count=half + 1)
                        else:
                            chunk_used("b", f"{tag}{half}_1")
                return cb

            cb = 0
            if "S" in stages:
                norm_T("n3", S_xn)
                norm_T_wait("n3")
                n = "dt"
                t = new_tile(pe, n)
                for b in range(NB):
                    for k in range(KT):
                        m = pe.matmul(t[:, b * SH:(b + 1) * SH], S_uT[:, k, b * P:b * P + P],
                                      PR("dt_w")[:, k * SH:(k + 1) * SH], start=(k == 0), stop=(k == KT - 1))
                is_filled(m, n)

                def turn_xs(j):
                    n = f"xsT{j}"
                    t = new_tile(pe, n)
                    pe.wait_ge(S("conv_out"), 16 + j + 1)
                    for b in range(NB):
                        m = pe.transpose(t[:, b * P:b * P + P], S_xsT[:, j % 3, b * P:b * P + P], ident)
                    is_filled(m, n)

                for c in range(8):
                    w = chunk("b", cb)
                    cb += 1
                    for j in range(4):
                        channel_tile(f"xbc{4 * c + j}", w, 512, j * P, S_uT, KT)
                        if 4 * c + j >= 18:
                            turn_xs(4 * c + j - 18)
                    chunk_used("b", f"xbc{4 * c + 3}")
                for c in range(4):
                    w = chunk("b", cb)
                    cb += 1
                    for b in range(NB):
                        token_tile(f"z{c}_{b}", w, 512, 0, 512, S_uT, b, KT)
                        if c == 0:
                            turn_xs(14 + b)
                    chunk_used("b", f"z{c}_1")
                n = "acum"
                t = new_tile(pe, n)
                pe.wait_ge(S("a_decay"), 1)
                av = S_dt[:, 1, :]
                pe.matmul(t[:, 0:64], C("upto"), av, start=True, stop=True)
                is_filled(pe.matmul(t[:, 64:96], C("ones"), av[:, 0:SH], start=True, stop=True), n)
                for i in range(2):
                    n = f"Bt{i}"
                    t = new_tile(pe, n)
                    for k in range(4):
                        m = pe.transpose(t[:, k * P:k * P + P], S_BT[:, 4 * i + k, 0:P], ident)
                    is_filled(m, n)
                for i in range(2):
                    wait_drained(pe, f"Bt{i}")
                for j in range(16):
                    wait_drained(pe, f"xsT{j}")

                def decays(i):
                    g, c = divmod(i, 2)
                    n = f"seg{i}"
                    t = new_tile(pe, n)
                    pe.matmul(t[:, :], ident, C("future").unsqueeze(1).to_broadcast([P, SR, P]), start=True,
                              stop=False, skip_group_check=True)
                    for r in range(SR):
                        h = c * SH + g * SR + r
                        m = pe.matmul(t[:, r * P:r * P + P], S_dt[:, 1, h:h + 1].to_broadcast([P, P]),
                                      C("upto"), start=False, stop=(r == SR - 1), skip_group_check=True)
                    is_filled(m, n)
                    n = f"cb{i}"
                    t = new_tile(pe, n)
                    is_filled(pe.matmul(t[:, 0:P], S_BT[:, g, c * P:c * P + P], S_CT[:, g, c * P:c * P + P],
                                        start=True, stop=True), n)

                def mixes(i):
                    g, c = divmod(i, 2)
                    n = f"yd{i}"
                    t = new_tile(pe, n)
                    wait_drained(pe, f"cb{i}")
                    pe.wait_ge(S("xdt_ready"), i + 1)
                    for r in range(SR):
                        m = pe.matmul(t[:, r * SP_:(r + 1) * SP_], S_M[:, i % 2, r * P:r * P + P],
                                      S_xdt[:, i % 2, r * SP_:(r + 1) * SP_], start=True, stop=True)
                    if c == 0:
                        is_filled(m, n)
                        n = f"st{g}"
                        t = new_tile(pe, n)
                        pe.wait_ge(S("xde_ready"), g + 1)
                        m = pe.matmul(t[:, 0:256], S_Bt[:, g, :], S_xde, start=True, stop=True)
                    else:
                        wait_drained(pe, f"st{g}")
                        m = pe.matmul(t[:, 256:512], S_CT[:, g, P:T], S_st[:, g % 2, :], start=True, stop=True)
                    is_filled(m, n)

                for i in range(2 * SG + 1):
                    if i < 2 * SG:
                        decays(i)
                    if i >= 1:
                        mixes(i - 1)
                pe.wait_ge(S("y_norm"), NB)
                for i in range(8):
                    n = f"yT{i}"
                    t = new_tile(pe, n)
                    for k in range(2):
                        for b in range(NB):
                            m = pe.transpose(t[:, k * T + b * P:k * T + b * P + P],
                                             S_xs[:, b, (2 * i + k) * P:(2 * i + k + 1) * P], ident)
                    is_filled(m, n)
                for i in range(8):
                    wait_drained(pe, f"yT{i}")

                cb = out_tiles("so", S_yT, cb)

            if "M" in stages:
                norm_T("n4", M_xn)
                norm_T_wait("n4")
                w = chunk("b", cb)
                for b in range(NB):
                    token_tile(f"cq{b}", w, MQL, 0, MQL, M_uT, b, KT)
                chunk_used("b", "cq1")
                w = chunk("b", cb + 1)
                for b in range(NB):
                    token_tile(f"ckv{b}", w, 512, 0, MKVL, M_uT, b, KT)
                _, t = channel_tile("kr", w, 512, MKVL, M_uT, KT, last=False)
                channel_tile("kr", w, 512, MKVL + P, M_uT, KT, c0=T, tl=t)
                chunk_used("b", "kr")
                for c in range(4):
                    w = chunk("b", cb + 2 + c)
                    for j in range(2):
                        n = f"mz{2 * c + j}"
                        _, t = channel_tile(n, w, 512, 2 * j * P, M_uT, KT, last=False)
                        channel_tile(n, w, 512, (2 * j + 1) * P, M_uT, KT, c0=T, tl=t)
                    chunk_used("b", f"mz{2 * c + 1}")
                pe.wait_ge(S("lat_norm"), 4)
                n = "ckvT"
                t = new_tile(pe, n)
                for k in range(2):
                    for b in range(NB):
                        m = pe.transpose(t[:, k * T + b * P:k * T + b * P + P], M_ckv[:, b, k * P:k * P + P], ident)
                is_filled(m, n)
                for i, ks in enumerate(((0, 1), (2,))):
                    n = f"cqT{i}"
                    t = new_tile(pe, n)
                    for j, k in enumerate(ks):
                        for b in range(NB):
                            m = pe.transpose(t[:, j * T + b * P:j * T + b * P + P], M_cq[:, b, k * P:k * P + P], ident)
                    is_filled(m, n)
                wait_drained(pe, "ckvT")
                w = chunk("b", cb + 6)
                for i in range(MH // 2):
                    n = f"kn{i}"
                    _, t = channel_tile(n, w, 2048, 2 * i * P, M_ckvT, 2, last=False)
                    channel_tile(n, w, 2048, (2 * i + 1) * P, M_ckvT, 2, c0=T, tl=t)
                chunk_used("b", f"kn{MH // 2 - 1}")
                w = chunk("b", cb + 7)
                for j in range(4):
                    for b in range(NB):
                        token_tile(f"mv{j}_{b}", w, 2048, j * 512, 512, M_ckvT, b, 2)
                chunk_used("b", "mv3_1")
                wait_drained(pe, "cqT0")
                wait_drained(pe, "cqT1")

                def queries(i):
                    w = chunk("b", cb + 8 + i // 2)
                    o = (i % 2) * 512
                    n = f"qn{i}"
                    _, t = channel_tile(n, w, D, o, M_cqT, 3, last=False)
                    channel_tile(n, w, D, o + P, M_cqT, 3, c0=T, tl=t)
                    n = f"qr{i}"
                    _, t = channel_tile(n, w, D, o + 2 * P, M_cqT, 3, last=False)
                    channel_tile(n, w, D, o + 3 * P, M_cqT, 3, c0=T, tl=t)
                    if i % 2:
                        chunk_used("b", f"qr{i}")

                def m_scores(h):
                    i, lo = h // 2, 64 * (h % 2)
                    if h % 2 == 0:
                        wait_drained(pe, f"qn{i}")
                        pe.wait_ge(S("qrope_ready"), i + 1)
                    n = f"ms{h}"
                    t = new_tile(pe, n)
                    qn, qr = M_qn[:, 2 * (i % 2) + h % 2, :], M_qr[lo:lo + 64, i % 2, :]
                    pe.matmul(t[:, 0:384], ident, C("causal"), start=True, stop=False, skip_group_check=True)
                    pe.matmul(t[:, 0:P], qn[:, 0:P], M_kn[:, h, 0:P], start=False, stop=False, skip_group_check=True)
                    pe.matmul(t[:, P:384], qn[:, P:T], M_kn[:, h, :], start=False, stop=False, skip_group_check=True)
                    pe.matmul(t[:, 0:P], qr[:, 0:P], M_kr[lo:lo + 64, 0:P], start=False, stop=False,
                              skip_group_check=True)
                    is_filled(pe.matmul(t[:, P:384], qr[:, P:T], M_kr[lo:lo + 64, :], start=False, stop=True,
                                        skip_group_check=True), n)

                def m_turn(h):
                    n = f"mpt{h}"
                    t = new_tile(pe, n)
                    pe.wait_ge(S("mp_ready"), 2 * (h + 1))
                    for j in range(3):
                        m = pe.transpose(t[:, j * P:j * P + P], M_p[:, h % 2, j * P:j * P + P], ident)
                    is_filled(m, n)

                def m_values(h):
                    n = f"mo{h}"
                    t = new_tile(pe, n)
                    wait_drained(pe, f"mpt{h}")
                    pT = M_pT[:, h % 2, :]
                    pe.matmul(t[:, 0:T], M_v[:, 0, h * P:h * P + P], pT[:, 0:T], start=True, stop=False,
                              skip_group_check=True)
                    is_filled(pe.matmul(t[:, P:T], M_v[:, 1, h * P:h * P + P], pT[:, T:384], start=False, stop=True,
                                        skip_group_check=True), n)

                for i in range(MH // 2):
                    wait_drained(pe, f"kn{i}")
                for j in range(4):
                    for b in range(NB):
                        wait_drained(pe, f"mv{j}_{b}")
                pe.wait_ge(S("krope_ready"), 1)
                queries(0)
                for h in range(MH + 2):
                    if h % 2 == 0 and h // 2 + 1 < MH // 2:
                        queries(h // 2 + 1)
                    if h < MH:
                        m_scores(h)
                    if 1 <= h <= MH:
                        m_turn(h - 1)
                    if h >= 2:
                        m_values(h - 2)
                for h in range(MH):
                    wait_drained(pe, f"mo{h}")
                cb = out_tiles("mo_out", M_z, cb + 12)

        @block.scalar
        def _(act):
            link = chain(act, "act_own")

            def norm_stats(tag, xn):
                for b in range(NB):
                    m = nc.scalar.activation(xn[:, b, :], res[:, b, :], ACT.Square, accum_out=ss[:, b:b + 1])
                link(m)
                nc.scalar.activation(rt[:, 0:NB], ss[:, 0:NB], ACT.Sqrt, bias=eps, scale=1.0 / D)\
                    .then_inc(S(tag + "_rt"), 1)

            def take(name, dst, src, func=ACT.Copy, **kw):
                wait_filled(act, name)
                is_drained(nc.scalar.activation(dst, src, func, **kw), name)

            act.wait_ge(S("loaded_con"), 16)
            act.wait_ge(S("loaded_par"), 16)
            act.wait_ge(S("loaded_x"), 16)
            if "1" in stages:
                norm_stats("n1", A_xn)
                act.wait_ge(S("lam_dot"), 1)
                nc.scalar.activation(lamv[:, 2:4], lamv[:, 0:2], ACT.Exp).then_inc(S("lam_exp"), 1)
                for i in range(4):
                    for j in (2 * i, 2 * i + 1):
                        wait_drained(act, f"qk{j}")
                    nc.scalar.activation(A_sq[:, 2 * i:2 * i + 2, :], A_qk[:, 2 * i:2 * i + 2, :], ACT.Square)\
                        .then_inc(S("sq_ready"), 1)
                for b in range(NB):
                    take(f"v{b}", A_v[:, b, :], tile(f"v{b}")[:, :])
                act.wait_ge(S("u_zero"), 1)
                for j in range(4):
                    take(f"u{j}", A_u[:, j, UPAD:], tile(f"u{j}")[:, 0:T])
                for i in range(4):
                    n = f"sq{i}"
                    wait_filled(act, n)
                    is_drained(nc.scalar.activation(A_sq[:, 2 * i:2 * i + 2, :], three(tile(n)[:, :], T), ACT.Sqrt,
                                                    bias=eps, scale=1.0 / HD1), n)
                for j in range(16):
                    take(f"gate{j}", A_sig[:, j % 8, j // 8, :], tile(f"gate{j}")[:, 0:T], ACT.Sigmoid)
                for g in range(4):
                    take(f"pw{g}", A_yT[:, g, :], tile(f"pw{g}")[:, 0:T], ACT.Copy, scale=PR("pool_scale")[:, g:g + 1])
                for h in range(H1):
                    for m_ in range(2):
                        n = f"s{h}_{m_}"
                        wait_filled(act, n)
                        act.wait_ge(S("max_ready"), 2 * h + m_ + 1)
                        if h >= 2:
                            act.wait_ge(S("a_ready"), h - 1)
                        q = 4 * (h % 2) + 2 * m_
                        nc.scalar.activation(A_p[:, 2 * (h % 2) + m_, 0:P], tile(n)[:, 0:P], ACT.Exp,
                                             bias=mx[:, q:q + 1], accum_out=sm[:, q:q + 1])
                        is_drained(nc.scalar.activation(A_p[:, 2 * (h % 2) + m_, P:384], tile(n)[:, P:384], ACT.Exp,
                                                        bias=mx[:, q + 1:q + 2], accum_out=sm[:, q + 1:q + 2]), n)
                for h in range(H1):
                    for b in range(NB):
                        act.wait_ge(drained[where[f"o{h}"][0]], where[f"o{h}"][1])
                        m = nc.scalar.activation(A_mix[:, 4 * b + h, 0:P], A_o[:, b, h * P:h * P + P], ACT.Square,
                                                 accum_out=ss[:, b * 4 + h:b * 4 + h + 1])
                link(m)
                nc.scalar.activation(rt[:, 0:8], ss[:, 0:8], ACT.Sqrt, bias=eps, scale=1.0 / P)\
                    .then_inc(S("o_rt"), 1)
            if "E" in stages:
                if "1" in stages:
                    for c in range(2):
                        for b in range(NB):
                            wait_drained(act, f"wo{c}_{b}")
                norm_stats("n2", E_xn)
                act.wait_ge(S("route_gap"), 1)
                gap = buf(E_t, NB, 5)
                nc.scalar.activation(gap, gap, ACT.Exp).then_inc(S("route_exp"), 1)
                act.wait_ge(pairs_known, 1)
                pairs = act.value_load(steps32[0:1, 0:1], min_val=PAIRS, max_val=PAIRS * PASSES)
                A, B, Cb, Dk = bank[4], bank[5], bank[6], bank[7]
                with act.Fori(0, pairs) as i:
                    act.wait_ge(S("swt_mm"), i + 1)
                    nc.scalar.activation(E_SWT, A[:, 0:T], ACT.Copy).then_inc(S("swt_out"), 1)
                    act.wait_ge(moe_gate, i + 1)
                    nc.scalar.activation(E_sg, B[:, :], ACT.Silu).then_inc(S("sg_ready"), 1)
                    act.wait_ge(S("hdt_mm"), i + 1)
                    nc.scalar.activation(E_hdT, three(Dk[:, :], P), ACT.Copy).then_inc(S("hdt_out"), 1)
                    act.wait_ge(moe_y1, i + 1)
                    nc.scalar.activation(E_y[:, 1, :], Cb[:, :], ACT.Copy).then_inc(S("y1_out"), 1)
                act.wait_ge(S("scattered"), pairs)
                for b in range(NB):
                    nc.scalar.activation(res[:, b, 0:512], bank[2 * b][:, :], ACT.Copy).then_inc(S("moe_taken"), 1)
            if "S" in stages:
                if "E" in stages:
                    act.wait_ge(S("moe_taken"), 4)
                norm_stats("n3", S_xn)
                V = lambda k: S_dt[:, k, :]
                act.wait_ge(S("dt_abs"), 1)
                link(nc.scalar.activation(V(3), V(2), ACT.Exp, scale=-1.0))
                link(nc.scalar.activation(V(11)[:, 0:SH], PR("a_log"), ACT.Exp))
                nc.scalar.activation(V(4), V(3), ACT.Ln, bias=1.0).then_inc(S("dt_ln"), 1)
                act.wait_ge(S("pad_zero"), 1)
                for j in range(32):
                    n = f"xbc{j}"
                    src = tile(n)[:, 0:T]
                    wait_filled(act, n)
                    if j >= 3:
                        act.wait_ge(S("conv_out"), j - 2)
                    ch = (j + 16) % 32
                    nc.scalar.activation(S_raw[:, j % 3, 3:3 + T], src, ACT.Copy)
                    is_drained(nc.scalar.activation(S_cv[:, j % 3, :], src, ACT.Identity,
                                                    scale=PR("conv_w")[:, ch * CONV + 3:ch * CONV + 4],
                                                    bias=PR("conv_b")[:, ch:ch + 1]), n)
                    if j >= 1:
                        conv_silu(j - 1, act)
                conv_silu(31, act)
                for c in range(4):
                    for b in range(NB):
                        n = f"z{c}_{b}"
                        take(n, S_z[:, b, c * 512:(c + 1) * 512], tile(n)[:, :], ACT.Silu)
                act.wait_ge(S("acum_out"), 1)
                nc.scalar.activation(V(8), V(5), ACT.Exp).then_inc(S("decay_exp"), 1)
                for i in range(2 * SG):
                    g, c = divmod(i, 2)
                    n = f"seg{i}"
                    wait_filled(act, n)
                    if i >= 2:
                        wait_drained(act, f"cb{i - 2}")
                    for r in range(SR):
                        h = c * SH + g * SR + r
                        m = nc.scalar.activation(S_E[:, i % 2, r * P:r * P + P], tile(n)[:, r * P:r * P + P], ACT.Exp,
                                                 bias=V(7)[:, h:h + 1])
                    is_drained(m, n)
                    if c == 0:
                        wait_filled(act, f"st{g}")
                        is_drained(nc.scalar.activation(S_st[:, g % 2, :], tile(f"st{g}")[:, 0:256], ACT.Copy), f"st{g}")
                for i in range(2 * SG):
                    wait_drained(act, f"yd{i}")
                for i in range(2 * SG):
                    g, c = divmod(i, 2)
                    m = nc.scalar.activation(S_yT[:, i, :], S_xs[:, c, g * 256:(g + 1) * 256], ACT.Square,
                                             accum_out=ss[:, c * SG + g:c * SG + g + 1])
                link(m)
                nc.scalar.activation(rt[:, :], ss[:, :], ACT.Sqrt, bias=eps, scale=1.0 / 256).then_inc(S("y_rt"), 1)
                for c in range(2):
                    for b in range(NB):
                        wait_drained(act, f"so{c}_{b}")
            if "M" in stages:
                norm_stats("n4", M_xn)
                for b in range(NB):
                    n = f"cq{b}"
                    wait_filled(act, n)
                    nc.scalar.activation(M_cq[:, b, :], tile(n)[:, 0:MQL], ACT.Copy)
                    is_drained(nc.scalar.activation(work[:, 12032 + b * 512:12032 + b * 512 + MQL], tile(n)[:, 0:MQL], ACT.Square,
                                                    accum_out=ss[:, b:b + 1]), n)
                for b in range(NB):
                    n = f"ckv{b}"
                    wait_filled(act, n)
                    nc.scalar.activation(M_ckv[:, b, :], tile(n)[:, 0:MKVL], ACT.Copy)
                    is_drained(nc.scalar.activation(work[:, 13056 + b * 512:13056 + b * 512 + MKVL], tile(n)[:, 0:MKVL], ACT.Square,
                                                    accum_out=ss[:, 2 + b:3 + b]), n)
                wait_drained(act, "ckv1")
                wait_drained(act, "cq1")
                nc.scalar.activation(rt[:, 0:2], ss[:, 0:2], ACT.Sqrt, bias=eps, scale=1.0 / MQL)
                nc.scalar.activation(rt[:, 2:4], ss[:, 2:4], ACT.Sqrt, bias=eps, scale=1.0 / MKVL)\
                    .then_inc(S("lat_rt"), 1)
                for i in range(MH // 2):
                    take(f"mz{i}", M_z[:, 2 * i:2 * i + 2, :], three(tile(f"mz{i}")[:, :], T), ACT.Silu)
                for i in range(MH // 2):
                    take(f"kn{i}", M_kn[:, 2 * i:2 * i + 2, :], three(tile(f"kn{i}")[:, :], T))

                def q_copy(i):
                    take(f"qn{i}", M_qn[:, 2 * (i % 2):2 * (i % 2) + 2, :], three(tile(f"qn{i}")[:, :], T))

                q_copy(0)
                for h in range(MH):
                    if h % 2 == 0 and h // 2 + 1 < MH // 2:
                        if h >= 2:
                            wait_filled(act, f"ms{h - 1}")
                        q_copy(h // 2 + 1)
                    n = f"ms{h}"
                    wait_filled(act, n)
                    act.wait_ge(S("mmax_ready"), h + 1)
                    if h >= 2:
                        wait_filled(act, f"mpt{h - 2}")
                    q = 2 * (h % 2)
                    nc.scalar.activation(M_p[:, h % 2, 0:P], tile(n)[:, 0:P], ACT.Exp, scale=MSCALE,
                                         bias=mx[:, q:q + 1], accum_out=sm[:, q:q + 1])
                    is_drained(nc.scalar.activation(M_p[:, h % 2, P:384], tile(n)[:, P:384], ACT.Exp, scale=MSCALE,
                                                    bias=mx[:, q + 1:q + 2], accum_out=sm[:, q + 1:q + 2]), n)
                for c in range(2):
                    for b in range(NB):
                        wait_drained(act, f"mo_out{c}_{b}")
            if stages[-1] == "E":
                act.wait_ge(S("moe_taken"), 4)
            if stages[-1] == "1":
                for c in range(2):
                    for b in range(NB):
                        wait_drained(act, f"wo{c}_{b}")
            norm_stats("n5", F_out)

        @block.vector
        def _(dve):
            v = nc.vector
            link = chain(dve, "dve_own")

            def norm_apply(tag, xn):
                dve.wait_ge(S(tag + "_rt"), 1)
                link(v.reciprocal(rs[:, 0:NB], rt[:, 0:NB]))
                for b in range(NB):
                    v.tensor_scalar(xn[:, b, :], res[:, b, :], rs[:, b:b + 1], None, ALU.mult)\
                        .then_inc(S(tag + "_xn"), 1)

            def norm_out(tag, dst, gain):
                for i in range(KT // 2):
                    n = f"{tag}_T{i}"
                    wait_filled(dve, n)
                    is_drained(v.tensor_tensor(dst[:, 2 * i:2 * i + 2, :], three(tile(n)[:, :], T),
                                               PR(gain)[:, 2 * i:2 * i + 2].unsqueeze(2).to_broadcast([P, 2, T]),
                                               ALU.mult), n)

            def residual(tag):
                for c in range(2):
                    for b in range(NB):
                        n = f"{tag}{c}_{b}"
                        wait_filled(dve, n)
                        dst = res[:, b, c * 512:(c + 1) * 512]
                        is_drained(v.tensor_tensor(dst, tile(n)[:, :], dst, ALU.add), n)
                for c in range(2):
                    for b in range(NB):
                        wait_drained(dve, f"{tag}{c}_{b}")

            dve.wait_ge(S("loaded_con"), 16)
            dve.wait_ge(S("loaded_par"), 16)
            dve.wait_ge(S("loaded_x"), 16)
            if "1" in stages:
                v.memset(A_u[:, :, 0:UPAD], 0.0).then_inc(S("u_zero"), 1)
                norm_apply("n1", A_xn)
                lam = PR("lam")
                for m_ in range(2):
                    m = v.tensor_tensor_reduce(A_gt[:, m_, 0:HD1], lam[:, 2 * m_ * HD1:(2 * m_ + 1) * HD1],
                                               lam[:, (2 * m_ + 1) * HD1:(2 * m_ + 2) * HD1], 1.0, 0.0, ALU.mult,
                                               ALU.add, lamv[:, m_:m_ + 1])
                m.then_inc(S("lam_dot"), 1)
                v.tensor_scalar(qg8, PR("qg"), HD1 ** -0.5, None, ALU.mult)
                v.tensor_scalar(sg08, PR("subln"), 1.0 - LAMBDA_INIT, None, ALU.mult)
                norm_out("n1", A_hT, "g1")
                dve.wait_ge(S("lam_exp"), 1)
                link(v.tensor_tensor(neglam, lamv[:, 3:4], lamv[:, 2:3], ALU.subtract))
                link(v.tensor_scalar(neglam, neglam, -LAMBDA_INIT, None, ALU.add))
                for j in range(8):
                    n = f"qk{j}"
                    wait_filled(dve, n)
                    is_drained(v.tensor_copy(A_qk[:, j, :], tile(n)[:, 0:T]), n)
                for i in range(4):
                    wait_drained(dve, f"sq{i}")
                    sl = slice(2 * i, 2 * i + 2)
                    link(v.reciprocal(A_sq[:, sl, :], A_sq[:, sl, :]))
                    g = qg8 if i < 2 else PR("kg")
                    v.scalar_tensor_tensor(out=A_qk[:, sl, :], in0=A_qk[:, sl, :], scalar=g, in1=A_sq[:, sl, :],
                                           op0=ALU.mult, op1=ALU.mult).then_inc(S("qk_ready"), 1)
                for g, w in enumerate(POOL_WINDOWS):
                    dve.wait_ge(S("pool_part"), (g + 1) * (g + 2) // 2)
                    s = A_pl[:, g % 2, g * (UPAD + T) + UPAD:(g + 1) * (UPAD + T)]
                    u = A_u[:, g, UPAD:]
                    link(v.tensor_tensor(A_dT[:, g, 0:UPAD], s[:, 0:UPAD], C("count")[:, g * UPAD:(g + 1) * UPAD],
                                         ALU.mult))
                    link(v.tensor_tensor(A_dT[:, g, 0:UPAD], A_dT[:, g, 0:UPAD], u[:, 0:UPAD], ALU.subtract))
                    v.scalar_tensor_tensor(out=A_dT[:, g, UPAD:], in0=s[:, UPAD:], scalar=1.0 / w, in1=u[:, UPAD:],
                                           op0=ALU.mult, op1=ALU.subtract).then_inc(S("pool_d"), 1)

                def maxima(h):
                    for m_ in range(2):
                        n = f"s{h}_{m_}"
                        wait_filled(dve, n)
                        q = 4 * (h % 2) + 2 * m_
                        v.tensor_reduce(mx[:, q:q + 1], tile(n)[:, 0:P], AX_X, ALU.max)
                        link(v.tensor_reduce(mx[:, q + 1:q + 2], tile(n)[:, P:384], AX_X, ALU.max))
                        v.tensor_scalar(mx[:, q:q + 2], mx[:, q:q + 2], -1.0, None, ALU.mult)\
                            .then_inc(S("max_ready"), 1)

                def combine(h):
                    for m_ in range(2):
                        wait_drained(dve, f"s{h}_{m_}")
                    q = 4 * (h % 2)
                    link(v.reciprocal(sm[:, q:q + 4], sm[:, q:q + 4]))
                    link(v.tensor_scalar(sm[:, q + 2:q + 4], sm[:, q + 2:q + 4], neglam, None, ALU.mult))
                    p0, p1 = A_p[:, 2 * (h % 2), :], A_p[:, 2 * (h % 2) + 1, :]
                    v.tensor_scalar(p0[:, 0:P], p0[:, 0:P], sm[:, q:q + 1], None, ALU.mult)
                    link(v.tensor_scalar(p0[:, P:384], p0[:, P:384], sm[:, q + 1:q + 2], None, ALU.mult))
                    if h >= 2:
                        wait_filled(dve, f"at{h - 2}")
                    v.scalar_tensor_tensor(out=A_a[:, h % 2, 0:P], in0=p1[:, 0:P], scalar=sm[:, q + 2:q + 3],
                                           in1=p0[:, 0:P], op0=ALU.mult, op1=ALU.add)
                    v.scalar_tensor_tensor(out=A_a[:, h % 2, P:384], in0=p1[:, P:384], scalar=sm[:, q + 3:q + 4],
                                           in1=p0[:, P:384], op0=ALU.mult, op1=ALU.add).then_inc(S("a_ready"), 1)

                def probs_out(h):
                    n = f"at{h}"
                    wait_filled(dve, n)
                    if h >= 2:
                        wait_filled(dve, f"o{h - 2}")
                    is_drained(v.tensor_copy(A_aT[:, h % 2, :], tile(n)[:, 0:384]), n)

                def o_out(h):
                    n = f"o{h}"
                    wait_filled(dve, n)
                    is_drained(v.tensor_copy(A_o[:, :, h * P:h * P + P], three(tile(n)[:, 0:T], P)), n)

                for h in range(H1 + 2):
                    if h < H1:
                        maxima(h)
                    if 1 <= h <= H1:
                        combine(h - 1)
                        probs_out(h - 1)
                    if h >= 2:
                        o_out(h - 2)
                dve.wait_ge(S("o_rt"), 1)
                link(v.reciprocal(rs[:, 0:8], rt[:, 0:8]))
                for b in range(NB):
                    o4 = three(A_o[:, b, :], P)
                    v.tensor_tensor(o4, o4, rs[:, 4 * b:4 * b + 4].unsqueeze(2).to_broadcast([P, 4, P]), ALU.mult)\
                        .then_inc(S("o_norm"), 1)
                for i in range(2):
                    n = f"oT{i}"
                    wait_filled(dve, n)
                    is_drained(v.tensor_scalar(A_oT[:, 2 * i:2 * i + 2, :], three(tile(n)[:, :], T), sg08, None,
                                               ALU.mult), n)
                for j in range(KT):
                    n = f"up{j}"
                    wait_filled(dve, n)
                    if j >= 2:
                        dve.wait_ge(S("mix_ready"), j - 1)
                    is_drained(v.tensor_tensor(three(A_gt[:, j % 2, :], T), three(tile(n)[:, :], T), A_sig[:, j, :, :],
                                               ALU.mult), n)
                residual("wo")

            if "E" in stages:
                norm_apply("n2", E_xn)
                norm_out("n2", E_hnT, "g2")
                NL = NG + NE
                lg = buf(E_t + 10, NB, NL)
                gap = buf(E_t, NB, 5)
                f1, g1h = buf(E_t + 100, NB, NG), buf(E_t + 120, NB, NG)
                c1, c2, c3, c4 = (buf(E_t + 140 + 2 * k, NB, 1) for k in range(4))
                le, eq = buf(E_t + 200, NB, NE), buf(E_t + 264, NB, NE)
                e1, e2 = buf(E_t + 328, NB, NE), buf(E_t + 392, NB, NE)
                le2, rk = buf(E_t + 456, NB, NE), buf(E_t + 520, NB, NE)
                mem, wt = buf(E_t + 600, NB, NE), buf(E_t + 664, NB, NE)
                n = "route"
                wait_filled(dve, n)
                is_drained(v.tensor_tensor(lg, three(tile(n)[:, 0:NB * NL], NL),
                                           PR("router_b").unsqueeze(1).to_broadcast([P, NB, NL]), ALU.add), n)
                wait_drained(dve, n)

                def first_max(src, k, width, top, hot, tmp):
                    bc = [P, NB, width]
                    rev = C("rev")[:, NE - width:NE].unsqueeze(1).to_broadcast(bc)
                    link(v.tensor_reduce(top, src, AX_X, ALU.max))
                    link(v.tensor_tensor(tmp, src, top.to_broadcast(bc), ALU.is_equal))
                    link(v.tensor_tensor(tmp, tmp, rev, ALU.mult))
                    link(v.tensor_reduce(c4, tmp, AX_X, ALU.max))
                    link(v.tensor_tensor(hot, tmp, c4.to_broadcast(bc), ALU.is_equal))

                first_max(lg[:, :, 0:NG], 0, NG, c1, g1h, f1)
                link(v.tensor_tensor(gap[:, :, 0:NG], lg[:, :, 0:NG], c1.to_broadcast([P, NB, NG]), ALU.subtract))
                link(v.tensor_scalar(g1h, g1h, 1.0, -NEG, ALU.subtract, ALU.mult))
                link(v.tensor_tensor(le.rearrange("p b (g e) -> p b g e", e=EPG),
                                     lg[:, :, NG:NL].rearrange("p b (g e) -> p b g e", e=EPG),
                                     g1h.unsqueeze(3).to_broadcast([P, NB, NG, EPG]), ALU.add))
                first_max(le, 1, NE, c1, e1, eq)
                link(v.scalar_tensor_tensor(out=le2, in0=e1, scalar=-3e38, in1=le, op0=ALU.mult, op1=ALU.add))
                first_max(le2, 2, NE, c2, e2, eq)
                v.tensor_tensor(mem, e1, e2, ALU.add).then_inc(S("member_ready"), 1)
                link(v.tensor_tensor(gap[:, :, NG:5], c2, c1, ALU.subtract))
                v.memset(E_rank, -1.0)
                v.memset(E_w, 0.0).then_inc(S("route_gap"), 1)
                dve.wait_ge(S("route_exp"), 1)
                link(v.tensor_reduce(c1, gap[:, :, 0:NG], AX_X, ALU.add))
                link(v.tensor_scalar(c2, gap[:, :, NG:5], 1.0, None, ALU.add))
                link(v.tensor_tensor(c1, c1, c2, ALU.mult))
                link(v.reciprocal(c3, c1))
                link(v.tensor_tensor(c2, c3, gap[:, :, NG:5], ALU.mult))
                v.tensor_tensor(e1, e1, c3.to_broadcast([P, NB, NE]), ALU.mult)
                link(v.tensor_tensor(e2, e2, c2.to_broadcast([P, NB, NE]), ALU.mult))
                link(v.tensor_tensor(wt, e1, e2, ALU.add))
                n = "rank"
                wait_filled(dve, n)
                cnt = buf(E_t + 740, NE)
                cm, cf = buf(E_t + 780, 1), buf(E_t + 784, 4)
                link(v.tensor_copy(cnt, tile(n)[:, 2 * NE:3 * NE]))
                link(v.tensor_scalar(rk, three(tile(n)[:, 0:2 * NE], NE), 1.0, None, ALU.add))
                link(v.tensor_tensor(rk, rk, mem, ALU.mult))
                is_drained(v.tensor_reduce(cm, cnt, AX_X, ALU.max), n)
                wait_drained(dve, n)
                for p in range(PASSES):
                    v.tensor_scalar(E_rank[:, :, p * NE:(p + 1) * NE], rk, -1.0 - p * SLOTS, None, ALU.add)
                    m = v.tensor_copy(E_w[:, :, p * NE:(p + 1) * NE], wt)
                link(m)
                for k in range(PASSES - 1):
                    m = v.tensor_scalar(cf[:, k:k + 1], cm, float(SLOTS * (k + 1)), float(PAIRS), ALU.is_gt, ALU.mult)
                link(m)
                link(v.tensor_reduce(cf[:, 3:4], cf[:, 0:3], AX_X, ALU.add))
                v.tensor_scalar(steps32[:, :], cf[0:1, 3:4], float(PAIRS), None, ALU.add).then_inc(pairs_known, 1)
                dve.wait_ge(pairs_known, 1)
                A, B, Cb, Dk = bank[4], bank[5], bank[6], bank[7]
                g2 = PR("g2")

                def picks(e):
                    bc = [P, NB, 2, SLOTS]
                    v.tensor_tensor(E_S.rearrange("p b (j s) -> p b j s", s=SLOTS),
                                    C("slot").unsqueeze(1).unsqueeze(1).to_broadcast(bc),
                                    E_rank[:, :, e].unsqueeze(3).to_broadcast(bc), ALU.is_equal)\
                        .then_inc(S("pick_ready"), 1)

                def weighted(e):
                    bc = [P, NB, 2, SLOTS]
                    v.tensor_tensor(E_SW.rearrange("p b (j s) -> p b j s", s=SLOTS),
                                    E_S.rearrange("p b (j s) -> p b j s", s=SLOTS),
                                    E_w[:, :, e].unsqueeze(3).to_broadcast(bc), ALU.mult)\
                        .then_inc(S("weight_ready"), 1)

                def tokens_out(half, sem):
                    v.tensor_tensor(E_xe[:, 4 * half:4 * half + 4, :], three(A[:, :], P),
                                    g2[:, 4 * half:4 * half + 4].unsqueeze(2).to_broadcast([P, 4, P]), ALU.mult)\
                        .then_inc(sem, 1)

                picks(slice(0, 2))
                dve.wait_ge(S("pick_ready"), 1)
                weighted(slice(0, 2))
                dve.wait_ge(S("xlo_mm"), 1)
                tokens_out(0, S("xlo_out"))
                dve.wait_ge(S("xhi_mm"), 1)
                tokens_out(1, S("xhi_out"))
                pairs = dve.value_load(steps32[0:1, 0:1], min_val=PAIRS, max_val=PAIRS * PASSES)
                with dve.Fori(0, pairs) as i:
                    dve.wait_ge(S("xhi_mm"), i + 1)
                    picks(bass.ds(i * 2 + 2, 2))
                    dve.wait_ge(S("pick_ready"), i + 2)
                    dve.wait_ge(S("swt_mm"), i + 1)
                    weighted(bass.ds(i * 2 + 2, 2))
                    dve.wait_ge(moe_up, i + 1)
                    dve.wait_ge(S("sg_ready"), i + 1)
                    v.tensor_tensor(E_hd, Cb[:, :], E_sg, ALU.mult).then_inc(S("hd_ready"), 1)
                    dve.wait_ge(S("xlo_mm"), i + 2)
                    tokens_out(0, S("xlo_out"))
                    dve.wait_ge(S("xhi_mm"), i + 2)
                    tokens_out(1, S("xhi_out"))
                    dve.wait_ge(moe_y0, i + 1)
                    v.tensor_copy(E_y[:, 0, :], B[:, :]).then_inc(S("y0_out"), 1)
                dve.wait_ge(S("scattered"), pairs)
                for b in range(NB):
                    v.tensor_copy(res[:, b, 512:D], bank[2 * b + 1][:, :]).then_inc(S("moe_taken"), 1)

            if "S" in stages:
                if "E" in stages:
                    dve.wait_ge(S("moe_taken"), 4)
                norm_apply("n3", S_xn)
                norm_out("n3", S_uT, "gs")
                v.memset(S_raw[:, :, 0:3], 0.0).then_inc(S("pad_zero"), 1)
                V = lambda k: S_dt[:, k, :]
                n = "dt"
                wait_filled(dve, n)
                is_drained(v.tensor_tensor(three(V(0), SH), three(tile(n)[:, 0:64], SH),
                                           PR("dt_b").unsqueeze(1).to_broadcast([P, NB, SH]), ALU.add), n)
                wait_drained(dve, n)
                link(v.tensor_scalar(V(2), V(0), -1.0, None, ALU.mult))
                v.tensor_tensor(V(2), V(2), V(0), ALU.max).then_inc(S("dt_abs"), 1)
                dve.wait_ge(S("dt_abs"), 1)
                link(v.tensor_scalar(V(0), V(0), 0.0, None, ALU.max))
                dve.wait_ge(S("dt_ln"), 1)
                link(v.tensor_scalar(V(5), V(3), 1.0, None, ALU.add))
                link(v.tensor_scalar(V(5), V(5), 1.0, None, ALU.subtract))
                link(v.tensor_scalar(V(6), V(5), 0.0, None, ALU.is_equal))
                link(v.tensor_tensor(V(5), V(5), V(6), ALU.add))
                link(v.reciprocal(V(5), V(5)))
                link(v.tensor_tensor(V(5), V(5), V(4), ALU.mult))
                link(v.tensor_tensor(V(5), V(5), V(6), ALU.add))
                link(v.tensor_tensor(V(5), V(5), V(3), ALU.mult))
                link(v.tensor_tensor(V(0), V(0), V(5), ALU.add))
                v.scalar_tensor_tensor(out=three(V(1), SH), in0=three(V(0), SH), scalar=-1.0,
                                       in1=V(11)[:, 0:SH].unsqueeze(1).to_broadcast([P, NB, SH]),
                                       op0=ALU.mult, op1=ALU.mult).then_inc(S("a_decay"), 1)
                for j in range(32):
                    ch = (j + 16) % 32
                    wait_drained(dve, f"xbc{j}")
                    for k in range(3):
                        m = v.scalar_tensor_tensor(out=S_cv[:, j % 3, :], in0=S_raw[:, j % 3, k:k + T],
                                                   scalar=PR("conv_w")[:, ch * CONV + k:ch * CONV + k + 1],
                                                   in1=S_cv[:, j % 3, :], op0=ALU.mult, op1=ALU.add)
                        if k < 2:
                            link(m)
                    m.then_inc(S("conv_sum"), 1)
                    if j >= 18:
                        xs_out(j - 18, dve)
                xs_out(14, dve)
                xs_out(15, dve)
                n = "acum"
                wait_filled(dve, n)
                ac = tile(n)
                v.tensor_copy(V(5)[:, 0:SH], ac[:, SH:2 * SH])
                link(v.tensor_scalar(V(7), ac[:, 0:64], -1.0, None, ALU.mult))
                is_drained(v.tensor_tensor(V(5)[:, SH:64], ac[:, 64:96], V(7)[:, 0:SH], ALU.add), n)
                dve.wait_ge(drained[where[n][0]], where[n][1])
                v.tensor_copy(V(6), V(5)).then_inc(S("acum_out"), 1)
                for i in range(2):
                    n = f"Bt{i}"
                    wait_filled(dve, n)
                    is_drained(v.tensor_copy(S_Bt[:, 4 * i:4 * i + 4, :], three(tile(n)[:, :], P)), n)

                def m_mul(i):
                    n = f"cb{i}"
                    wait_filled(dve, n)
                    wait_drained(dve, f"seg{i}")
                    if i >= 2:
                        wait_filled(dve, f"yd{i - 2}")
                    m = v.tensor_tensor(three(S_M[:, i % 2, :], P), three(S_E[:, i % 2, :], P),
                                        tile(n)[:, 0:P].unsqueeze(1).to_broadcast([P, SR, P]), ALU.mult)
                    is_drained(m, n)

                def y_add(i):
                    g, c = divmod(i, 2)
                    n = f"yd{i}"
                    wait_filled(dve, n)
                    dst = S_xs[:, c, g * 256:(g + 1) * 256]
                    dve.wait_ge(S("xd_ready"), i + 1)
                    if c == 1:
                        ea = V(8)[:, g * SR:(g + 1) * SR].unsqueeze(2).to_broadcast([P, SR, SP_])
                        link(v.tensor_tensor(three(S_yo, SP_), three(tile(n)[:, 256:512], SP_), ea, ALU.mult))
                        link(v.tensor_tensor(dst, S_yo, S_xd, ALU.add))
                        link(v.tensor_tensor(dst, tile(n)[:, 0:256], dst, ALU.add))
                    else:
                        link(v.tensor_tensor(dst, tile(n)[:, 0:256], S_xd, ALU.add))
                    is_drained(v.tensor_tensor(dst, dst, S_z[:, c, g * 256:(g + 1) * 256], ALU.mult), n)

                for i in range(2 * SG + 1):
                    if i < 2 * SG:
                        m_mul(i)
                    if i >= 1:
                        y_add(i - 1)
                dve.wait_ge(S("y_rt"), 1)
                link(v.reciprocal(rs[:, :], rt[:, :]))
                for c in range(NB):
                    y8 = three(S_xs[:, c, :], 256)
                    v.tensor_tensor(y8, y8, rs[:, c * SG:(c + 1) * SG].unsqueeze(2).to_broadcast([P, SG, 256]),
                                    ALU.mult).then_inc(S("y_norm"), 1)
                for i in range(8):
                    n = f"yT{i}"
                    wait_filled(dve, n)
                    is_drained(v.tensor_tensor(S_yT[:, 2 * i:2 * i + 2, :], three(tile(n)[:, :], T),
                                               PR("ssm_g")[:, 2 * i:2 * i + 2].unsqueeze(2).to_broadcast([P, 2, T]),
                                               ALU.mult), n)
                residual("so")

            if "M" in stages:
                norm_apply("n4", M_xn)
                norm_out("n4", M_uT, "gm")
                rope = three(C("rope"), T)

                def rotate(n, k):
                    wait_filled(dve, n)
                    is_drained(v.tensor_tensor(three(M_rt[:, k, :], T), three(tile(n)[:, :], T), rope, ALU.mult), n)

                def rotate_queries(i):
                    if i == 1:
                        dve.wait_ge(S("krope_ready"), 1)
                    if i >= 2:
                        dve.wait_ge(S("qrope_ready"), i - 1)
                    rotate(f"qr{i}", i % 2)

                dve.wait_ge(S("lat_rt"), 1)
                rotate("kr", 1)
                link(v.reciprocal(rs[:, 0:4], rt[:, 0:4]))
                for b in range(NB):
                    v.tensor_scalar(M_ckv[:, b, :], M_ckv[:, b, :], rs[:, 2 + b:3 + b], None, ALU.mult)\
                        .then_inc(S("lat_norm"), 1)
                    v.tensor_scalar(M_cq[:, b, :], M_cq[:, b, :], rs[:, b:b + 1], None, ALU.mult)\
                        .then_inc(S("lat_norm"), 1)
                n = "ckvT"
                wait_filled(dve, n)
                is_drained(v.tensor_tensor(M_ckvT, three(tile(n)[:, :], T),
                                           PR("ckv_g").unsqueeze(2).to_broadcast([P, 2, T]), ALU.mult), n)
                for i, (a, z) in enumerate(((0, 2), (2, 3))):
                    n = f"cqT{i}"
                    wait_filled(dve, n)
                    is_drained(v.tensor_tensor(M_cqT[:, a:z, :], three(tile(n)[:, 0:(z - a) * T], T),
                                               PR("cq_g")[:, a:z].unsqueeze(2).to_broadcast([P, z - a, T]),
                                               ALU.mult), n)
                for j in range(4):
                    for b in range(NB):
                        n = f"mv{j}_{b}"
                        wait_filled(dve, n)
                        is_drained(v.tensor_copy(M_v[:, b, j * 512:(j + 1) * 512], tile(n)[:, :]), n)

                def m_max(h):
                    n = f"ms{h}"
                    wait_filled(dve, n)
                    q = 2 * (h % 2)
                    v.tensor_reduce(mx[:, q:q + 1], tile(n)[:, 0:P], AX_X, ALU.max)
                    link(v.tensor_reduce(mx[:, q + 1:q + 2], tile(n)[:, P:384], AX_X, ALU.max))
                    v.tensor_scalar(mx[:, q:q + 2], mx[:, q:q + 2], -MSCALE, None, ALU.mult)\
                        .then_inc(S("mmax_ready"), 1)

                def m_probs(h):
                    wait_drained(dve, f"ms{h}")
                    q = 2 * (h % 2)
                    link(v.reciprocal(sm[:, q:q + 2], sm[:, q:q + 2]))
                    p = M_p[:, h % 2, :]
                    v.tensor_scalar(p[:, 0:P], p[:, 0:P], sm[:, q:q + 1], None, ALU.mult).then_inc(S("mp_ready"), 1)
                    v.tensor_scalar(p[:, P:384], p[:, P:384], sm[:, q + 1:q + 2], None, ALU.mult)\
                        .then_inc(S("mp_ready"), 1)

                def m_pT(h):
                    n = f"mpt{h}"
                    wait_filled(dve, n)
                    if h >= 2:
                        wait_filled(dve, f"mo{h - 2}")
                    is_drained(v.tensor_copy(M_pT[:, h % 2, :], tile(n)[:, 0:384]), n)

                def m_o(h):
                    n = f"mo{h}"
                    wait_filled(dve, n)
                    is_drained(v.tensor_tensor(M_z[:, h, :], tile(n)[:, 0:T], M_z[:, h, :], ALU.mult), n)

                for i in range(MH // 2):
                    wait_drained(dve, f"mz{i}")
                rotate_queries(0)
                for h in range(MH + 2):
                    if h % 2 == 0 and h // 2 + 1 < MH // 2:
                        rotate_queries(h // 2 + 1)
                    if h < MH:
                        m_max(h)
                    if 1 <= h <= MH:
                        m_probs(h - 1)
                        m_pT(h - 1)
                    if h >= 2:
                        m_o(h - 2)
                residual("mo_out")
            dve.wait_ge(S("n5_rt"), 1)
            link(v.reciprocal(rs[:, 0:NB], rt[:, 0:NB]))
            for b in range(NB):
                v.scalar_tensor_tensor(out=F_out[:, b, :], in0=res[:, b, :], scalar=rs[:, b:b + 1], in1=PR("final_g"),
                                       op0=ALU.mult, op1=ALU.mult).then_inc(S("out_ready"), 1)

        @block.gpsimd
        def _(pool):
            g_ = nc.gpsimd
            if "1" in stages:
                W = UPAD + T
                for g, w in enumerate(POOL_WINDOWS):
                    wait_drained(pool, f"u{g}")
                    src, d = A_u[:, g, :], 1
                    for k in range(g + 1):
                        dst = A_pl[:, k % 2, g * W:(g + 1) * W]
                        if k > 0:
                            pool.wait_ge(S("pool_part"), g * (g + 1) // 2 + k)
                        else:
                            pool.wait_ge(S("u_zero"), 1)
                        lo = 2 * d - 1
                        m = g_.tensor_tensor(dst[:, lo:W], src[:, lo:W], src[:, lo - d:W - d], ALU.add)
                        m.then_inc(S("pool_part"), 1)
                        src, d = dst, 2 * d
                for j in range(KT):
                    wait_drained(pool, f"up{j}")
                    g_.tensor_tensor(A_mix[:, j, :], A_gt[:, j % 2, 0:T], A_gt[:, j % 2, T:2 * T], ALU.add)\
                        .then_inc(S("mix_ready"), 1)
            if "S" in stages:
                pool.wait_ge(S("decay_exp"), 1)
                for j in range(16):
                    wait_drained(pool, f"xsT{j}")
                bc = [P, SR, SP_]
                for i in range(2 * SG):
                    g, c = divmod(i, 2)
                    xs = three(S_xs[:, c, g * 256:(g + 1) * 256], SP_)
                    if i >= 2:
                        wait_filled(pool, f"yd{i - 2}")
                    hs = slice(c * SH + g * SR, c * SH + (g + 1) * SR)
                    g_.tensor_tensor(three(S_xdt[:, i % 2, :], SP_), xs,
                                     S_dt[:, 0, hs].unsqueeze(2).to_broadcast(bc), ALU.mult)\
                        .then_inc(S("xdt_ready"), 1)
                    if c == 0:
                        pool.wait_ge(S("xdt_ready"), i + 1)
                        if g >= 1:
                            wait_filled(pool, f"st{g - 1}")
                        g_.tensor_tensor(three(S_xde, SP_), three(S_xdt[:, i % 2, :], SP_),
                                         S_dt[:, 8, SH + g * SR:SH + (g + 1) * SR].unsqueeze(2).to_broadcast(bc),
                                         ALU.mult).then_inc(S("xde_ready"), 1)
                    if i >= 1:
                        wait_drained(pool, f"yd{i - 1}")
                    g_.tensor_tensor(three(S_xd, SP_), xs,
                                     PR("d_skip")[:, g * SR:(g + 1) * SR].unsqueeze(2).to_broadcast(bc), ALU.mult)\
                        .then_inc(S("xd_ready"), 1)
            if "M" in stages:
                wait_drained(pool, "kr")
                g_.tensor_tensor(M_kr, M_rt[:, 1, 0:T], M_rt[:, 1, T:512], ALU.add).then_inc(S("krope_ready"), 1)
                for i in range(MH // 2):
                    wait_drained(pool, f"qr{i}")
                    if i >= 2:
                        wait_filled(pool, f"ms{2 * i - 3}")
                    g_.tensor_tensor(M_qr[:, i % 2, :], M_rt[:, i % 2, 0:T], M_rt[:, i % 2, T:512], ALU.add)\
                        .then_inc(S("qrope_ready"), 1)

        @block.sync
        def _(sp):
            sp.dma_start(res[:, :, :], x.rearrange("(b p) d -> p b d", p=P)).then_inc(S("loaded_x"), 16)
            sp.dma_start(con[:, :], consts).then_inc(S("loaded_con"), 16)
            sp.dma_start(par[:, :], params).then_inc(S("loaded_par"), 16)

            def load(slot, c, sem):
                sp.dma_start(ring[:, slot, :], weights[c, :, :]).then_inc(sem, 16)

            def load_at(slot, c, sem):
                sp.dma_start(ring[:, slot:slot + 1, :], weights[bass.ds(c, 1), :, :].rearrange("c p n -> p c n"))\
                    .then_inc(sem, 16)

            if "1" in stages:
                for c in range(CHUNKS_A):
                    if c >= RING:
                        sp.wait_ge(*last_use["a"][c - RING])
                    load(c % RING, c, full_a[c % RING])
            released = (moe_gate, moe_gate, moe_up, moe_up, moe_y1, moe_y1)
            if "E" in stages:
                for s in range(RING):
                    if "1" in stages:
                        sp.wait_ge(*last_use["a"][CHUNKS_A - RING + s])
                    load(s, CHUNKS_A + s, full_a[s])
                with sp.Fori(1, PAIRS) as i:
                    for s in range(RING):
                        sp.wait_ge(released[s], i)
                        load_at(s, CHUNKS_A + RING * i + s, full_a[s])
                sp.wait_ge(pairs_known, 1)
                pairs = sp.value_load(steps32[0:1, 0:1], min_val=PAIRS, max_val=PAIRS * PASSES)
                with sp.If(pairs > PAIRS):
                    with sp.Fori(PAIRS, pairs, PAIRS) as first:
                        with sp.Fori(0, PAIRS) as k:
                            for s in range(RING):
                                sp.wait_ge(released[s], first + k)
                                load_at(s, CHUNKS_A + RING * k + s, full_a[s])
            first_b = CHUNKS_A + CHUNKS_E
            if "S" in stages or "M" in stages:
                nB = (CHUNKS_S if "S" in stages else 0) + (CHUNKS_M if "M" in stages else 0)
                off = 0 if "S" in stages else CHUNKS_S
                for c in range(nB):
                    if c < RING and "E" in stages:
                        sp.wait_ge(released[c], pairs)
                    if c >= RING:
                        sp.wait_ge(*last_use["b"][c - RING])
                    load(c % RING, first_b + off + c, full_b[c % RING])
            for b in range(NB):
                sp.wait_ge(S("out_ready"), b + 1)
                sp.dma_start(out[b * P:(b + 1) * P, :], F_out[:, b, :]).then_inc(S("stored"), 16)
            sp.wait_ge(S("stored"), 16 * NB)
    return nc


def pack(inp):
    f = lambda n: np.asarray(inp[n], dtype=np.float32)
    chunks = []

    def chunk(w):
        rows, width = w.shape
        a = w.reshape(rows // P, P, width).transpose(1, 0, 2).reshape(P, -1)
        if a.shape[1] < SLOT:
            a = np.concatenate([a, np.zeros((P, SLOT - a.shape[1]), np.float32)], axis=1)
        chunks.append(a)

    w = f("w_in")[0]
    for c in (1, 2, 3, 0, 4, 5, 6, 7):
        chunk(w[:, c * 512:(c + 1) * 512])
    chunk(f("w_pool_up")[0])
    chunk(f("w_attn_up")[0])
    for c in range(2):
        chunk(f("w_out")[0][:, c * 512:(c + 1) * 512])
    wg, wu, wd = f("w_expert_gate")[0], f("w_expert_up")[0], f("w_expert_down")[0]
    for e in range(0, NE, 2):
        for m in (wg, wu, wd):
            chunk(m[e])
            chunk(m[e + 1])
    w = f("ssm_in_w_2")[0]
    di, bc = 2048, 1024
    xbc = w[:, di:di + di + 2 * bc]
    for c in (4, 5, 6, 7, 0, 1, 2, 3):
        chunk(xbc[:, c * 512:(c + 1) * 512])
    for c in range(4):
        chunk(w[:, c * 512:(c + 1) * 512])

    def out_chunks(w):
        for half in range(2):
            for q in range(2):
                chunk(w[q * 1024:(q + 1) * 1024, half * 512:(half + 1) * 512])

    out_chunks(f("ssm_out_w_2")[0])
    w = f("mla_in_w_2")[0]
    chunk(w[:, 0:MQL])
    o = MQL + MKVL
    kr = w[:, o:o + MR]
    krs = np.concatenate([kr[:, MR // 2:], kr[:, :MR // 2]], axis=1)
    chunk(np.concatenate([w[:, MQL:o], kr, kr, krs, krs], axis=1))
    for c in range(4):
        chunk(w[:, o + MR + c * 512:o + MR + (c + 1) * 512])
    w = f("mla_ukv_w_2")[0].reshape(MKVL, MH, 2, P)
    chunk(np.ascontiguousarray(w[:, :, 0]).reshape(MKVL, -1))
    chunk(np.ascontiguousarray(w[:, :, 1]).reshape(MKVL, -1))
    w = f("mla_uq_w_2")[0].reshape(MQL, MH, P + MR)
    for i in range(0, MH, 4):
        cols = []
        for h in (i, i + 2):
            r0, r1 = w[:, h, P:], w[:, h + 1, P:]
            sw = lambda r: np.concatenate([r[:, MR // 2:], r[:, :MR // 2]], axis=1)
            cols += [w[:, h, :P], w[:, h + 1, :P], r0, r1, sw(r0), sw(r1)]
        chunk(np.concatenate(cols, axis=1))
    out_chunks(f("mla_out_w_2")[0])
    weights = np.stack(chunks)

    tiles = lambda v: v.reshape(-1, P).T
    wide = lambda v: np.broadcast_to(v.reshape(1, -1), (P, v.size))
    rows = lambda w: w.reshape(w.shape[0] // P, P, -1).transpose(1, 0, 2).reshape(P, -1)
    ssm_in = f("ssm_in_w_2")[0]
    parts = dict(
        g1=tiles(f("norm1_g")[0]), g2=tiles(f("norm2_g")[0]), gs=tiles(f("norm_w_2")[0]), gm=tiles(f("norm_w_2")[1]),
        pool_scale=tiles(f("pool_scale")[0]), qg=np.tile(f("q_norm_g")[0], 2)[:, None],
        kg=np.tile(f("k_norm_g")[0], 2)[:, None], subln=f("subln_g")[0][:, None],
        lam=wide(np.concatenate([f(n)[0] for n in ("lambda_q1", "lambda_k1", "lambda_q2", "lambda_k2")])),
        router_b=wide(np.concatenate([f("b_router_group")[0], f("b_router_expert")[0]])),
        conv_w=f("ssm_conv_w_2")[0].T.reshape(32, P, CONV).transpose(1, 0, 2).reshape(P, -1),
        conv_b=tiles(f("ssm_conv_b_2")[0]), dt_b=wide(f("ssm_dt_bias_2")[0]), a_log=wide(f("ssm_A_log_2")[0]),
        d_skip=wide(f("ssm_D_2")[0]), ssm_g=tiles(f("ssm_norm_w_2")[0]), cq_g=tiles(f("mla_q_norm_w_2")[0]),
        ckv_g=tiles(f("mla_kv_norm_w_2")[0]),
        router_w=rows(np.concatenate([f("w_router_group")[0], f("w_router_expert")[0]], axis=1)),
        pool_w=f("pool_w")[0].transpose(1, 0, 2).reshape(P, -1), dt_w=rows(ssm_in[:, 6144:6176]),
        final_g=wide(f("final_norm_w_2")))
    params = np.concatenate([parts[n].reshape(P, -1) for n in PARAM_WIDTHS], axis=1)
    assert params.shape[1] == NPARAM
    return weights, np.ascontiguousarray(params)


def kernel(**inputs):
    import concourse.bacc as bacc
    from concourse.bass_utils import run_bass_kernel_spmd

    nc = bacc.Bacc("TRN2", target_bir_lowering=False, num_devices=1)
    weights, params = pack(inputs)
    cmap, consts = constants()
    arrays = {"weights_dram": weights, "params_dram": params, "consts_dram": consts,
              "x_dram": np.ascontiguousarray(np.asarray(inputs["x"], dtype=np.float32)[0])}
    aps = [nc.dram_tensor(n, a.shape, F32, kind="ExternalInput").ap() for n, a in arrays.items()]
    out = nc.dram_tensor("out_dram", (T, D), F32, kind="ExternalOutput").ap()
    program(nc, *aps, out, cmap)
    r = run_bass_kernel_spmd(nc, [arrays], core_ids=[0])
    return np.asarray(r.results[0]["out_dram"]).reshape(1, T, D)
```

```python
import math
from contextlib import ExitStack

import numpy as np
import concourse.bass as bass
from concourse import mybir

F32 = mybir.dt.float32
F32R = mybir.dt.float32r
BF16 = mybir.dt.bfloat16
I32 = mybir.dt.int32
ALU = mybir.AluOpType
ACT = mybir.ActivationFunctionType
AX_X = mybir.AxisListType.X

P = 128
T = 256
NB = T // P
D = 1024
KT = D // P
EPS = 1e-6
NEG = -1e30
LAMBDA_INIT = 0.8 - 0.6 * math.exp(-0.3 * 0)

H1, HD1 = 4, 64
POOL_WINDOWS = (2, 4, 8, 16)
UPAD = 16

NE, EPG, NG = 32, 8, 4
SLOTS = 64
PASSES = T // SLOTS
PAIRS = NE // 2
ROUNDS = PAIRS // 2
MORE = ROUNDS * (PASSES - 1)

SG, SR, SP_, SN = 8, 4, 64, 128
SH = SG * SR
CONV = 4
ATTEND_AT = (5, 7, 9, 11, 13, 15)

MH = 16
MQL, MKVL, MR = 384, 256, 64
MSCALE = (128 + MR) ** -0.5

PIECE = 1024
UNIT = 2 * PIECE
RING = 8
WBUFS = 3
PIECES_A = 48
PIECES_S = 65
PIECES_M = 64
UNITS_A = PIECES_A // 2
UNITS_E = NE * 6
PAIR_UNITS = 12


def constants():
    c, at, parts = {}, 0, []

    def put(name, a):
        nonlocal at
        a = np.ascontiguousarray(a, dtype=np.float32).reshape(P, -1)
        c[name] = (at, a.shape[1])
        at += a.shape[1]
        parts.append(a)

    i = np.arange(P)
    def put_bf16(name, a):
        bits = np.ascontiguousarray(a, dtype=np.float32).view(np.uint32) >> 16
        put(name, np.ascontiguousarray(bits[:, 0::2] | (bits[:, 1::2] << 16)).view(np.float32))

    put("ident", np.eye(P))
    put("eps", np.full((P, 1), EPS))
    put("upto", i[:, None] <= i[None, :])
    put("before", i[:, None] < i[None, :])
    put("ones", np.ones((P, P)))
    put("halves", (i[:, None] // HD1) == (i[None, :] // HD1))
    put_bf16("ident16", np.eye(P))
    put_bf16("future", np.where(i[:, None] <= i[None, :], 0.0, NEG))
    dist = np.concatenate([i[:, None] - i[None, :], i[:, None] + P - np.arange(T)[None, :]], axis=1)
    put_bf16("causal", np.where(dist >= 0, 0.0, NEG))
    slopes = [2.0 ** (-8.0 * (h + 1) / H1) for h in range(H1)]
    put_bf16("alibi", np.concatenate([np.where(dist >= 0, -s * dist, NEG) for s in slopes], axis=1))
    half = MR // 2
    inv = (500000.0 ** (-np.arange(half, dtype=np.float32) / np.float32(half))).astype(np.float32)
    ang = inv[:, None] * np.arange(T, dtype=np.float32)[None, :]
    cos, sin = np.cos(ang), np.sin(ang)
    put("rope", np.concatenate([np.tile(cos, (4, 1)), np.tile(np.concatenate([-sin, sin]), (2, 1))], axis=1))
    put("slot", np.tile(np.arange(SLOTS), (P, 1)))
    put("rev", np.tile(np.arange(NE, 0, -1), (P, 1)))
    put("count", np.tile(np.concatenate([1.0 / np.minimum(np.arange(UPAD) + 1, w) for w in POOL_WINDOWS]), (P, 1)))
    return c, np.concatenate(parts, axis=1)


PARAM_WIDTHS = dict(
    g1=KT, g2=KT, gs=KT, gm=KT, pool_scale=4, qg=1, kg=1, subln=1, lam=4 * HD1, router_b=NG + NE,
    conv_w=32 * CONV, conv_b=32, dt_b=SH, a_log=SH, d_skip=SH, ssm_g=16, cq_g=3, ckv_g=2,
    router_w=KT * (NG + NE), pool_w=4 * P)
PARAMS, _at = {}, 0
for _n, _w in PARAM_WIDTHS.items():
    PARAMS[_n] = (_at, _w)
    _at += _w
NPARAM = _at


def program(nc, weights, params, consts, x, final_g, out, cmap, stages="1ESM"):
    NCONST = sum(w for _, w in cmap.values())
    ctx = ExitStack()
    with ctx:
        def sbuf(name, shape, dt=F32):
            return ctx.enter_context(nc.sbuf_tensor(name, shape, dt))

        ring = sbuf("ring", [P, RING, UNIT])
        w_hi, w_lo = sbuf("w_hi", [P, WBUFS, PIECE], F32R), sbuf("w_lo", [P, WBUFS, PIECE], F32R)
        x_hi, x_lo = sbuf("x_hi", [P, 16, T], F32R), sbuf("x_lo", [P, 16, T], F32R)
        a_hi, a_lo = sbuf("a_hi", [P, 2 * SH], F32R), sbuf("a_lo", [P, 2 * SH], F32R)
        upto = sbuf("upto_r", [P, P], F32R)
        con = sbuf("con", [P, NCONST])
        par = sbuf("par", [P, NPARAM])
        res = sbuf("res", [P, NB, D])
        work = sbuf("work", [P, 18240])
        small = sbuf("small", [P, 96])
        more32 = sbuf("more32", [1, 1], I32)
        bank = [ctx.enter_context(nc.psum_tensor(f"bank{b}", [P, 512], F32)) for b in range(8)]

        def C(name):
            o, w = cmap[name]
            return con[:, o:o + w]

        def C16(name):
            return C(name).bitcast(BF16)

        def PR(name):
            o, w = PARAMS[name]
            return par[:, o:o + w]

        def view(t, at, *shape):
            n = int(np.prod(shape))
            v = t[:, at:at + n]
            if len(shape) == 2:
                v = v.rearrange("p (a b) -> p a b", b=shape[1])
            if len(shape) == 3:
                v = v.rearrange("p (a b c) -> p a b c", b=shape[1], c=shape[2])
            return v

        def buf(at, *shape):
            return view(work, at, *shape)

        def three(ap, b):
            return ap.rearrange("p (a b) -> p a b", b=b)

        def four(ap, b, c):
            return ap.rearrange("p (a b c) -> p a b c", b=b, c=c)

        sems = {}

        def S(name):
            if name not in sems:
                sems[name] = ctx.enter_context(nc.semaphore(name))
            return sems[name]

        ident = C("ident")
        eps = C("eps")

        filled = [S(f"filled{b}") for b in range(8)]
        drained = [S(f"drained{b}") for b in range(8)]
        where, used, turn = {}, [0] * 8, [0]

        def new_tile(pe, name):
            b = turn[0] % 8
            turn[0] += 1
            used[b] += 1
            where[name] = (b, used[b])
            if used[b] > 1:
                pe.wait_ge(drained[b], used[b] - 1)
            return bank[b]

        def is_filled(ins, name):
            ins.then_inc(filled[where[name][0]], 1)
            piece_at[name] = len(last_use)

        def wait_filled(e, name):
            e.wait_ge(filled[where[name][0]], where[name][1])

        def is_drained(ins, name):
            ins.then_inc(drained[where[name][0]], 1)

        def wait_drained(e, name):
            e.wait_ge(drained[where[name][0]], where[name][1])

        def tile(name):
            return bank[where[name][0]]

        def chain(e, name):
            n = [0]

            def link(ins):
                n[0] += 1
                ins.then_inc(S(name), 1)
                e.wait_ge(S(name), n[0])
            return link

        raw_a = [S(f"raw_a{s}") for s in range(RING)]
        raw_b = [S(f"raw_b{s}") for s in range(RING)]
        split_hi, split_lo = S("split_hi"), S("split_lo")
        last_use = []
        piece_at, hi_at = {}, {}
        units_used = S("units_used")

        def slot_of(n):
            return (n // 2 if n < first_b else (n - first_b) // 2) % RING

        def raw_wait(e, n):
            u = n // 2 if n < first_b else (n - first_b) // 2
            e.wait_ge((raw_a if n < first_b else raw_b)[u % RING], 16 * (u // RING + 1))

        first_b = PIECES_A if "1" in stages else 0
        first_m = first_b + (PIECES_S if "S" in stages else 0)
        pairs_known = S("pairs_known")

        ss, rt, rs = small[:, 0:16], small[:, 16:32], small[:, 32:48]
        lamv, neglam = small[:, 48:52], small[:, 52:53]
        mx, sm = small[:, 56:72], small[:, 72:88]
        qg8 = small[:, 88:89]
        sg08 = small[:, 89:90]

        A_xn, A_u, A_qk = buf(0, NB, D), buf(2048, 4, UPAD + T), buf(3136, 8, T)
        A_v, A_sig = buf(5184, NB, 512), buf(6208, KT, 2, T)
        A_sq, A_o, A_gt = buf(10304, 8, T), buf(10304, NB, 512), buf(11328, 2, 512)
        A_pl, A_dT = buf(12352, 2, 4 * (UPAD + T)), buf(14528, 4, T)
        A_junk, A_m32 = buf(12352, 8, P), buf(13376, 4, T)
        A_p, A_a, A_aT = buf(15552, 4, 384), buf(0, 2, 384), buf(768, 2, 384)
        A_lj = buf(17100, 2, HD1)

        E_xn, E_hnT, E_xe = buf(0, NB, D), buf(2048, KT, T), buf(4096, KT, P)
        E_S, E_SW, E_SWT = buf(5120, NB, P), buf(5376, NB, P), buf(5632, T)
        E_sg, E_hd, E_hdT = buf(5888, 512), buf(6400, 512), buf(6912, 4, P)
        E_y = buf(7424, 2, 512)
        XW = PASSES * NE + 2
        E_rank, E_w = buf(8448, NB, XW), buf(8448 + 2 * XW, NB, XW)
        E_t = 9000

        S_xn = buf(4096, NB, D)
        S_BT, S_CT = buf(0, SG, T), buf(2048, SG, T)
        S_junk = buf(0, 16, T)
        S_xs, S_z = buf(4096, NB, 2048), buf(8192, NB, 2048)
        S_raw, S_cv, S_xsT = buf(12288, 3, 260), buf(13068, 3, T), buf(13836, 3, T)
        S_E, S_M = buf(12288, 2, 512), buf(13312, 2, 512)
        S_dt = buf(14604, 12, 64)
        S_xdt, S_xde = buf(15372, 2, 256), buf(15884, 256)
        S_Bt, S_st, S_yo, S_xd = buf(16140, SG, P), buf(17164, 2, 256), buf(17676, 256), buf(17932, 256)

        M_xn, M_cq, M_ckv = buf(0, NB, D), buf(2048, NB, MQL), buf(2816, NB, MKVL)
        M_kr, M_rt = buf(3328, T), buf(3584, 2, 512)
        M_z, M_kn, M_v = buf(4608, MH, T), buf(8704, MH, T), buf(12800, NB, 2048)
        M_junk = buf(8704, 4, 512)
        M_qn, M_qr = buf(0, 4, T), buf(1024, 2, T)
        M_p, M_pT = buf(1536, 2, 384), buf(2304, 2, 384)
        F_out, F_g = buf(4608, NB, D), buf(17000, D)
        ckv0, cq0 = 8, 13

        def splitter(e, limit, split):
            done = [0]

            def until(n):
                while done[0] <= min(n, limit[0] - 1):
                    split(done[0])
                    done[0] += 1
            return until

        def conv_silu(j, act):
            act.wait_ge(S("conv_sum"), j + 1)
            if j < 8:
                dst = S_BT[:, j, :]
            elif j < 16:
                dst = S_CT[:, j - 8, :]
            else:
                if j >= 19:
                    wait_filled(act, f"xsT{j - 19}")
                dst = S_xsT[:, (j - 16) % 3, :]
            nc.scalar.activation(dst, S_cv[:, j % 3, :], ACT.Silu).then_inc(S("conv_out"), 1)

        def xs_out(j, await_tile):
            n = f"xsT{j}"
            await_tile(n)
            is_drained(nc.vector.tensor_copy(S_xs[:, :, j * P:j * P + P], three(tile(n)[:, 0:T], P)), n)

        block = ctx.enter_context(nc.Block())

        @block.tensor
        def _(pe):
            def next_piece():
                n = len(last_use)
                pe.wait_ge(split_lo, n + 1)
                return n

            def piece_used(name=None, sem=None, count=0):
                if name is not None:
                    sem, count = filled[where[name][0]], where[name][1]
                last_use.append((sem, count))

            def products(out, a, b, first, last):
                for i, (p, q) in enumerate(((0, 0), (0, 1), (1, 0))):
                    m = pe.matmul(out, a[p], b[q], start=first and i == 0, stop=last and i == 2)
                return m

            def wpart(n, at, width):
                return [w[:, n % WBUFS, at:at + width] for w in (w_hi, w_lo)]

            def xpart(k, lo=0, hi=T):
                return [x_[:, k, lo:hi] for x_ in (x_hi, x_lo)]

            part_count = [0]

            def token_piece(names, n, kts, k0, kall, width, x0):
                if k0 == 0:
                    ts = [new_tile(pe, nm) for nm in names]
                    token_piece.ts = ts
                ts = token_piece.ts
                for b in range(NB):
                    for k in range(kts):
                        m = products(ts[b][:, 0:width], xpart(x0 + k0 + k, b * P, b * P + P),
                                     wpart(n, k * width, width), k0 + k == 0, k0 + k == kall - 1)
                    if k0 + kts == kall:
                        is_filled(m, names[b])
                if k0 + kts == kall:
                    piece_used(names[1])
                else:
                    part_count[0] += 1
                    m.then_inc(S("part_done"), 1)
                    piece_used(sem=S("part_done"), count=part_count[0])

            def token_tiles(names, kall, kts, width, x0):
                for k0 in range(0, kall, kts):
                    token_piece(names, next_piece(), kts, k0, kall, width, x0)

            def channels(t, c0, n, at, step, kts, x0):
                for k in range(kts):
                    m = products(t[:, c0:c0 + T], wpart(n, at + k * step, P), xpart(x0 + k), k == 0, k == kts - 1)
                return m

            def channel_tile(name, kts=KT, x0=0):
                n = next_piece()
                t = new_tile(pe, name)
                is_filled(channels(t, 0, n, 0, P, kts, x0), name)
                piece_used(name)

            def channel_pair(name, kts=KT, x0=0):
                t = new_tile(pe, name)
                n = next_piece()
                part_count[0] += 1
                channels(t, 0, n, 0, P, kts, x0).then_inc(S("part_done"), 1)
                piece_used(sem=S("part_done"), count=part_count[0])
                n = next_piece()
                is_filled(channels(t, T, n, 0, P, kts, x0), name)
                piece_used(name)

            def norm_T(tag, xn):
                pe.wait_ge(S(tag + "_xn"), NB)
                for i in range(KT // 2):
                    t = new_tile(pe, f"{tag}_T{i}")
                    for k in range(2):
                        for b in range(NB):
                            m = pe.transpose(t[:, k * T + b * P:k * T + b * P + P],
                                             xn[:, b, (2 * i + k) * P:(2 * i + k + 1) * P], ident)
                    is_filled(m, f"{tag}_T{i}")

            def norm_T_wait(tag):
                for i in range(KT // 2):
                    wait_drained(pe, f"{tag}_T{i}")

            def out_tiles(tag, kall):
                for half in range(2):
                    token_tiles([f"{tag}{half}_{b}" for b in range(NB)], kall, 2, 512, 0)

            pe.wait_ge(S("loaded_con"), 16)
            if "1" in stages:
                norm_T("n1", A_xn)
                norm_T_wait("n1")
                for j in range(8):
                    channel_tile(f"qk{j}")
                token_tiles(["v0", "v1"], KT, 2, 512, 0)
                for j in range(4):
                    channel_tile(f"u{j}")
                for i in range(4):
                    n = f"sq{i}"
                    t = new_tile(pe, n)
                    pe.wait_ge(S("sq_ready"), i + 1)
                    is_filled(pe.matmul(t[:, :], C("halves"), A_sq[:, 2 * i:2 * i + 2, :], start=True, stop=True), n)

                def scores(h):
                    for m_ in range(2):
                        n = f"s{h}_{m_}"
                        t = new_tile(pe, n)
                        lo = 64 * m_
                        pe.matmul(t[:, 0:384], C16("ident16"), C16("alibi")[:, h * 384:(h + 1) * 384], start=True, stop=False,
                                  skip_group_check=True)
                        pe.matmul(t[:, 0:P], A_qk[lo:lo + 64, h, 0:P], A_qk[lo:lo + 64, 4 + h, 0:P],
                                  start=False, stop=False, skip_group_check=True)
                        is_filled(pe.matmul(t[:, P:384], A_qk[lo:lo + 64, h, P:T], A_qk[lo:lo + 64, 4 + h, :],
                                            start=False, stop=True, skip_group_check=True), n)

                def turn_probs(h):
                    n = f"at{h}"
                    t = new_tile(pe, n)
                    pe.wait_ge(S("a_ready"), h + 1)
                    for j in range(3):
                        m = pe.transpose(t[:, j * P:j * P + P], A_a[:, h % 2, j * P:j * P + P], ident)
                    is_filled(m, n)

                def values(h):
                    n = f"o{h}"
                    t = new_tile(pe, n)
                    wait_drained(pe, f"at{h}")
                    if h == 0:
                        wait_drained(pe, "v0")
                        wait_drained(pe, "v1")
                    aT = A_aT[:, h % 2, :]
                    pe.matmul(t[:, 0:P], aT[:, 0:P], A_v[:, 0, h * P:h * P + P], start=True, stop=True)
                    pe.matmul(t[:, P:T], aT[:, P:T], A_v[:, 0, h * P:h * P + P], start=True, stop=False)
                    is_filled(pe.matmul(t[:, P:T], aT[:, T:384], A_v[:, 1, h * P:h * P + P],
                                        start=False, stop=True), n)

                def attend(h):
                    if h < H1:
                        scores(h)
                    if 1 <= h <= H1:
                        turn_probs(h - 1)
                    if h >= 2:
                        values(h - 2)

                for j in range(16):
                    channel_tile(f"gate{j}")
                    if j == ATTEND_AT[0]:
                        pe.wait_ge(S("qk_ready"), 4)
                    if j in ATTEND_AT:
                        attend(ATTEND_AT.index(j))
                for g in range(4):
                    n = f"pw{g}"
                    t = new_tile(pe, n)
                    pe.wait_ge(S("pool_d"), g + 1)
                    is_filled(pe.matmul(t[:, 0:T], PR("pool_w")[:, g * P:g * P + P], A_dT[:, g, :],
                                        start=True, stop=True), n)
                pe.wait_ge(S("o_norm"), NB)
                for i in range(2):
                    n = f"oT{i}"
                    t = new_tile(pe, n)
                    for k in range(2):
                        for b in range(NB):
                            m = pe.transpose(t[:, k * T + b * P:k * T + b * P + P],
                                             A_o[:, b, (2 * i + k) * P:(2 * i + k + 1) * P], ident)
                    is_filled(m, n)
                for g in range(4):
                    wait_drained(pe, f"pw{g}")
                for i in range(2):
                    wait_drained(pe, f"oT{i}")
                for j in range(KT):
                    nm = f"up{j}"
                    n = next_piece()
                    t = new_tile(pe, nm)
                    channels(t, 0, n, 0, P, 4, 8)
                    is_filled(channels(t, T, n, 4 * P, P, 4, 12), nm)
                    piece_used(nm)
                pe.wait_ge(S("mix_ready"), KT)
                for c in range(2):
                    token_tiles([f"wo{c}_{b}" for b in range(NB)], KT, 2, 512, 0)

            if "E" in stages:
                norm_T("n2", E_xn)
                norm_T_wait("n2")
                n = "route"
                t = new_tile(pe, n)
                NL = NG + NE
                for b in range(NB):
                    for k in range(KT):
                        m = pe.matmul(t[:, b * NL:(b + 1) * NL], E_hnT[:, k, b * P:b * P + P],
                                      PR("router_w")[:, k * NL:(k + 1) * NL], start=(k == 0), stop=(k == KT - 1))
                is_filled(m, n)
                n = "rank"
                t = new_tile(pe, n)
                pe.wait_ge(S("member_ready"), 1)
                mem = buf(E_t + 600, NB, NE)
                pe.matmul(t[:, 0:NE], C("before"), mem[:, 0, :], start=True, stop=True)
                pe.matmul(t[:, NE:2 * NE], C("ones"), mem[:, 0, :], start=True, stop=False)
                pe.matmul(t[:, NE:2 * NE], C("before"), mem[:, 1, :], start=False, stop=True)
                pe.matmul(t[:, 2 * NE:3 * NE], C("ones"), mem[:, 0, :], start=True, stop=False)
                is_filled(pe.matmul(t[:, 2 * NE:3 * NE], C("ones"), mem[:, 1, :], start=False, stop=True), n)
                for b in range(8):
                    if used[b]:
                        pe.wait_ge(drained[b], used[b])
                for b in range(NB):
                    for j in range(2):
                        m = pe.matmul(bank[2 * b + j][:, :], ident, res[:, b, j * 512:(j + 1) * 512],
                                      start=True, stop=False, skip_group_check=True)
                A, B, Cb, Dk = bank[4], bank[5], bank[6], bank[7]

                def gather(half, sem):
                    for k in range(4):
                        for b in range(NB):
                            kk = 4 * half + k
                            m = pe.matmul(A[:, k * P:k * P + P], E_xn[:, b, kk * P:kk * P + P], E_S[:, b, :],
                                          start=(b == 0), stop=(b == NB - 1))
                    m.then_inc(sem, 1)

                pe.wait_ge(S("pick_ready"), 1)
                gather(0, S("xlo_mm"))
                pe.wait_ge(S("xlo_out"), 1)
                gather(1, S("xhi_mm"))
                pe.wait_ge(pairs_known, 1)
                rounds = pe.value_load(more32[0:1, 0:1], min_val=0, max_val=MORE) + ROUNDS
                base = UNITS_A // RING if "1" in stages else 0
                with pe.Fori(0, rounds) as it:
                    for two in range(2):
                        i = it * 2 + two
                        pe.wait_ge(S("weight_ready"), i + 1)
                        pe.wait_ge(S("xhi_out"), i + 1)
                        for b in range(NB):
                            m = pe.transpose(A[:, b * P:b * P + P], E_SW[:, b, :], ident)
                        m.then_inc(S("swt_mm"), 1)

                        def unit(k, t, lhs, first, last):
                            u = PAIR_UNITS * two + k
                            pe.wait_ge(raw_a[u % RING], it * (16 * 3) + 16 * (base + 1 + u // RING))
                            for c in range(2):
                                for j in range(2):
                                    m = pe.matmul(t[64 * j:64 * j + 64, :], lhs(c)[:, 64 * j:64 * j + 64],
                                                  ring[:, u % RING, (2 * j + c) * 512:(2 * j + c + 1) * 512],
                                                  start=first and c == 0, stop=last and c == 1)
                            m.then_inc(units_used, 1)

                        for q, t in enumerate((B, Cb)):
                            for k in range(4):
                                unit(4 * q + k, t, lambda c: E_xe[:, 2 * k + c, :], k == 0, k == 3)
                        pe.wait_ge(S("pick_ready"), i + 2)
                        pe.wait_ge(S("swt_out"), i + 1)
                        gather(0, S("xlo_mm"))
                        pe.wait_ge(S("hd_ready"), i + 1)
                        for k in range(4):
                            m = pe.transpose(Dk[:, k * P:k * P + P], E_hd[:, k * P:k * P + P], ident)
                        m.then_inc(S("hdt_mm"), 1)
                        pe.wait_ge(S("xlo_out"), i + 2)
                        gather(1, S("xhi_mm"))
                        pe.wait_ge(S("hdt_out"), i + 1)
                        for q, t in enumerate((B, Cb)):
                            for k in range(2):
                                unit(8 + 2 * q + k, t, lambda c: E_hdT[:, 2 * k + c, :], k == 0, k == 1)
                        for q, sem in enumerate((S("y0_out"), S("y1_out"))):
                            pe.wait_ge(sem, i + 1)
                            for b in range(NB):
                                m = pe.matmul(bank[2 * b + q][:, :], E_SWT[:, b * P:b * P + P], E_y[:, q, :],
                                              start=False, stop=False, skip_group_check=True)
                        m.then_inc(S("scattered"), 1)
                pe.wait_ge(S("moe_taken"), 4)

            if "S" in stages:
                norm_T("n3", S_xn)
                norm_T_wait("n3")
                nm, n = "dt", next_piece()
                t = new_tile(pe, nm)
                for b in range(NB):
                    for k in range(KT):
                        m = products(t[:, b * SH:(b + 1) * SH], xpart(k, b * P, b * P + P), wpart(n, k * SH, SH),
                                     k == 0, k == KT - 1)
                is_filled(m, nm)
                piece_used(nm)

                def turn_xs(j):
                    n = f"xsT{j}"
                    t = new_tile(pe, n)
                    pe.wait_ge(S("conv_out"), 16 + j + 1)
                    for b in range(NB):
                        m = pe.transpose(t[:, b * P:b * P + P], S_xsT[:, j % 3, b * P:b * P + P], ident)
                    is_filled(m, n)

                for j in range(32):
                    channel_tile(f"xbc{j}")
                    if j >= 18:
                        turn_xs(j - 18)
                for c in range(4):
                    token_tiles([f"z{c}_{b}" for b in range(NB)], KT, 2, 512, 0)
                    if c == 0:
                        turn_xs(14)
                        turn_xs(15)
                n = "acum"
                t = new_tile(pe, n)
                pe.wait_ge(S("a_decay"), 3)
                av = S_dt[:, 1, :]
                pe.matmul(t[:, 0:64], C("upto"), av, start=True, stop=True)
                is_filled(pe.matmul(t[:, 64:96], C("ones"), av[:, 0:SH], start=True, stop=True), n)
                for i in range(2):
                    n = f"Bt{i}"
                    t = new_tile(pe, n)
                    for k in range(4):
                        m = pe.transpose(t[:, k * P:k * P + P], S_BT[:, 4 * i + k, 0:P], ident)
                    is_filled(m, n)
                for i in range(2):
                    wait_drained(pe, f"Bt{i}")
                for j in range(16):
                    wait_drained(pe, f"xsT{j}")

                def decays(i):
                    g, c = divmod(i, 2)
                    n = f"seg{i}"
                    t = new_tile(pe, n)
                    pe.matmul(t[:, :], C16("ident16"), C16("future").unsqueeze(1).to_broadcast([P, SR, P]), start=True,
                              stop=False, skip_group_check=True)
                    for r in range(SR):
                        h = c * SH + g * SR + r
                        for a in (a_hi, a_lo):
                            m = pe.matmul(t[:, r * P:r * P + P], a[:, h:h + 1].to_broadcast([P, P]), upto[:, :],
                                          start=False, stop=(r == SR - 1 and a is a_lo), skip_group_check=True)
                    is_filled(m, n)
                    n = f"cb{i}"
                    t = new_tile(pe, n)
                    is_filled(pe.matmul(t[:, 0:P], S_BT[:, g, c * P:c * P + P], S_CT[:, g, c * P:c * P + P],
                                        start=True, stop=True), n)

                def mixes(i):
                    g, c = divmod(i, 2)
                    n = f"yd{i}"
                    t = new_tile(pe, n)
                    wait_drained(pe, f"cb{i}")
                    pe.wait_ge(S("xdt_ready"), i + 1)
                    for r in range(SR):
                        m = pe.matmul(t[:, r * SP_:(r + 1) * SP_], S_M[:, i % 2, r * P:r * P + P],
                                      S_xdt[:, i % 2, r * SP_:(r + 1) * SP_], start=True, stop=True)
                    if c == 0:
                        is_filled(m, n)
                        n = f"st{g}"
                        t = new_tile(pe, n)
                        pe.wait_ge(S("xde_ready"), g + 1)
                        m = pe.matmul(t[:, 0:256], S_Bt[:, g, :], S_xde, start=True, stop=True)
                    else:
                        wait_drained(pe, f"st{g}")
                        m = pe.matmul(t[:, 256:512], S_CT[:, g, P:T], S_st[:, g % 2, :], start=True, stop=True)
                    is_filled(m, n)

                for i in range(2 * SG + 1):
                    if i < 2 * SG:
                        decays(i)
                    if i >= 1:
                        mixes(i - 1)
                pe.wait_ge(S("y_norm"), NB)
                for i in range(8):
                    n = f"yT{i}"
                    t = new_tile(pe, n)
                    for k in range(2):
                        for b in range(NB):
                            m = pe.transpose(t[:, k * T + b * P:k * T + b * P + P],
                                             S_xs[:, b, (2 * i + k) * P:(2 * i + k + 1) * P], ident)
                    is_filled(m, n)
                for i in range(8):
                    wait_drained(pe, f"yT{i}")

                out_tiles("so", 16)

            if "M" in stages:
                norm_T("n4", M_xn)
                norm_T_wait("n4")
                token_tiles(["cq0", "cq1"], KT, 2, MQL, 0)
                token_tiles(["ckv0", "ckv1"], KT, 4, MKVL, 0)
                channel_pair("kr")
                for i in range(MH // 2):
                    channel_pair(f"mz{i}")
                pe.wait_ge(S("lat_norm"), 4)
                n = "ckvT0"
                t = new_tile(pe, n)
                for k in range(2):
                    for b in range(NB):
                        m = pe.transpose(t[:, k * T + b * P:k * T + b * P + P], M_ckv[:, b, k * P:k * P + P], ident)
                is_filled(m, n)
                for i, ks in enumerate(((0, 1), (2,))):
                    n = f"cqT{i}"
                    t = new_tile(pe, n)
                    for j, k in enumerate(ks):
                        for b in range(NB):
                            m = pe.transpose(t[:, j * T + b * P:j * T + b * P + P], M_cq[:, b, k * P:k * P + P], ident)
                    is_filled(m, n)
                wait_drained(pe, "ckvT0")
                for i in range(MH // 4):
                    n = next_piece()
                    for q in range(2):
                        nm = f"kn{2 * i + q}"
                        t = new_tile(pe, nm)
                        channels(t, 0, n, 4 * q * P, P, 2, ckv0)
                        is_filled(channels(t, T, n, (4 * q + 2) * P, P, 2, ckv0), nm)
                    piece_used(nm)
                for j in range(4):
                    token_tiles([f"mv{j}_{b}" for b in range(NB)], 2, 2, 512, ckv0)
                wait_drained(pe, "cqT0")
                wait_drained(pe, "cqT1")

                def queries(i):
                    for nm in (f"qn{i}", f"qr{i}"):
                        n = next_piece()
                        t = new_tile(pe, nm)
                        channels(t, 0, n, 0, P, 3, cq0)
                        is_filled(channels(t, T, n, 3 * P, P, 3, cq0), nm)
                        piece_used(nm)

                def m_scores(h):
                    i, lo = h // 2, 64 * (h % 2)
                    if h % 2 == 0:
                        wait_drained(pe, f"qn{i}")
                        pe.wait_ge(S("qrope_ready"), i + 1)
                    n = f"ms{h}"
                    t = new_tile(pe, n)
                    qn, qr = M_qn[:, 2 * (i % 2) + h % 2, :], M_qr[lo:lo + 64, i % 2, :]
                    pe.matmul(t[:, 0:384], C16("ident16"), C16("causal"), start=True, stop=False, skip_group_check=True)
                    pe.matmul(t[:, 0:P], qn[:, 0:P], M_kn[:, h, 0:P], start=False, stop=False, skip_group_check=True)
                    pe.matmul(t[:, P:384], qn[:, P:T], M_kn[:, h, :], start=False, stop=False, skip_group_check=True)
                    pe.matmul(t[:, 0:P], qr[:, 0:P], M_kr[lo:lo + 64, 0:P], start=False, stop=False,
                              skip_group_check=True)
                    is_filled(pe.matmul(t[:, P:384], qr[:, P:T], M_kr[lo:lo + 64, :], start=False, stop=True,
                                        skip_group_check=True), n)

                def m_turn(h):
                    n = f"mpt{h}"
                    t = new_tile(pe, n)
                    pe.wait_ge(S("mp_ready"), 2 * (h + 1))
                    for j in range(3):
                        m = pe.transpose(t[:, j * P:j * P + P], M_p[:, h % 2, j * P:j * P + P], ident)
                    is_filled(m, n)

                def m_values(h):
                    n = f"mo{h}"
                    t = new_tile(pe, n)
                    wait_drained(pe, f"mpt{h}")
                    pT = M_pT[:, h % 2, :]
                    pe.matmul(t[:, 0:T], M_v[:, 0, h * P:h * P + P], pT[:, 0:T], start=True, stop=False,
                              skip_group_check=True)
                    is_filled(pe.matmul(t[:, P:T], M_v[:, 1, h * P:h * P + P], pT[:, T:384], start=False, stop=True,
                                        skip_group_check=True), n)

                for i in range(MH // 2):
                    wait_drained(pe, f"kn{i}")
                for j in range(4):
                    for b in range(NB):
                        wait_drained(pe, f"mv{j}_{b}")
                pe.wait_ge(S("krope_ready"), 1)
                queries(0)
                for h in range(MH + 2):
                    if h % 2 == 0 and h // 2 + 1 < MH // 2:
                        queries(h // 2 + 1)
                    if h < MH:
                        m_scores(h)
                    if 1 <= h <= MH:
                        m_turn(h - 1)
                    if h >= 2:
                        m_values(h - 2)
                pe.wait_ge(S("g_ready"), MH)
                out_tiles("mo_out", 16)

        @block.scalar
        def _(act):
            link = chain(act, "act_own")
            limit = [PIECES_A if "1" in stages else 0]

            def split_high(n):
                raw_wait(act, n)
                if n >= WBUFS:
                    act.wait_ge(*last_use[n - WBUFS])
                at = (n % 2) * PIECE
                nc.scalar.activation(w_hi[:, n % WBUFS, :], ring[:, slot_of(n), at:at + PIECE], ACT.Copy)\
                    .then_inc(split_hi, 1)

            until = splitter(act, limit, split_high)

            def await_tile(name):
                until(piece_at[name] + 2)
                wait_filled(act, name)

            x_count = [0]

            def high(dst, src, **kw):
                nc.scalar.activation(dst, src, ACT.Copy, **kw).then_inc(S("x_high"), 1)
                x_count[0] += 1
                return x_count[0]

            def high_tiles(tag, gain, tiles, n_per, k0):
                for i in range(tiles):
                    n = f"{tag}{i}"
                    await_tile(n)
                    for k in range(n_per if n_per * (i + 1) <= gain.shape[1] else 1):
                        kk = n_per * i + k
                        hi_at[n, k] = high(x_hi[:, k0 + kk, :], tile(n)[:, k * T:(k + 1) * T], scale=gain[:, kk:kk + 1])

            def norm_stats(tag, xn):
                for b in range(NB):
                    m = nc.scalar.activation(xn[:, b, :], res[:, b, :], ACT.Square, accum_out=ss[:, b:b + 1])
                link(m)
                nc.scalar.activation(rt[:, 0:NB], ss[:, 0:NB], ACT.Sqrt, bias=eps, scale=1.0 / D)\
                    .then_inc(S(tag + "_rt"), 1)

            def take(name, dst, src, func=ACT.Copy, **kw):
                await_tile(name)
                is_drained(nc.scalar.activation(dst, src, func, **kw), name)

            act.wait_ge(S("loaded_con"), 16)
            act.wait_ge(S("loaded_par"), 16)
            act.wait_ge(S("loaded_x"), 32)
            if "1" in stages:
                norm_stats("n1", A_xn)
                act.wait_ge(S("lam_dot"), 1)
                nc.scalar.activation(lamv[:, 2:4], lamv[:, 0:2], ACT.Exp).then_inc(S("lam_exp"), 1)
                until(1)
                high_tiles("n1_T", PR("g1"), 4, 2, 0)
                for i in range(4):
                    until(2 * i + 3)
                    for j in (2 * i, 2 * i + 1):
                        wait_drained(act, f"qk{j}")
                    nc.scalar.activation(A_sq[:, 2 * i:2 * i + 2, :], A_qk[:, 2 * i:2 * i + 2, :], ACT.Square)\
                        .then_inc(S("sq_ready"), 1)
                for b in range(NB):
                    take(f"v{b}", A_v[:, b, :], tile(f"v{b}")[:, :])
                act.wait_ge(S("u_zero"), 1)
                for j in range(4):
                    take(f"u{j}", A_u[:, j, UPAD:], tile(f"u{j}")[:, 0:T])
                for i in range(4):
                    n = f"sq{i}"
                    await_tile(n)
                    is_drained(nc.scalar.activation(A_sq[:, 2 * i:2 * i + 2, :], three(tile(n)[:, :], T), ACT.Sqrt,
                                                    bias=eps, scale=1.0 / HD1), n)
                def exps(h):
                    for m_ in range(2):
                        n = f"s{h}_{m_}"
                        await_tile(n)
                        act.wait_ge(S("max_ready"), 2 * h + m_ + 1)
                        if h >= 2:
                            act.wait_ge(S("a_ready"), h - 1)
                        q = 4 * (h % 2) + 2 * m_
                        nc.scalar.activation(A_p[:, 2 * (h % 2) + m_, 0:P], tile(n)[:, 0:P], ACT.Exp,
                                             bias=mx[:, q:q + 1], accum_out=sm[:, q:q + 1])
                        is_drained(nc.scalar.activation(A_p[:, 2 * (h % 2) + m_, P:384], tile(n)[:, P:384], ACT.Exp,
                                                        bias=mx[:, q + 1:q + 2], accum_out=sm[:, q + 1:q + 2]), n)

                for j in range(16):
                    take(f"gate{j}", A_sig[:, j % 8, j // 8, :], tile(f"gate{j}")[:, 0:T], ACT.Sigmoid)
                    if j in ATTEND_AT[:H1]:
                        exps(ATTEND_AT.index(j))
                for g in range(4):
                    n = f"pw{g}"
                    await_tile(n)
                    hi_at[n] = high(x_hi[:, 8 + g, :], tile(n)[:, 0:T], scale=PR("pool_scale")[:, g:g + 1])
                for h in range(H1):
                    for b in range(NB):
                        act.wait_ge(drained[where[f"o{h}"][0]], where[f"o{h}"][1])
                        m = nc.scalar.activation(A_junk[:, 4 * b + h, :], A_o[:, b, h * P:h * P + P], ACT.Square,
                                                 accum_out=ss[:, b * 4 + h:b * 4 + h + 1])
                link(m)
                nc.scalar.activation(rt[:, 0:8], ss[:, 0:8], ACT.Sqrt, bias=eps, scale=1.0 / P)\
                    .then_inc(S("o_rt"), 1)
                for i in range(2):
                    n = f"oT{i}"
                    await_tile(n)
                    hi_at[n] = high(x_hi[:, 12 + 2 * i:14 + 2 * i, :], three(tile(n)[:, :], T), scale=sg08)
                for j in range(KT):
                    until(piece_at[f"up{j}"] + 2)
                    act.wait_ge(S("mix_sum"), j + 1)
                    hi_at["mix", j] = high(x_hi[:, j, :], A_m32[:, j % 4, :])
                until(PIECES_A)
            if "E" in stages:
                if "1" in stages:
                    for c in range(2):
                        for b in range(NB):
                            wait_drained(act, f"wo{c}_{b}")
                norm_stats("n2", E_xn)
                act.wait_ge(S("route_gap"), 1)
                gap = buf(E_t, NB, 5)
                nc.scalar.activation(gap, gap, ACT.Exp).then_inc(S("route_exp"), 1)
                act.wait_ge(pairs_known, 1)
                rounds = act.value_load(more32[0:1, 0:1], min_val=0, max_val=MORE) + ROUNDS
                B, Cb, Dk = bank[5], bank[6], bank[7]
                with act.Fori(0, rounds) as it:
                    for two in range(2):
                        i = it * 2 + two
                        act.wait_ge(units_used, i * PAIR_UNITS + 4)
                        nc.scalar.activation(E_sg, B[:, :], ACT.Silu).then_inc(S("sg_ready"), 1)
                        act.wait_ge(S("hdt_mm"), i + 1)
                        nc.scalar.activation(E_hdT, three(Dk[:, :], P), ACT.Copy).then_inc(S("hdt_out"), 1)
                        act.wait_ge(units_used, i * PAIR_UNITS + 12)
                        nc.scalar.activation(E_y[:, 1, :], Cb[:, :], ACT.Copy).then_inc(S("y1_out"), 1)
                act.wait_ge(S("scattered"), rounds * 2)
                for b in range(NB):
                    nc.scalar.activation(res[:, b, 0:512], bank[2 * b][:, :], ACT.Copy).then_inc(S("moe_taken"), 1)
            if "S" in stages:
                if "E" in stages:
                    act.wait_ge(S("moe_taken"), 4)
                limit[0] = first_b + PIECES_S
                norm_stats("n3", S_xn)
                V = lambda k: S_dt[:, k, :]
                until(first_b + 1)
                high_tiles("n3_T", PR("gs"), 4, 2, 0)
                until(first_b + 2)
                act.wait_ge(S("dt_abs"), 1)
                link(nc.scalar.activation(V(3), V(2), ACT.Exp, scale=-1.0))
                link(nc.scalar.activation(V(11)[:, 0:SH], PR("a_log"), ACT.Exp))
                nc.scalar.activation(V(4), V(3), ACT.Ln, bias=1.0).then_inc(S("dt_ln"), 1)
                act.wait_ge(S("pad_zero"), 1)
                for j in range(32):
                    n = f"xbc{j}"
                    src = tile(n)[:, 0:T]
                    await_tile(n)
                    if j >= 3:
                        act.wait_ge(S("conv_out"), j - 2)
                    ch = (j + 16) % 32
                    nc.scalar.activation(S_raw[:, j % 3, 3:3 + T], src, ACT.Copy)
                    is_drained(nc.scalar.activation(S_cv[:, j % 3, :], src, ACT.Identity,
                                                    scale=PR("conv_w")[:, ch * CONV + 3:ch * CONV + 4],
                                                    bias=PR("conv_b")[:, ch:ch + 1]), n)
                    if j >= 1:
                        conv_silu(j - 1, act)
                conv_silu(31, act)
                for c in range(4):
                    for b in range(NB):
                        n = f"z{c}_{b}"
                        take(n, S_z[:, b, c * 512:(c + 1) * 512], tile(n)[:, :], ACT.Silu)
                until(piece_at["acum"] + 2)
                act.wait_ge(S("acum_out"), 1)
                nc.scalar.activation(V(8), V(5), ACT.Exp).then_inc(S("decay_exp"), 1)
                for i in range(2 * SG):
                    g, c = divmod(i, 2)
                    n = f"seg{i}"
                    await_tile(n)
                    if i >= 2:
                        wait_drained(act, f"cb{i - 2}")
                    for r in range(SR):
                        h = c * SH + g * SR + r
                        m = nc.scalar.activation(S_E[:, i % 2, r * P:r * P + P], tile(n)[:, r * P:r * P + P], ACT.Exp,
                                                 bias=V(7)[:, h:h + 1])
                    is_drained(m, n)
                    if c == 0:
                        wait_filled(act, f"st{g}")
                        is_drained(nc.scalar.activation(S_st[:, g % 2, :], tile(f"st{g}")[:, 0:256], ACT.Copy), f"st{g}")
                for i in range(2 * SG):
                    wait_drained(act, f"yd{i}")
                for i in range(2 * SG):
                    g, c = divmod(i, 2)
                    m = nc.scalar.activation(S_junk[:, i, :], S_xs[:, c, g * 256:(g + 1) * 256], ACT.Square,
                                             accum_out=ss[:, c * SG + g:c * SG + g + 1])
                link(m)
                nc.scalar.activation(rt[:, :], ss[:, :], ACT.Sqrt, bias=eps, scale=1.0 / 256).then_inc(S("y_rt"), 1)
                high_tiles("yT", PR("ssm_g"), 8, 2, 0)
                until(first_b + PIECES_S)
                for c in range(2):
                    for b in range(NB):
                        wait_drained(act, f"so{c}_{b}")
            if "M" in stages:
                limit[0] = first_m + PIECES_M
                norm_stats("n4", M_xn)
                until(first_m + 1)
                high_tiles("n4_T", PR("gm"), 4, 2, 0)
                for b in range(NB):
                    n = f"cq{b}"
                    await_tile(n)
                    nc.scalar.activation(M_cq[:, b, :], tile(n)[:, 0:MQL], ACT.Copy)
                    is_drained(nc.scalar.activation(M_junk[:, b, 0:MQL], tile(n)[:, 0:MQL], ACT.Square,
                                                    accum_out=ss[:, b:b + 1]), n)
                for b in range(NB):
                    n = f"ckv{b}"
                    await_tile(n)
                    nc.scalar.activation(M_ckv[:, b, :], tile(n)[:, 0:MKVL], ACT.Copy)
                    is_drained(nc.scalar.activation(M_junk[:, 2 + b, 0:MKVL], tile(n)[:, 0:MKVL], ACT.Square,
                                                    accum_out=ss[:, 2 + b:3 + b]), n)
                wait_drained(act, "ckv1")
                wait_drained(act, "cq1")
                nc.scalar.activation(rt[:, 0:2], ss[:, 0:2], ACT.Sqrt, bias=eps, scale=1.0 / MQL)
                nc.scalar.activation(rt[:, 2:4], ss[:, 2:4], ACT.Sqrt, bias=eps, scale=1.0 / MKVL)\
                    .then_inc(S("lat_rt"), 1)
                for i in range(MH // 2):
                    take(f"mz{i}", M_z[:, 2 * i:2 * i + 2, :], three(tile(f"mz{i}")[:, :], T), ACT.Silu)
                high_tiles("ckvT", PR("ckv_g"), 1, 2, ckv0)
                high_tiles("cqT", PR("cq_g"), 2, 2, cq0)
                for i in range(MH // 2):
                    take(f"kn{i}", M_kn[:, 2 * i:2 * i + 2, :], three(tile(f"kn{i}")[:, :], T))

                def q_copy(i):
                    take(f"qn{i}", M_qn[:, 2 * (i % 2):2 * (i % 2) + 2, :], three(tile(f"qn{i}")[:, :], T))

                def o_high(h):
                    until(piece_at[f"mo{h}"] + 2)
                    wait_drained(act, f"mo{h}")
                    hi_at["g", h] = high(x_hi[:, h, :], M_z[:, h, :])

                q_copy(0)
                for h in range(MH):
                    if h % 2 == 0 and h // 2 + 1 < MH // 2:
                        if h >= 2:
                            wait_filled(act, f"ms{h - 1}")
                        q_copy(h // 2 + 1)
                    n = f"ms{h}"
                    await_tile(n)
                    act.wait_ge(S("mmax_ready"), h + 1)
                    if h >= 2:
                        wait_filled(act, f"mpt{h - 2}")
                    q = 2 * (h % 2)
                    nc.scalar.activation(M_p[:, h % 2, 0:P], tile(n)[:, 0:P], ACT.Exp, scale=MSCALE,
                                         bias=mx[:, q:q + 1], accum_out=sm[:, q:q + 1])
                    is_drained(nc.scalar.activation(M_p[:, h % 2, P:384], tile(n)[:, P:384], ACT.Exp, scale=MSCALE,
                                                    bias=mx[:, q + 1:q + 2], accum_out=sm[:, q + 1:q + 2]), n)
                    if h >= 3:
                        o_high(h - 3)
                for h in range(MH - 3, MH):
                    o_high(h)
                until(first_m + PIECES_M)
                for c in range(2):
                    for b in range(NB):
                        wait_drained(act, f"mo_out{c}_{b}")
            if stages[-1] == "E":
                act.wait_ge(S("moe_taken"), 4)
            if stages[-1] == "1":
                for c in range(2):
                    for b in range(NB):
                        wait_drained(act, f"wo{c}_{b}")
            norm_stats("n5", F_out)

        @block.vector
        def _(dve):
            v = nc.vector
            link = chain(dve, "dve_own")
            limit = [PIECES_A if "1" in stages else 0]

            def split_low(n):
                dve.wait_ge(split_hi, n + 1)
                at = (n % 2) * PIECE
                v.tensor_tensor(w_lo[:, n % WBUFS, :], ring[:, slot_of(n), at:at + PIECE],
                                w_hi[:, n % WBUFS, :].bitcast(F32), ALU.subtract).then_inc(split_lo, 1)

            until = splitter(dve, limit, split_low)

            def await_tile(name):
                until(piece_at[name] + 2)
                wait_filled(dve, name)

            def low(n, dst, src, gain, hi, count):
                dve.wait_ge(S("x_high"), count)
                return v.scalar_tensor_tensor(out=dst, in0=src, scalar=gain, in1=hi.bitcast(F32), op0=ALU.mult,
                                              op1=ALU.subtract)

            def low_tiles(tag, gain, tiles, n_per, k0):
                for i in range(tiles):
                    n = f"{tag}{i}"
                    await_tile(n)
                    ks = range(n_per if n_per * (i + 1) <= gain.shape[1] else 1)
                    dve.wait_ge(S("x_high"), hi_at[n, ks[-1]])
                    for k in ks:
                        kk = n_per * i + k
                        m = low(n, x_lo[:, k0 + kk, :], tile(n)[:, k * T:(k + 1) * T], gain[:, kk:kk + 1],
                                x_hi[:, k0 + kk, :], hi_at[n, k])
                    is_drained(m, n)

            def norm_apply(tag, xn):
                dve.wait_ge(S(tag + "_rt"), 1)
                link(v.reciprocal(rs[:, 0:NB], rt[:, 0:NB]))
                for b in range(NB):
                    v.tensor_scalar(xn[:, b, :], res[:, b, :], rs[:, b:b + 1], None, ALU.mult)\
                        .then_inc(S(tag + "_xn"), 1)

            def norm_out(tag, dst, gain):
                for i in range(KT // 2):
                    n = f"{tag}_T{i}"
                    wait_filled(dve, n)
                    is_drained(v.tensor_tensor(dst[:, 2 * i:2 * i + 2, :], three(tile(n)[:, :], T),
                                               PR(gain)[:, 2 * i:2 * i + 2].unsqueeze(2).to_broadcast([P, 2, T]),
                                               ALU.mult), n)

            def residual(tag):
                for c in range(2):
                    for b in range(NB):
                        n = f"{tag}{c}_{b}"
                        await_tile(n)
                        dst = res[:, b, c * 512:(c + 1) * 512]
                        is_drained(v.tensor_tensor(dst, tile(n)[:, :], dst, ALU.add), n)
                for c in range(2):
                    for b in range(NB):
                        wait_drained(dve, f"{tag}{c}_{b}")

            dve.wait_ge(S("loaded_con"), 16)
            dve.wait_ge(S("loaded_par"), 16)
            dve.wait_ge(S("loaded_x"), 32)
            if "1" in stages:
                v.memset(A_u[:, :, 0:UPAD], 0.0).then_inc(S("u_zero"), 1)
                norm_apply("n1", A_xn)
                lam = PR("lam")
                for m_ in range(2):
                    m = v.tensor_tensor_reduce(A_lj[:, m_, :], lam[:, 2 * m_ * HD1:(2 * m_ + 1) * HD1],
                                               lam[:, (2 * m_ + 1) * HD1:(2 * m_ + 2) * HD1], 1.0, 0.0, ALU.mult,
                                               ALU.add, lamv[:, m_:m_ + 1])
                m.then_inc(S("lam_dot"), 1)
                v.tensor_scalar(qg8, PR("qg"), HD1 ** -0.5, None, ALU.mult)
                v.tensor_scalar(sg08, PR("subln"), 1.0 - LAMBDA_INIT, None, ALU.mult)
                low_tiles("n1_T", PR("g1"), 4, 2, 0)
                until(1)
                dve.wait_ge(S("lam_exp"), 1)
                link(v.tensor_tensor(neglam, lamv[:, 3:4], lamv[:, 2:3], ALU.subtract))
                link(v.tensor_scalar(neglam, neglam, -LAMBDA_INIT, None, ALU.add))
                for j in range(8):
                    n = f"qk{j}"
                    await_tile(n)
                    is_drained(v.tensor_copy(A_qk[:, j, :], tile(n)[:, 0:T]), n)
                for i in range(4):
                    until(piece_at[f"sq{i}"] + 2)
                    wait_drained(dve, f"sq{i}")
                    sl = slice(2 * i, 2 * i + 2)
                    link(v.reciprocal(A_sq[:, sl, :], A_sq[:, sl, :]))
                    g = qg8 if i < 2 else PR("kg")
                    v.scalar_tensor_tensor(out=A_qk[:, sl, :], in0=A_qk[:, sl, :], scalar=g, in1=A_sq[:, sl, :],
                                           op0=ALU.mult, op1=ALU.mult).then_inc(S("qk_ready"), 1)
                for g, w in enumerate(POOL_WINDOWS):
                    until(piece_at["gate0"] + g // 2)
                    dve.wait_ge(S("pool_part"), (g + 1) * (g + 2) // 2)
                    s = A_pl[:, g % 2, g * (UPAD + T) + UPAD:(g + 1) * (UPAD + T)]
                    u = A_u[:, g, UPAD:]
                    link(v.tensor_tensor(A_dT[:, g, 0:UPAD], s[:, 0:UPAD], C("count")[:, g * UPAD:(g + 1) * UPAD],
                                         ALU.mult))
                    link(v.tensor_tensor(A_dT[:, g, 0:UPAD], A_dT[:, g, 0:UPAD], u[:, 0:UPAD], ALU.subtract))
                    v.scalar_tensor_tensor(out=A_dT[:, g, UPAD:], in0=s[:, UPAD:], scalar=1.0 / w, in1=u[:, UPAD:],
                                           op0=ALU.mult, op1=ALU.subtract).then_inc(S("pool_d"), 1)

                def maxima(h):
                    for m_ in range(2):
                        n = f"s{h}_{m_}"
                        await_tile(n)
                        q = 4 * (h % 2) + 2 * m_
                        v.tensor_reduce(mx[:, q:q + 1], tile(n)[:, 0:P], AX_X, ALU.max)
                        link(v.tensor_reduce(mx[:, q + 1:q + 2], tile(n)[:, P:384], AX_X, ALU.max))
                        v.tensor_scalar(mx[:, q:q + 2], mx[:, q:q + 2], -1.0, None, ALU.mult)\
                            .then_inc(S("max_ready"), 1)

                def combine(h):
                    for m_ in range(2):
                        wait_drained(dve, f"s{h}_{m_}")
                    q = 4 * (h % 2)
                    link(v.reciprocal(sm[:, q:q + 4], sm[:, q:q + 4]))
                    link(v.tensor_scalar(sm[:, q + 2:q + 4], sm[:, q + 2:q + 4], neglam, None, ALU.mult))
                    p0, p1 = A_p[:, 2 * (h % 2), :], A_p[:, 2 * (h % 2) + 1, :]
                    v.tensor_scalar(p0[:, 0:P], p0[:, 0:P], sm[:, q:q + 1], None, ALU.mult)
                    link(v.tensor_scalar(p0[:, P:384], p0[:, P:384], sm[:, q + 1:q + 2], None, ALU.mult))
                    if h >= 2:
                        wait_filled(dve, f"at{h - 2}")
                    v.scalar_tensor_tensor(out=A_a[:, h % 2, 0:P], in0=p1[:, 0:P], scalar=sm[:, q + 2:q + 3],
                                           in1=p0[:, 0:P], op0=ALU.mult, op1=ALU.add)
                    v.scalar_tensor_tensor(out=A_a[:, h % 2, P:384], in0=p1[:, P:384], scalar=sm[:, q + 3:q + 4],
                                           in1=p0[:, P:384], op0=ALU.mult, op1=ALU.add).then_inc(S("a_ready"), 1)

                def probs_out(h):
                    n = f"at{h}"
                    await_tile(n)
                    if h >= 2:
                        wait_filled(dve, f"o{h - 2}")
                    is_drained(v.tensor_copy(A_aT[:, h % 2, :], tile(n)[:, 0:384]), n)

                def o_out(h):
                    n = f"o{h}"
                    await_tile(n)
                    is_drained(v.tensor_copy(A_o[:, :, h * P:h * P + P], three(tile(n)[:, 0:T], P)), n)

                for h in range(H1 + 2):
                    if h < H1:
                        maxima(h)
                    if 1 <= h <= H1:
                        combine(h - 1)
                        probs_out(h - 1)
                    if h >= 2:
                        o_out(h - 2)
                for g in range(4):
                    n = f"pw{g}"
                    await_tile(n)
                    is_drained(low(n, x_lo[:, 8 + g, :], tile(n)[:, 0:T], PR("pool_scale")[:, g:g + 1],
                                   x_hi[:, 8 + g, :], hi_at[n]), n)
                dve.wait_ge(S("o_rt"), 1)
                link(v.reciprocal(rs[:, 0:8], rt[:, 0:8]))
                for b in range(NB):
                    o4 = three(A_o[:, b, :], P)
                    v.tensor_tensor(o4, o4, rs[:, 4 * b:4 * b + 4].unsqueeze(2).to_broadcast([P, 4, P]), ALU.mult)\
                        .then_inc(S("o_norm"), 1)
                for i in range(2):
                    n = f"oT{i}"
                    await_tile(n)
                    sl = slice(12 + 2 * i, 14 + 2 * i)
                    is_drained(low(n, x_lo[:, sl, :], three(tile(n)[:, :], T), sg08, x_hi[:, sl, :], hi_at[n]), n)

                def mix_low(j):
                    dve.wait_ge(S("x_high"), hi_at["mix", j])
                    v.tensor_tensor(x_lo[:, j, :], A_m32[:, j % 4, :], x_hi[:, j, :].bitcast(F32), ALU.subtract)\
                        .then_inc(S("mix_ready"), 1)

                for j in range(KT):
                    n = f"up{j}"
                    await_tile(n)
                    if j >= 2:
                        dve.wait_ge(S("mix_sum"), j - 1)
                    is_drained(v.tensor_tensor(three(A_gt[:, j % 2, :], T), three(tile(n)[:, :], T), A_sig[:, j, :, :],
                                               ALU.mult), n)
                    if j >= 1:
                        mix_low(j - 1)
                mix_low(KT - 1)
                residual("wo")

            if "E" in stages:
                norm_apply("n2", E_xn)
                norm_out("n2", E_hnT, "g2")
                NL = NG + NE
                lg = buf(E_t + 10, NB, NL)
                gap = buf(E_t, NB, 5)
                f1, g1h = buf(E_t + 100, NB, NG), buf(E_t + 120, NB, NG)
                c1, c2, c3, c4 = (buf(E_t + 140 + 2 * k, NB, 1) for k in range(4))
                le, eq = buf(E_t + 200, NB, NE), buf(E_t + 264, NB, NE)
                e1, e2 = buf(E_t + 328, NB, NE), buf(E_t + 392, NB, NE)
                le2, rk = buf(E_t + 456, NB, NE), buf(E_t + 520, NB, NE)
                mem, wt = buf(E_t + 600, NB, NE), buf(E_t + 664, NB, NE)
                n = "route"
                wait_filled(dve, n)
                is_drained(v.tensor_tensor(lg, three(tile(n)[:, 0:NB * NL], NL),
                                           PR("router_b").unsqueeze(1).to_broadcast([P, NB, NL]), ALU.add), n)
                wait_drained(dve, n)

                def first_max(src, k, width, top, hot, tmp):
                    bc = [P, NB, width]
                    rev = C("rev")[:, NE - width:NE].unsqueeze(1).to_broadcast(bc)
                    link(v.tensor_reduce(top, src, AX_X, ALU.max))
                    link(v.tensor_tensor(tmp, src, top.to_broadcast(bc), ALU.is_equal))
                    link(v.tensor_tensor(tmp, tmp, rev, ALU.mult))
                    link(v.tensor_reduce(c4, tmp, AX_X, ALU.max))
                    link(v.tensor_tensor(hot, tmp, c4.to_broadcast(bc), ALU.is_equal))

                first_max(lg[:, :, 0:NG], 0, NG, c1, g1h, f1)
                link(v.tensor_tensor(gap[:, :, 0:NG], lg[:, :, 0:NG], c1.to_broadcast([P, NB, NG]), ALU.subtract))
                link(v.tensor_scalar(g1h, g1h, 1.0, -NEG, ALU.subtract, ALU.mult))
                link(v.tensor_tensor(le.rearrange("p b (g e) -> p b g e", e=EPG),
                                     lg[:, :, NG:NL].rearrange("p b (g e) -> p b g e", e=EPG),
                                     g1h.unsqueeze(3).to_broadcast([P, NB, NG, EPG]), ALU.add))
                first_max(le, 1, NE, c1, e1, eq)
                link(v.scalar_tensor_tensor(out=le2, in0=e1, scalar=-3e38, in1=le, op0=ALU.mult, op1=ALU.add))
                first_max(le2, 2, NE, c2, e2, eq)
                v.tensor_tensor(mem, e1, e2, ALU.add).then_inc(S("member_ready"), 1)
                link(v.tensor_tensor(gap[:, :, NG:5], c2, c1, ALU.subtract))
                v.memset(E_rank, -1.0)
                v.memset(E_w, 0.0).then_inc(S("route_gap"), 1)
                dve.wait_ge(S("route_exp"), 1)
                link(v.tensor_reduce(c1, gap[:, :, 0:NG], AX_X, ALU.add))
                link(v.tensor_scalar(c2, gap[:, :, NG:5], 1.0, None, ALU.add))
                link(v.tensor_tensor(c1, c1, c2, ALU.mult))
                link(v.reciprocal(c3, c1))
                link(v.tensor_tensor(c2, c3, gap[:, :, NG:5], ALU.mult))
                v.tensor_tensor(e1, e1, c3.to_broadcast([P, NB, NE]), ALU.mult)
                link(v.tensor_tensor(e2, e2, c2.to_broadcast([P, NB, NE]), ALU.mult))
                link(v.tensor_tensor(wt, e1, e2, ALU.add))
                n = "rank"
                wait_filled(dve, n)
                cnt = buf(E_t + 740, NE)
                cm, cf = buf(E_t + 780, 1), buf(E_t + 784, 4)
                link(v.tensor_copy(cnt, tile(n)[:, 2 * NE:3 * NE]))
                link(v.tensor_scalar(rk, three(tile(n)[:, 0:2 * NE], NE), 1.0, None, ALU.add))
                link(v.tensor_tensor(rk, rk, mem, ALU.mult))
                is_drained(v.tensor_reduce(cm, cnt, AX_X, ALU.max), n)
                wait_drained(dve, n)
                for p in range(PASSES):
                    v.tensor_scalar(E_rank[:, :, p * NE:(p + 1) * NE], rk, -1.0 - p * SLOTS, None, ALU.add)
                    m = v.tensor_copy(E_w[:, :, p * NE:(p + 1) * NE], wt)
                link(m)
                for k in range(PASSES - 1):
                    m = v.tensor_scalar(cf[:, k:k + 1], cm, float(SLOTS * (k + 1)), float(ROUNDS), ALU.is_gt, ALU.mult)
                link(m)
                link(v.tensor_reduce(cf[:, 3:4], cf[:, 0:3], AX_X, ALU.add))
                v.tensor_copy(more32[:, :], cf[0:1, 3:4]).then_inc(pairs_known, 1)
                dve.wait_ge(pairs_known, 1)
                A, B, Cb, Dk = bank[4], bank[5], bank[6], bank[7]
                g2 = PR("g2")

                def picks(e):
                    bc = [P, NB, 2, SLOTS]
                    v.tensor_tensor(E_S.rearrange("p b (j s) -> p b j s", s=SLOTS),
                                    C("slot").unsqueeze(1).unsqueeze(1).to_broadcast(bc),
                                    E_rank[:, :, e].unsqueeze(3).to_broadcast(bc), ALU.is_equal)\
                        .then_inc(S("pick_ready"), 1)

                def weighted(e):
                    bc = [P, NB, 2, SLOTS]
                    v.tensor_tensor(E_SW.rearrange("p b (j s) -> p b j s", s=SLOTS),
                                    E_S.rearrange("p b (j s) -> p b j s", s=SLOTS),
                                    E_w[:, :, e].unsqueeze(3).to_broadcast(bc), ALU.mult)\
                        .then_inc(S("weight_ready"), 1)

                def tokens_out(half, sem):
                    v.tensor_tensor(E_xe[:, 4 * half:4 * half + 4, :], three(A[:, :], P),
                                    g2[:, 4 * half:4 * half + 4].unsqueeze(2).to_broadcast([P, 4, P]), ALU.mult)\
                        .then_inc(sem, 1)

                picks(slice(0, 2))
                dve.wait_ge(S("pick_ready"), 1)
                weighted(slice(0, 2))
                dve.wait_ge(S("xlo_mm"), 1)
                tokens_out(0, S("xlo_out"))
                dve.wait_ge(S("xhi_mm"), 1)
                tokens_out(1, S("xhi_out"))
                rounds = dve.value_load(more32[0:1, 0:1], min_val=0, max_val=MORE) + ROUNDS
                with dve.Fori(0, rounds) as it:
                    for two in range(2):
                        i = it * 2 + two
                        dve.wait_ge(S("swt_mm"), i + 1)
                        v.tensor_copy(E_SWT, A[:, 0:T]).then_inc(S("swt_out"), 1)
                        dve.wait_ge(S("xhi_mm"), i + 1)
                        picks(bass.ds(i * 2 + 2, 2))
                        dve.wait_ge(S("pick_ready"), i + 2)
                        weighted(bass.ds(i * 2 + 2, 2))
                        dve.wait_ge(units_used, i * PAIR_UNITS + 8)
                        dve.wait_ge(S("sg_ready"), i + 1)
                        v.tensor_tensor(E_hd, Cb[:, :], E_sg, ALU.mult).then_inc(S("hd_ready"), 1)
                        dve.wait_ge(S("xlo_mm"), i + 2)
                        tokens_out(0, S("xlo_out"))
                        dve.wait_ge(S("xhi_mm"), i + 2)
                        tokens_out(1, S("xhi_out"))
                        dve.wait_ge(units_used, i * PAIR_UNITS + 10)
                        v.tensor_copy(E_y[:, 0, :], B[:, :]).then_inc(S("y0_out"), 1)
                dve.wait_ge(S("scattered"), rounds * 2)
                for b in range(NB):
                    v.tensor_copy(res[:, b, 512:D], bank[2 * b + 1][:, :]).then_inc(S("moe_taken"), 1)

            if "S" in stages:
                if "E" in stages:
                    dve.wait_ge(S("moe_taken"), 4)
                limit[0] = first_b + PIECES_S
                norm_apply("n3", S_xn)
                v.tensor_copy(upto[:, :], C("upto")).then_inc(S("upto_ready"), 1)
                low_tiles("n3_T", PR("gs"), 4, 2, 0)
                v.memset(S_raw[:, :, 0:3], 0.0).then_inc(S("pad_zero"), 1)
                V = lambda k: S_dt[:, k, :]
                n = "dt"
                await_tile(n)
                is_drained(v.tensor_tensor(three(V(0), SH), three(tile(n)[:, 0:64], SH),
                                           PR("dt_b").unsqueeze(1).to_broadcast([P, NB, SH]), ALU.add), n)
                wait_drained(dve, n)
                link(v.tensor_scalar(V(2), V(0), -1.0, None, ALU.mult))
                v.tensor_tensor(V(2), V(2), V(0), ALU.max).then_inc(S("dt_abs"), 1)
                dve.wait_ge(S("dt_abs"), 1)
                link(v.tensor_scalar(V(0), V(0), 0.0, None, ALU.max))
                until(piece_at["xbc0"] + 1)
                dve.wait_ge(S("dt_ln"), 1)
                link(v.tensor_scalar(V(5), V(3), 1.0, None, ALU.add))
                link(v.tensor_scalar(V(5), V(5), 1.0, None, ALU.subtract))
                link(v.tensor_scalar(V(6), V(5), 0.0, None, ALU.is_equal))
                link(v.tensor_tensor(V(5), V(5), V(6), ALU.add))
                link(v.reciprocal(V(5), V(5)))
                link(v.tensor_tensor(V(5), V(5), V(4), ALU.mult))
                link(v.tensor_tensor(V(5), V(5), V(6), ALU.add))
                link(v.tensor_tensor(V(5), V(5), V(3), ALU.mult))
                link(v.tensor_tensor(V(0), V(0), V(5), ALU.add))
                v.scalar_tensor_tensor(out=three(V(1), SH), in0=three(V(0), SH), scalar=-1.0,
                                       in1=V(11)[:, 0:SH].unsqueeze(1).to_broadcast([P, NB, SH]),
                                       op0=ALU.mult, op1=ALU.mult).then_inc(S("a_decay"), 1)
                dve.wait_ge(S("a_decay"), 1)
                v.tensor_copy(a_hi[:, :], V(1)).then_inc(S("a_decay"), 1)
                dve.wait_ge(S("a_decay"), 2)
                v.tensor_tensor(a_lo[:, :], V(1), a_hi[:, :].bitcast(F32), ALU.subtract).then_inc(S("a_decay"), 1)
                for j in range(32):
                    ch = (j + 16) % 32
                    until(piece_at[f"xbc{j}"] + 2)
                    wait_drained(dve, f"xbc{j}")
                    for k in range(3):
                        m = v.scalar_tensor_tensor(out=S_cv[:, j % 3, :], in0=S_raw[:, j % 3, k:k + T],
                                                   scalar=PR("conv_w")[:, ch * CONV + k:ch * CONV + k + 1],
                                                   in1=S_cv[:, j % 3, :], op0=ALU.mult, op1=ALU.add)
                        if k < 2:
                            link(m)
                    m.then_inc(S("conv_sum"), 1)
                    if j >= 18:
                        xs_out(j - 18, await_tile)
                xs_out(14, await_tile)
                xs_out(15, await_tile)
                for c in range(4):
                    until(piece_at[f"z{c}_1"])
                n = "acum"
                await_tile(n)
                ac = tile(n)
                v.tensor_copy(V(5)[:, 0:SH], ac[:, SH:2 * SH])
                link(v.tensor_scalar(V(7), ac[:, 0:64], -1.0, None, ALU.mult))
                is_drained(v.tensor_tensor(V(5)[:, SH:64], ac[:, 64:96], V(7)[:, 0:SH], ALU.add), n)
                dve.wait_ge(drained[where[n][0]], where[n][1])
                v.tensor_copy(V(6), V(5)).then_inc(S("acum_out"), 1)
                for i in range(2):
                    n = f"Bt{i}"
                    wait_filled(dve, n)
                    is_drained(v.tensor_copy(S_Bt[:, 4 * i:4 * i + 4, :], three(tile(n)[:, :], P)), n)

                def m_mul(i):
                    n = f"cb{i}"
                    await_tile(n)
                    wait_drained(dve, f"seg{i}")
                    if i >= 2:
                        wait_filled(dve, f"yd{i - 2}")
                    m = v.tensor_tensor(three(S_M[:, i % 2, :], P), three(S_E[:, i % 2, :], P),
                                        tile(n)[:, 0:P].unsqueeze(1).to_broadcast([P, SR, P]), ALU.mult)
                    is_drained(m, n)

                def y_add(i):
                    g, c = divmod(i, 2)
                    n = f"yd{i}"
                    wait_filled(dve, n)
                    dst = S_xs[:, c, g * 256:(g + 1) * 256]
                    dve.wait_ge(S("xd_ready"), i + 1)
                    if c == 1:
                        ea = V(8)[:, g * SR:(g + 1) * SR].unsqueeze(2).to_broadcast([P, SR, SP_])
                        link(v.tensor_tensor(three(S_yo, SP_), three(tile(n)[:, 256:512], SP_), ea, ALU.mult))
                        link(v.tensor_tensor(dst, S_yo, S_xd, ALU.add))
                        link(v.tensor_tensor(dst, tile(n)[:, 0:256], dst, ALU.add))
                    else:
                        link(v.tensor_tensor(dst, tile(n)[:, 0:256], S_xd, ALU.add))
                    is_drained(v.tensor_tensor(dst, dst, S_z[:, c, g * 256:(g + 1) * 256], ALU.mult), n)

                for i in range(2 * SG + 1):
                    if i < 2 * SG:
                        m_mul(i)
                    if i >= 1:
                        y_add(i - 1)
                dve.wait_ge(S("y_rt"), 1)
                link(v.reciprocal(rs[:, :], rt[:, :]))
                for c in range(NB):
                    y8 = three(S_xs[:, c, :], 256)
                    v.tensor_tensor(y8, y8, rs[:, c * SG:(c + 1) * SG].unsqueeze(2).to_broadcast([P, SG, 256]),
                                    ALU.mult).then_inc(S("y_norm"), 1)
                low_tiles("yT", PR("ssm_g"), 8, 2, 0)
                residual("so")

            if "M" in stages:
                limit[0] = first_m + PIECES_M
                norm_apply("n4", M_xn)
                low_tiles("n4_T", PR("gm"), 4, 2, 0)
                rope = three(C("rope"), T)

                def rotate(n, k):
                    await_tile(n)
                    is_drained(v.tensor_tensor(three(M_rt[:, k, :], T), three(tile(n)[:, :], T), rope, ALU.mult), n)

                def rotate_queries(i):
                    if i == 1:
                        dve.wait_ge(S("krope_ready"), 1)
                    if i >= 2:
                        dve.wait_ge(S("qrope_ready"), i - 1)
                    rotate(f"qr{i}", i % 2)

                until(piece_at["cq0"] + 1)
                until(piece_at["ckv0"] + 2)
                dve.wait_ge(S("lat_rt"), 1)
                rotate("kr", 1)
                link(v.reciprocal(rs[:, 0:4], rt[:, 0:4]))
                for b in range(NB):
                    v.tensor_scalar(M_ckv[:, b, :], M_ckv[:, b, :], rs[:, 2 + b:3 + b], None, ALU.mult)\
                        .then_inc(S("lat_norm"), 1)
                    v.tensor_scalar(M_cq[:, b, :], M_cq[:, b, :], rs[:, b:b + 1], None, ALU.mult)\
                        .then_inc(S("lat_norm"), 1)
                for i in range(MH // 2):
                    until(piece_at[f"mz{i}"] + 2)
                low_tiles("ckvT", PR("ckv_g"), 1, 2, ckv0)
                low_tiles("cqT", PR("cq_g"), 2, 2, cq0)
                for j in range(4):
                    for b in range(NB):
                        n = f"mv{j}_{b}"
                        await_tile(n)
                        is_drained(v.tensor_copy(M_v[:, b, j * 512:(j + 1) * 512], tile(n)[:, :]), n)

                def m_max(h):
                    n = f"ms{h}"
                    await_tile(n)
                    q = 2 * (h % 2)
                    v.tensor_reduce(mx[:, q:q + 1], tile(n)[:, 0:P], AX_X, ALU.max)
                    link(v.tensor_reduce(mx[:, q + 1:q + 2], tile(n)[:, P:384], AX_X, ALU.max))
                    v.tensor_scalar(mx[:, q:q + 2], mx[:, q:q + 2], -MSCALE, None, ALU.mult)\
                        .then_inc(S("mmax_ready"), 1)

                def m_probs(h):
                    wait_drained(dve, f"ms{h}")
                    q = 2 * (h % 2)
                    link(v.reciprocal(sm[:, q:q + 2], sm[:, q:q + 2]))
                    p = M_p[:, h % 2, :]
                    v.tensor_scalar(p[:, 0:P], p[:, 0:P], sm[:, q:q + 1], None, ALU.mult).then_inc(S("mp_ready"), 1)
                    v.tensor_scalar(p[:, P:384], p[:, P:384], sm[:, q + 1:q + 2], None, ALU.mult)\
                        .then_inc(S("mp_ready"), 1)

                def m_pT(h):
                    n = f"mpt{h}"
                    await_tile(n)
                    if h >= 2:
                        wait_filled(dve, f"mo{h - 2}")
                    is_drained(v.tensor_copy(M_pT[:, h % 2, :], tile(n)[:, 0:384]), n)

                def m_o(h):
                    n = f"mo{h}"
                    await_tile(n)
                    is_drained(v.tensor_tensor(M_z[:, h, :], tile(n)[:, 0:T], M_z[:, h, :], ALU.mult), n)

                def g_low(h):
                    dve.wait_ge(S("x_high"), hi_at["g", h])
                    v.tensor_tensor(x_lo[:, h, :], M_z[:, h, :], x_hi[:, h, :].bitcast(F32), ALU.subtract)\
                        .then_inc(S("g_ready"), 1)

                for i in range(MH // 2):
                    wait_drained(dve, f"mz{i}")
                rotate_queries(0)
                for h in range(MH + 2):
                    if h % 2 == 0 and h // 2 + 1 < MH // 2:
                        rotate_queries(h // 2 + 1)
                    if h < MH:
                        m_max(h)
                    if 1 <= h <= MH:
                        m_probs(h - 1)
                        m_pT(h - 1)
                    if h >= 2:
                        m_o(h - 2)
                    if h >= 4:
                        g_low(h - 4)
                g_low(MH - 2)
                g_low(MH - 1)
                residual("mo_out")
            dve.wait_ge(S("n5_rt"), 1)
            dve.wait_ge(S("loaded_g"), 16)
            link(v.reciprocal(rs[:, 0:NB], rt[:, 0:NB]))
            for b in range(NB):
                v.scalar_tensor_tensor(out=F_out[:, b, :], in0=res[:, b, :], scalar=rs[:, b:b + 1], in1=F_g,
                                       op0=ALU.mult, op1=ALU.mult).then_inc(S("out_ready"), 1)

        @block.gpsimd
        def _(pool):
            g_ = nc.gpsimd
            if "1" in stages:
                W = UPAD + T
                for g, w in enumerate(POOL_WINDOWS):
                    wait_drained(pool, f"u{g}")
                    src, d = A_u[:, g, :], 1
                    for k in range(g + 1):
                        dst = A_pl[:, k % 2, g * W:(g + 1) * W]
                        if k > 0:
                            pool.wait_ge(S("pool_part"), g * (g + 1) // 2 + k)
                        else:
                            pool.wait_ge(S("u_zero"), 1)
                        lo = 2 * d - 1
                        m = g_.tensor_tensor(dst[:, lo:W], src[:, lo:W], src[:, lo - d:W - d], ALU.add)
                        m.then_inc(S("pool_part"), 1)
                        src, d = dst, 2 * d
                for j in range(KT):
                    wait_drained(pool, f"up{j}")
                    if j >= 4:
                        pool.wait_ge(S("mix_ready"), j - 3)
                    g_.tensor_tensor(A_m32[:, j % 4, :], A_gt[:, j % 2, 0:T], A_gt[:, j % 2, T:2 * T], ALU.add)\
                        .then_inc(S("mix_sum"), 1)
            if "S" in stages:
                pool.wait_ge(S("decay_exp"), 1)
                for j in range(16):
                    wait_drained(pool, f"xsT{j}")
                bc = [P, SR, SP_]
                for i in range(2 * SG):
                    g, c = divmod(i, 2)
                    xs = three(S_xs[:, c, g * 256:(g + 1) * 256], SP_)
                    if i >= 2:
                        wait_filled(pool, f"yd{i - 2}")
                    hs = slice(c * SH + g * SR, c * SH + (g + 1) * SR)
                    g_.tensor_tensor(three(S_xdt[:, i % 2, :], SP_), xs,
                                     S_dt[:, 0, hs].unsqueeze(2).to_broadcast(bc), ALU.mult)\
                        .then_inc(S("xdt_ready"), 1)
                    if c == 0:
                        pool.wait_ge(S("xdt_ready"), i + 1)
                        if g >= 1:
                            wait_filled(pool, f"st{g - 1}")
                        g_.tensor_tensor(three(S_xde, SP_), three(S_xdt[:, i % 2, :], SP_),
                                         S_dt[:, 8, SH + g * SR:SH + (g + 1) * SR].unsqueeze(2).to_broadcast(bc),
                                         ALU.mult).then_inc(S("xde_ready"), 1)
                    if i >= 1:
                        wait_drained(pool, f"yd{i - 1}")
                    g_.tensor_tensor(three(S_xd, SP_), xs,
                                     PR("d_skip")[:, g * SR:(g + 1) * SR].unsqueeze(2).to_broadcast(bc), ALU.mult)\
                        .then_inc(S("xd_ready"), 1)
            if "M" in stages:
                wait_drained(pool, "kr")
                g_.tensor_tensor(M_kr, M_rt[:, 1, 0:T], M_rt[:, 1, T:512], ALU.add).then_inc(S("krope_ready"), 1)
                for i in range(MH // 2):
                    wait_drained(pool, f"qr{i}")
                    if i >= 2:
                        wait_filled(pool, f"ms{2 * i - 3}")
                    g_.tensor_tensor(M_qr[:, i % 2, :], M_rt[:, i % 2, 0:T], M_rt[:, i % 2, T:512], ALU.add)\
                        .then_inc(S("qrope_ready"), 1)

        @block.sync
        def _(sp):
            for b in range(NB):
                sp.dma_start(res[:, b, :], x[b * P:(b + 1) * P, :]).then_inc(S("loaded_x"), 16)
            sp.dma_start(con[:, :], consts).then_inc(S("loaded_con"), 16)
            sp.dma_start(par[:, :], params).then_inc(S("loaded_par"), 16)

            def load(slot, u, sem):
                sp.dma_start(ring[:, slot, :], weights[u, :, :]).then_inc(sem, 16)

            def load_at(slot, u, sem):
                sp.dma_start(ring[:, slot:slot + 1, :], weights[bass.ds(u, 1), :, :].rearrange("u p n -> p u n"))\
                    .then_inc(sem, 16)

            def slot_split(n):
                sp.wait_ge(split_lo, n)

            if "1" in stages:
                for u in range(UNITS_A):
                    if u >= RING:
                        slot_split(2 * (u - RING + 1))
                    load(u % RING, u, raw_a[u % RING])
            R2 = 2 * PAIR_UNITS
            if "E" in stages:
                for k in range(R2):
                    if k < RING and "1" in stages:
                        slot_split(2 * (UNITS_A - RING + k + 1))
                    if k >= RING:
                        sp.wait_ge(units_used, k - RING + 1)
                    load(k % RING, UNITS_A + k, raw_a[k % RING])
                with sp.Fori(1, ROUNDS) as it:
                    for k in range(R2):
                        sp.wait_ge(units_used, it * R2 + (k - RING + 1))
                        load_at(k % RING, it * R2 + (UNITS_A + k), raw_a[k % RING])
                sp.wait_ge(pairs_known, 1)
                rounds = sp.value_load(more32[0:1, 0:1], min_val=0, max_val=MORE) + ROUNDS
                with sp.If(rounds > ROUNDS):
                    with sp.Fori(ROUNDS, rounds, ROUNDS) as first:
                        with sp.Fori(0, ROUNDS) as it:
                            for k in range(R2):
                                sp.wait_ge(units_used, (first + it) * R2 + (k - RING + 1))
                                load_at(k % RING, it * R2 + (UNITS_A + k), raw_a[k % RING])
            pieces_b = (PIECES_S if "S" in stages else 0) + (PIECES_M if "M" in stages else 0)
            off = UNITS_A + UNITS_E
            for u in range((pieces_b + 1) // 2):
                if u < RING and "E" in stages:
                    sp.wait_ge(units_used, rounds * R2 + (u - RING + 1))
                if u >= RING:
                    slot_split(first_b + 2 * (u - RING + 1))
                load(u % RING, off + u, raw_b[u % RING])
            if "M" in stages or "S" in stages:
                wait_filled(sp, "n4_T0" if "M" in stages else "yT0")
            sp.dma_start(F_g, final_g.partition_broadcast(P)).then_inc(S("loaded_g"), 16)
            for b in range(NB):
                sp.wait_ge(S("out_ready"), b + 1)
                sp.dma_start(out[b * P:(b + 1) * P, :], F_out[:, b, :]).then_inc(S("stored"), 16)
            sp.wait_ge(S("stored"), 16 * NB)
    return nc


def pack(inp):
    f = lambda n: np.asarray(inp[n], dtype=np.float32)
    pieces = []

    def rows(w):
        return w.reshape(w.shape[0] // P, P, -1).transpose(1, 0, 2).reshape(P, -1)

    def piece(a):
        if a.shape[1] < PIECE:
            a = np.concatenate([a, np.zeros((P, PIECE - a.shape[1]), np.float32)], axis=1)
        pieces.append(a)

    def channel_pieces(w):
        for j in range(0, w.shape[1], P):
            piece(rows(w[:, j:j + P]))

    def token_pieces(w, kts):
        for k in range(0, w.shape[0], kts * P):
            piece(rows(w[k:k + kts * P]))

    w = f("w_in")[0]
    channel_pieces(w[:, 512:1536])
    token_pieces(w[:, 1536:2048], 2)
    channel_pieces(w[:, 0:512])
    channel_pieces(w[:, 2048:])
    wp, wa = f("w_pool_up")[0], f("w_attn_up")[0]
    for j in range(0, D, P):
        piece(np.concatenate([rows(wp[:, j:j + P]), rows(wa[:, j:j + P])], axis=1))
    for c in range(2):
        token_pieces(f("w_out")[0][:, c * 512:(c + 1) * 512], 2)
    before = np.stack(pieces)
    wg, wu, wd = f("w_expert_gate")[0], f("w_expert_up")[0], f("w_expert_down")[0]
    pair = [w.reshape(PAIRS, 2, D // (2 * P), 2, P, 512) for w in (wg, wu)]
    down = wd.reshape(PAIRS, 2, 2, 2, P, 2, 512)
    units = [w.transpose(0, 2, 4, 1, 3, 5).reshape(PAIRS, 4, P, UNIT) for w in pair]
    units.append(down.transpose(0, 5, 2, 4, 1, 3, 6).reshape(PAIRS, 4, P, UNIT))
    experts = np.concatenate(units, axis=1).reshape(UNITS_E, P, UNIT)

    pieces = []
    w = f("ssm_in_w_2")[0]
    piece(rows(w[:, 6144:6176]))
    channel_pieces(w[:, 4096:6144])
    channel_pieces(w[:, 2048:4096])
    for c in range(4):
        token_pieces(w[:, c * 512:(c + 1) * 512], 2)
    for c in range(2):
        token_pieces(f("ssm_out_w_2")[0][:, c * 512:(c + 1) * 512], 2)
    w = f("mla_in_w_2")[0]
    token_pieces(w[:, 0:MQL], 2)
    o = MQL + MKVL
    token_pieces(w[:, MQL:o], 4)
    kr = w[:, o:o + MR]
    swap = lambda r: np.concatenate([r[:, MR // 2:], r[:, :MR // 2]], axis=1)
    channel_pieces(np.concatenate([kr, kr, swap(kr), swap(kr)], axis=1))
    channel_pieces(w[:, o + MR:])
    w = f("mla_ukv_w_2")[0].reshape(MKVL, MH, 2, P)
    for h in range(0, MH, 4):
        piece(np.concatenate([rows(w[:, h + a, 0]) for a in range(4)], axis=1))
    for h in range(0, MH, 4):
        piece(rows(w[:, h:h + 4, 1].reshape(MKVL, -1)))
    w = f("mla_uq_w_2")[0].reshape(MQL, MH, P + MR)
    for h in range(0, MH, 2):
        r0, r1 = w[:, h, P:], w[:, h + 1, P:]
        piece(np.concatenate([rows(w[:, h, :P]), rows(w[:, h + 1, :P])], axis=1))
        piece(np.concatenate([rows(np.concatenate([r0, r1], axis=1)),
                              rows(np.concatenate([swap(r0), swap(r1)], axis=1))], axis=1))
    for c in range(2):
        token_pieces(f("mla_out_w_2")[0][:, c * 512:(c + 1) * 512], 2)
    if len(pieces) % 2:
        piece(np.zeros((P, PIECE), np.float32))
    after = np.stack(pieces)
    joined = lambda a: a.reshape(-1, 2, P, PIECE).transpose(0, 2, 1, 3).reshape(-1, P, UNIT)
    weights = np.concatenate([joined(before), experts, joined(after)])

    tiles = lambda v: v.reshape(-1, P).T
    wide = lambda v: np.broadcast_to(v.reshape(1, -1), (P, v.size))
    parts = dict(
        g1=tiles(f("norm1_g")[0]), g2=tiles(f("norm2_g")[0]), gs=tiles(f("norm_w_2")[0]), gm=tiles(f("norm_w_2")[1]),
        pool_scale=tiles(f("pool_scale")[0]), qg=np.tile(f("q_norm_g")[0], 2)[:, None],
        kg=np.tile(f("k_norm_g")[0], 2)[:, None], subln=f("subln_g")[0][:, None],
        lam=wide(np.concatenate([f(n)[0] for n in ("lambda_q1", "lambda_k1", "lambda_q2", "lambda_k2")])),
        router_b=wide(np.concatenate([f("b_router_group")[0], f("b_router_expert")[0]])),
        conv_w=f("ssm_conv_w_2")[0].T.reshape(32, P, CONV).transpose(1, 0, 2).reshape(P, -1),
        conv_b=tiles(f("ssm_conv_b_2")[0]), dt_b=wide(f("ssm_dt_bias_2")[0]), a_log=wide(f("ssm_A_log_2")[0]),
        d_skip=wide(f("ssm_D_2")[0]), ssm_g=tiles(f("ssm_norm_w_2")[0]), cq_g=tiles(f("mla_q_norm_w_2")[0]),
        ckv_g=tiles(f("mla_kv_norm_w_2")[0]),
        router_w=rows(np.concatenate([f("w_router_group")[0], f("w_router_expert")[0]], axis=1)),
        pool_w=f("pool_w")[0].transpose(1, 0, 2).reshape(P, -1))
    params = np.concatenate([parts[n].reshape(P, -1) for n in PARAM_WIDTHS], axis=1)
    assert params.shape[1] == NPARAM
    return weights, np.ascontiguousarray(params)


def kernel(**inputs):
    import concourse.bacc as bacc
    from concourse.bass_utils import run_bass_kernel_spmd

    nc = bacc.Bacc("TRN2", target_bir_lowering=False, num_devices=1, dynamic_dma_scratch_size=1024)
    weights, params = pack(inputs)
    cmap, consts = constants()
    arrays = {"weights_dram": weights, "params_dram": params, "consts_dram": consts,
              "x_dram": np.ascontiguousarray(np.asarray(inputs["x"], dtype=np.float32)[0]),
              "final_g_dram": np.asarray(inputs["final_norm_w_2"], dtype=np.float32)}
    aps = [nc.dram_tensor(n, a.shape, F32, kind="ExternalInput").ap() for n, a in arrays.items()]
    out = nc.dram_tensor("out_dram", (T, D), F32, kind="ExternalOutput").ap()
    program(nc, *aps, out, cmap)
    r = run_bass_kernel_spmd(nc, [arrays], core_ids=[0])
    return np.asarray(r.results[0]["out_dram"]).reshape(1, T, D)
```

```python
import math
from contextlib import ExitStack

import numpy as np
import concourse.bass as bass
from concourse import mybir

F32 = mybir.dt.float32
F32R = mybir.dt.float32r
BF16 = mybir.dt.bfloat16
I32 = mybir.dt.int32
ALU = mybir.AluOpType
ACT = mybir.ActivationFunctionType
AX_X = mybir.AxisListType.X

P = 128
T = 256
NB = T // P
D = 1024
KT = D // P
EPS = 1e-6
NEG = -1e30
LAMBDA_INIT = 0.8 - 0.6 * math.exp(-0.3 * 0)

H1, HD1 = 4, 64
POOL_WINDOWS = (2, 4, 8, 16)
UPAD = 16

NE, EPG, NG = 32, 8, 4
SLOTS = 64
PASSES = T // SLOTS
PAIRS = NE // 2
PER_ROUND = 4
ROUNDS = PAIRS // PER_ROUND
MORE = ROUNDS * (PASSES - 1)

SG, SR, SP_, SN = 8, 4, 64, 128
SH = SG * SR
CONV = 4
ATTEND_AT = (4, 6, 8, 10, 12, 13, 14)

MH = 16
MQL, MKVL, MR = 384, 256, 64
MSCALE = (128 + MR) ** -0.5

PIECE = 1024
UNIT = 2 * PIECE
RING = 8
RING_E = 16
WBUFS = 3
PIECES_A = 48
PIECES_S = 65
PIECES_M = 64
UNITS_A = PIECES_A // 2
UNITS_E = NE * 6
PAIR_UNITS = 12


def constants():
    c, at, parts = {}, 0, []

    def put(name, a):
        nonlocal at
        a = np.ascontiguousarray(a, dtype=np.float32).reshape(P, -1)
        c[name] = (at, a.shape[1])
        at += a.shape[1]
        parts.append(a)

    i = np.arange(P)
    def put_bf16(name, a):
        bits = np.ascontiguousarray(a, dtype=np.float32).view(np.uint32) >> 16
        put(name, np.ascontiguousarray(bits[:, 0::2] | (bits[:, 1::2] << 16)).view(np.float32))

    put("ident", np.eye(P))
    put("eps", np.full((P, 1), EPS))
    put("upto", i[:, None] <= i[None, :])
    put("before", i[:, None] < i[None, :])
    put("ones", np.ones((P, P)))
    put("halves", (i[:, None] // HD1) == (i[None, :] // HD1))
    put_bf16("ident16", np.eye(P))
    put_bf16("future", np.where(i[:, None] <= i[None, :], 0.0, NEG))
    dist = np.concatenate([i[:, None] - i[None, :], i[:, None] + P - np.arange(T)[None, :]], axis=1)
    put_bf16("causal", np.where(dist >= 0, 0.0, NEG))
    slopes = [2.0 ** (-8.0 * (h + 1) / H1) for h in range(H1)]
    put_bf16("alibi", np.concatenate([np.where(dist >= 0, -s * dist, NEG) for s in slopes], axis=1))
    half = MR // 2
    inv = (500000.0 ** (-np.arange(half, dtype=np.float32) / np.float32(half))).astype(np.float32)
    ang = inv[:, None] * np.arange(T, dtype=np.float32)[None, :]
    cos, sin = np.cos(ang), np.sin(ang)
    put("rope", np.concatenate([np.tile(cos, (4, 1)), np.tile(np.concatenate([-sin, sin]), (2, 1))], axis=1))
    put("slot", np.tile(np.arange(SLOTS), (P, 1)))
    put("rev", np.tile(np.arange(NE, 0, -1), (P, 1)))
    put("count", np.tile(np.concatenate([1.0 / np.minimum(np.arange(UPAD) + 1, w) for w in POOL_WINDOWS]), (P, 1)))
    return c, np.concatenate(parts, axis=1)


PARAM_WIDTHS = dict(
    g1=KT, g2=KT, gs=KT, gm=KT, pool_scale=4, qg=1, kg=1, subln=1, lam=4 * HD1, router_b=NG + NE,
    conv_w=32 * CONV, conv_b=32, dt_b=SH, a_log=SH, d_skip=SH, ssm_g=16, cq_g=3, ckv_g=2,
    router_w=KT * (NG + NE), pool_w=4 * P)
PARAMS, _at = {}, 0
for _n, _w in PARAM_WIDTHS.items():
    PARAMS[_n] = (_at, _w)
    _at += _w
NPARAM = _at


def program(nc, weights, params, consts, x, final_g, out, cmap, stages="1ESM"):
    NCONST = sum(w for _, w in cmap.values())
    ctx = ExitStack()
    with ctx:
        def sbuf(name, shape, dt=F32):
            return ctx.enter_context(nc.sbuf_tensor(name, shape, dt))

        ring = sbuf("ring", [P, RING, UNIT])
        w_hi, w_lo = sbuf("w_hi", [P, WBUFS, PIECE], F32R), sbuf("w_lo", [P, WBUFS, PIECE], F32R)
        parts = sbuf("parts", [P, 2, 16, T])
        parts_at = nc.sbuf_base - 2 * 16 * T * 4
        x_hi, x_lo = (nc.alloc_sbuf_tensor_at(n, [P, 16, T], F32R, offset=parts_at + i * 16 * T * 4)
                      for i, n in enumerate(("x_hi", "x_lo")))
        a_hi, a_lo = sbuf("a_hi", [P, 2 * SH], F32R), sbuf("a_lo", [P, 2 * SH], F32R)
        neg_hi, neg_lo = sbuf("neg_hi", [P, 2 * SH], F32R), sbuf("neg_lo", [P, 2 * SH], F32R)
        upto, ones = sbuf("upto_r", [P, P], F32R), sbuf("ones_r", [P, P], F32R)
        con = sbuf("con", [P, NCONST])
        par = sbuf("par", [P, NPARAM])
        res = sbuf("res", [P, NB, D])
        work = sbuf("work", [P, 18496])
        small = sbuf("small", [P, 116])
        more32 = sbuf("more32", [1, 1], I32)
        bank = [ctx.enter_context(nc.psum_tensor(f"bank{b}", [P, 512], F32)) for b in range(8)]

        def C(name):
            o, w = cmap[name]
            return con[:, o:o + w]

        def C16(name):
            return C(name).bitcast(BF16)

        def PR(name):
            o, w = PARAMS[name]
            return par[:, o:o + w]

        def view(t, at, *shape):
            n = int(np.prod(shape))
            v = t[:, at:at + n]
            if len(shape) == 2:
                v = v.rearrange("p (a b) -> p a b", b=shape[1])
            if len(shape) == 3:
                v = v.rearrange("p (a b c) -> p a b c", b=shape[1], c=shape[2])
            return v

        def buf(at, *shape):
            return view(work, at, *shape)

        def three(ap, b):
            return ap.rearrange("p (a b) -> p a b", b=b)

        def four(ap, b, c):
            return ap.rearrange("p (a b c) -> p a b c", b=b, c=c)

        sems = {}

        def S(name):
            if name not in sems:
                sems[name] = ctx.enter_context(nc.semaphore(name))
            return sems[name]

        ident = C("ident")
        eps = C("eps")

        filled = [S(f"filled{b}") for b in range(8)]
        drained = [S(f"drained{b}") for b in range(8)]
        where, used, turn = {}, [0] * 8, [0]

        def new_tile(pe, name):
            b = turn[0] % 8
            turn[0] += 1
            used[b] += 1
            where[name] = (b, used[b])
            if used[b] > 1:
                pe.wait_ge(drained[b], used[b] - 1)
            return bank[b]

        def is_filled(ins, name):
            ins.then_inc(filled[where[name][0]], 1)
            piece_at[name] = len(last_use)

        def wait_filled(e, name):
            e.wait_ge(filled[where[name][0]], where[name][1])

        def is_drained(ins, name):
            ins.then_inc(drained[where[name][0]], 1)

        def wait_drained(e, name):
            e.wait_ge(drained[where[name][0]], where[name][1])

        def tile(name):
            return bank[where[name][0]]

        def chain(e, name):
            n = [0]

            def link(ins):
                n[0] += 1
                ins.then_inc(S(name), 1)
                e.wait_ge(S(name), n[0])
            return link

        raw_a = [S(f"raw_a{s}") for s in range(RING)]
        raw_b = [S(f"raw_b{s}") for s in range(RING)]
        raw_e = [S(f"raw_e{s}") for s in range(RING_E)]
        split_hi, split_lo = S("split_hi"), S("split_lo")
        last_use = []
        piece_at, hi_at = {}, {}
        units_used = S("units_used")

        def slot_of(n):
            return (n // 2 if n < first_b else (n - first_b) // 2) % RING

        def slot_e(s):
            if s < RING:
                return ring[:, s, :]
            if s < 12:
                return buf(E_SLOTS + (s - RING) * UNIT, UNIT)
            half = parts[:, (s - 12) // 2, 8 * (s % 2):8 * (s % 2) + 8, :]
            return half.rearrange("p k t -> p (k t)")

        def raw_wait(e, n):
            u = n // 2 if n < first_b else (n - first_b) // 2
            e.wait_ge((raw_a if n < first_b else raw_b)[u % RING], 16 * (u // RING + 1))

        first_b = PIECES_A if "1" in stages else 0
        first_m = first_b + (PIECES_S if "S" in stages else 0)
        pieces_end = first_m + (PIECES_M if "M" in stages else 0)
        pairs_known = S("pairs_known")

        ss, rt, rs = small[:, 0:16], small[:, 16:32], small[:, 32:48]
        lamv, neglam = small[:, 48:52], small[:, 52:53]
        mx, sm = small[:, 56:72], small[:, 72:88]
        half = small[:, 114:116]
        qg8 = small[:, 88:89]
        sg08 = small[:, 89:90]

        A_xn, A_u, A_qk = buf(0, NB, D), buf(2048, 4, UPAD + T), buf(3136, 8, T)
        A_v, A_sig = buf(5184, NB, 512), buf(6208, KT, 2, T)
        A_sq, A_o, A_gt = buf(10304, 8, T), buf(10304, NB, 512), buf(11328, 2, 512)
        A_pl, A_dT = buf(12352, 2, 4 * (UPAD + T)), buf(14528, 4, T)
        A_junk, A_m32 = buf(12352, 8, P), buf(13376, 4, T)
        A_p, A_a, A_aT = buf(15552, 4, 384), buf(0, 2, 384), buf(768, 2, 384)
        A_lj = buf(17100, 2, HD1)

        E_xn, E_hnT, E_xe = buf(0, NB, D), buf(2048, KT, T), buf(4096, KT, P)
        E_S, E_SW, E_SWT = buf(5120, NB, P), buf(5376, NB, P), buf(5632, T)
        E_sg, E_hd, E_hdT = buf(5888, 512), buf(6400, 512), buf(6912, 4, P)
        E_y = buf(7424, 2, 512)
        XW = PASSES * NE + 2
        E_rank, E_w = buf(8448, NB, XW), buf(8448 + 2 * XW, NB, XW)
        E_t = 9000
        E_SLOTS = 18496 - 4 * UNIT

        S_xn = buf(4096, NB, D)
        S_BT, S_CT = buf(0, SG, T), buf(2048, SG, T)
        S_xs, S_z = buf(4096, NB, 2048), buf(8192, NB, 2048)
        S_raw, S_cv, S_xsT = buf(12288, 3, 260), buf(13068, 3, T), buf(13836, 3, T)
        S_E, S_M = buf(12288, 2, 512), buf(13312, 2, 512)
        S_dt, S_dtT = buf(14604, 12, 64), buf(15372, T)[0:SH, :]
        S_tri = [x_[:, 8:12, :].rearrange("p (a b) t -> p a (b t)", a=2) for x_ in (x_hi, x_lo)]
        S_xdt, S_xde = buf(15372, 2, 256), buf(15884, 256)
        S_Bt, S_st, S_yo, S_xd = buf(16140, SG, P), buf(17164, 2, 256), buf(17676, 256), buf(17932, 256)

        M_xn, M_cq, M_ckv = buf(0, NB, D), buf(2048, NB, MQL), buf(2816, NB, MKVL)
        M_kr, M_rt = buf(18240, T), buf(3584, 2, 512)
        M_z, M_kn, M_v = buf(4608, MH, T), buf(8704, MH, T), buf(12800, NB, 2048)
        M_junk = buf(8704, 4, 512)
        M_qn, M_qr = buf(0, 4, T), buf(1024, 2, T)
        M_p, M_pT = buf(1536, 3, 384), buf(2688, 2, 384)
        F_out, F_g = buf(4608, NB, D), buf(17000, D)
        ckv0, cq0 = 8, 13

        def splitter(e, limit, split):
            done = [0]

            def until(n):
                while done[0] <= min(n, limit[0] - 1):
                    split(done[0])
                    done[0] += 1
            return until

        def at_first(i):
            return i // 2

        def conv_silu(j, act):
            act.wait_ge(S("conv_sum"), j + 1)
            if j < 8:
                dst = S_BT[:, j, :]
            elif j < 16:
                dst = S_CT[:, j - 8, :]
            else:
                if j >= 19:
                    wait_filled(act, f"xsT{j - 19}")
                dst = S_xsT[:, (j - 16) % 3, :]
            nc.scalar.activation(dst, S_cv[:, j % 3, :], ACT.Silu).then_inc(S("conv_out"), 1)

        def xs_out(j, await_tile):
            n = f"xsT{j}"
            await_tile(n)
            is_drained(nc.vector.tensor_copy(S_xs[:, :, j * P:j * P + P], three(tile(n)[:, 0:T], P)), n)

        def y_scale(engine, g):
            y = S_xs[:, :, g * 256:(g + 1) * 256]
            k = rs[:, g:2 * SG:SG].unsqueeze(2).to_broadcast([P, NB, 256])
            return engine.tensor_tensor(y, y, k, ALU.mult)

        block = ctx.enter_context(nc.Block())

        @block.tensor
        def _(pe):
            def next_piece():
                n = len(last_use)
                pe.wait_ge(split_lo, n + 1)
                return n

            def piece_used(name=None, sem=None, count=0):
                if name is not None:
                    sem, count = filled[where[name][0]], where[name][1]
                last_use.append((sem, count))

            def products(out, a, b, first, last):
                for i, (p, q) in enumerate(((0, 0), (0, 1), (1, 0))):
                    m = pe.matmul(out, a[p], b[q], start=first and i == 0, stop=last and i == 2)
                return m

            def wpart(n, at, width):
                return [w[:, n % WBUFS, at:at + width] for w in (w_hi, w_lo)]

            def xpart(k, lo=0, hi=T):
                return [x_[:, k, lo:hi] for x_ in (x_hi, x_lo)]

            part_count = [0]
            x_made = []

            def token_piece(names, n, kts, k0, kall, width, x0):
                if k0 == 0:
                    ts = [new_tile(pe, nm) for nm in names]
                    token_piece.ts = ts
                ts = token_piece.ts
                for b in range(NB):
                    for k in range(kts):
                        await_x(x0 + k0 + k)
                        m = products(ts[b][:, 0:width], xpart(x0 + k0 + k, b * P, b * P + P),
                                     wpart(n, k * width, width), k0 + k == 0, k0 + k == kall - 1)
                    if k0 + kts == kall:
                        is_filled(m, names[b])
                if k0 + kts == kall:
                    piece_used(names[1])
                else:
                    part_count[0] += 1
                    m.then_inc(S("part_done"), 1)
                    piece_used(sem=S("part_done"), count=part_count[0])

            def token_tiles(names, kall, kts, width, x0):
                for k0 in range(0, kall, kts):
                    token_piece(names, next_piece(), kts, k0, kall, width, x0)

            def channels(t, c0, n, at, step, kts, x0):
                for k in range(kts):
                    await_x(x0 + k)
                    m = products(t[:, c0:c0 + T], wpart(n, at + k * step, P), xpart(x0 + k), k == 0, k == kts - 1)
                return m

            def channel_tile(name, kts=KT, x0=0):
                n = next_piece()
                t = new_tile(pe, name)
                is_filled(channels(t, 0, n, 0, P, kts, x0), name)
                piece_used(name)

            def channel_pair(name, kts=KT, x0=0):
                t = new_tile(pe, name)
                n = next_piece()
                part_count[0] += 1
                channels(t, 0, n, 0, P, kts, x0).then_inc(S("part_done"), 1)
                piece_used(sem=S("part_done"), count=part_count[0])
                n = next_piece()
                is_filled(channels(t, T, n, 0, P, kts, x0), name)
                piece_used(name)

            def keep_warm(t, n):
                for _ in range(n):
                    pe.matmul(t[:, 0:P], ident, ident, start=True, stop=True)

            def norm_T(tag, xn, warm=0):
                for i in range(KT // 2):
                    t = new_tile(pe, f"{tag}_T{i}")
                    if i == 0:
                        keep_warm(t, warm)
                    pe.wait_ge(S(tag + "_xn"), NB * (1 + i // 2))
                    for k in range(2):
                        for b in range(NB):
                            m = pe.transpose(t[:, k * T + b * P:k * T + b * P + P],
                                             xn[:, b, (2 * i + k) * P:(2 * i + k + 1) * P], ident)
                    is_filled(m, f"{tag}_T{i}")

                for i in range(KT // 2):
                    made_by(2 * i, f"{tag}_T{i}")

            def made_by(k, name=None, sem=None, count=0):
                if name is not None:
                    sem, count = drained[where[name][0]], where[name][1]
                x_made.append((k, sem, count))

            def await_x(k):
                while x_made and x_made[0][0] <= k:
                    pe.wait_ge(*x_made.pop(0)[1:])

            def out_tiles(tag, kall):
                for half in range(2):
                    token_tiles([f"{tag}{half}_{b}" for b in range(NB)], kall, 2, 512, 0)

            pe.wait_ge(S("loaded_first"), 32)
            if "1" not in stages:
                pe.wait_ge(S("loaded_rest"), 32)
            if "1" in stages:
                norm_T("n1", A_xn, 14)
                for j in range(8):
                    channel_tile(f"qk{j}")
                token_tiles(["v0", "v1"], KT, 2, 512, 0)
                def head_squares(i):
                    n = f"sq{i}"
                    t = new_tile(pe, n)
                    pe.wait_ge(S("sq_ready"), i + 1)
                    is_filled(pe.matmul(t[:, :], C("halves"), A_sq[:, 2 * i:2 * i + 2, :], start=True, stop=True), n)

                pe.wait_ge(S("loaded_rest"), 32)
                head_squares(0)
                head_squares(1)
                for j in range(4):
                    channel_tile(f"u{j}")
                    if j < 2:
                        head_squares(2 + j)

                def scores(h):
                    for m_ in range(2):
                        n = f"s{h}_{m_}"
                        t = new_tile(pe, n)
                        lo = 64 * m_
                        pe.matmul(t[:, 0:384], C16("ident16"), C16("alibi")[:, h * 384:(h + 1) * 384], start=True, stop=False,
                                  skip_group_check=True)
                        pe.matmul(t[:, 0:P], A_qk[lo:lo + 64, h, 0:P], A_qk[lo:lo + 64, 4 + h, 0:P],
                                  start=False, stop=False, skip_group_check=True)
                        is_filled(pe.matmul(t[:, P:384], A_qk[lo:lo + 64, h, P:T], A_qk[lo:lo + 64, 4 + h, :],
                                            start=False, stop=True, skip_group_check=True), n)

                def turn_probs(h):
                    n = f"at{h}"
                    t = new_tile(pe, n)
                    pe.wait_ge(S("a_ready"), h + 1)
                    for j in range(3):
                        m = pe.transpose(t[:, j * P:j * P + P], A_a[:, h % 2, j * P:j * P + P], ident)
                    is_filled(m, n)

                def values(h):
                    n = f"o{h}"
                    t = new_tile(pe, n)
                    wait_drained(pe, f"at{h}")
                    if h == 0:
                        wait_drained(pe, "v0")
                        wait_drained(pe, "v1")
                    aT = A_aT[:, h % 2, :]
                    pe.matmul(t[:, 0:P], aT[:, 0:P], A_v[:, 0, h * P:h * P + P], start=True, stop=True)
                    pe.matmul(t[:, P:T], aT[:, P:T], A_v[:, 0, h * P:h * P + P], start=True, stop=False)
                    is_filled(pe.matmul(t[:, P:T], aT[:, T:384], A_v[:, 1, h * P:h * P + P],
                                        start=False, stop=True), n)

                def attend(h):
                    if h < H1:
                        scores(h)
                    if 2 <= h <= H1 + 1:
                        turn_probs(h - 2)
                    if h >= 3:
                        values(h - 3)

                for j in range(16):
                    channel_tile(f"gate{j}")
                    if j == ATTEND_AT[0]:
                        pe.wait_ge(S("qk_ready"), 8)
                    if j in ATTEND_AT:
                        attend(ATTEND_AT.index(j))
                for g in range(4):
                    n = f"pw{g}"
                    t = new_tile(pe, n)
                    pe.wait_ge(S("pool_d"), g + 1)
                    is_filled(pe.matmul(t[:, 0:T], PR("pool_w")[:, g * P:g * P + P], A_dT[:, g, :],
                                        start=True, stop=True), n)
                pe.wait_ge(S("o_norm"), NB)
                for i in range(2):
                    n = f"oT{i}"
                    t = new_tile(pe, n)
                    for k in range(2):
                        for b in range(NB):
                            m = pe.transpose(t[:, k * T + b * P:k * T + b * P + P],
                                             A_o[:, b, (2 * i + k) * P:(2 * i + k + 1) * P], ident)
                    is_filled(m, n)
                for g in range(4):
                    made_by(8 + g, f"pw{g}")
                for i in range(2):
                    made_by(12 + 2 * i, f"oT{i}")
                for j in range(KT):
                    nm = f"up{j}"
                    n = next_piece()
                    t = new_tile(pe, nm)
                    channels(t, 0, n, 0, P, 4, 8)
                    is_filled(channels(t, T, n, 4 * P, P, 4, 12), nm)
                    piece_used(nm)
                for j in range(KT):
                    made_by(j, sem=S("mix_ready"), count=j + 1)
                for c in range(2):
                    token_tiles([f"wo{c}_{b}" for b in range(NB)], KT, 2, 512, 0)

            if "E" in stages:
                def seed(c):
                    for b in range(NB):
                        pe.matmul(bank[2 * b + c][:, :], ident, res[:, b, c * 512:(c + 1) * 512],
                                  start=True, stop=False, skip_group_check=True)

                for b in range(4):
                    if used[b]:
                        pe.wait_ge(drained[b], used[b])
                if "1" not in stages:
                    for b in range(NB):
                        pe.wait_ge(S(f"loaded_x{b}"), 16)
                if "1" in stages:
                    for b in range(NB):
                        wait_drained(pe, f"wo0_{b}")
                seed(0)
                turn[0] = 4
                norm_T("n2", E_xn)
                await_x(KT - 1)
                n = "route"
                turn[0] = 4
                t = new_tile(pe, n)
                NL = NG + NE
                for b in range(NB):
                    for k in range(KT):
                        m = pe.matmul(t[:, b * NL:(b + 1) * NL], E_hnT[:, k, b * P:b * P + P],
                                      PR("router_w")[:, k * NL:(k + 1) * NL], start=(k == 0), stop=(k == KT - 1))
                is_filled(m, n)
                seed(1)
                n = "rank"
                t = new_tile(pe, n)
                keep_warm(t, 16)
                pe.wait_ge(S("member_ready"), 1)
                mem = buf(E_t + 600, NB, NE)
                pe.matmul(t[:, 0:NE], C("before"), mem[:, 0, :], start=True, stop=True)
                pe.matmul(t[:, NE:2 * NE], C("ones"), mem[:, 0, :], start=True, stop=False)
                pe.matmul(t[:, NE:2 * NE], C("before"), mem[:, 1, :], start=False, stop=True)
                pe.matmul(t[:, 2 * NE:3 * NE], C("ones"), mem[:, 0, :], start=True, stop=False)
                is_filled(pe.matmul(t[:, 2 * NE:3 * NE], C("ones"), mem[:, 1, :], start=False, stop=True), n)
                for b in (4, 7):
                    pe.wait_ge(drained[b], used[b])
                A, B, Cb, Dk = bank[4], bank[5], bank[6], bank[7]

                def gather(half, sem, A=A):
                    for k in range(4):
                        for b in range(NB):
                            kk = 4 * half + k
                            m = pe.matmul(A[:, k * P:k * P + P], E_xn[:, b, kk * P:kk * P + P], E_S[:, b, :],
                                          start=(b == 0), stop=(b == NB - 1))
                    m.then_inc(sem, 1)

                pe.wait_ge(S("pick_ready"), 1)
                gather(0, S("xlo_mm"))
                gather(1, S("xhi_mm"), Dk)
                for b in (5, 6):
                    pe.wait_ge(drained[b], used[b])
                pe.wait_ge(pairs_known, 1)
                rounds = pe.value_load(more32[0:1, 0:1], min_val=0, max_val=MORE) + ROUNDS
                with pe.Fori(0, rounds) as it:
                    for two in range(PER_ROUND):
                        i = it * PER_ROUND + two
                        pe.wait_ge(S("weight_ready"), i + 1)
                        pe.wait_ge(S("xhi_out"), i + 1)
                        for b in range(NB):
                            m = pe.transpose(A[:, b * P:b * P + P], E_SW[:, b, :], ident)
                        m.then_inc(S("swt_mm"), 1)

                        def unit(k, t, lhs, first, last):
                            u = PAIR_UNITS * two + k
                            s = u % RING_E
                            pe.wait_ge(raw_e[s], it * (16 * PER_ROUND * PAIR_UNITS // RING_E) + 16 * (1 + u // RING_E))
                            for c in range(2):
                                for j in range(2):
                                    m = pe.matmul(t[64 * j:64 * j + 64, :], lhs(c)[:, 64 * j:64 * j + 64],
                                                  slot_e(s)[:, (2 * j + c) * 512:(2 * j + c + 1) * 512],
                                                  start=first and c == 0, stop=last and c == 1)
                            m.then_inc(units_used, 1)

                        for q, t in enumerate((B, Cb)):
                            for k in range(4):
                                unit(4 * q + k, t, lambda c: E_xe[:, 2 * k + c, :], k == 0, k == 3)
                        pe.wait_ge(S("pick_ready"), i + 2)
                        pe.wait_ge(S("swt_out"), i + 1)
                        gather(0, S("xlo_mm"))
                        pe.wait_ge(S("hd_ready"), i + 1)
                        for k in range(4):
                            m = pe.transpose(Dk[:, k * P:k * P + P], E_hd[:, k * P:k * P + P], ident)
                        m.then_inc(S("hdt_mm"), 1)
                        pe.wait_ge(S("xlo_out"), i + 2)
                        gather(1, S("xhi_mm"))
                        pe.wait_ge(S("hdt_out"), i + 1)
                        for q, t in enumerate((B, Cb)):
                            for k in range(2):
                                unit(8 + 2 * q + k, t, lambda c: E_hdT[:, 2 * k + c, :], k == 0, k == 1)
                        for q, sem in enumerate((S("y0_out"), S("y1_out"))):
                            pe.wait_ge(sem, i + 1)
                            for b in range(NB):
                                m = pe.matmul(bank[2 * b + q][:, :], E_SWT[:, b * P:b * P + P], E_y[:, q, :],
                                              start=False, stop=False, skip_group_check=True)
                        m.then_inc(S("scattered"), 1)
                keep_warm(Dk, 12)
                pe.wait_ge(S("sum_out"), 4)
                pe.wait_ge(S("sum_squared"), 4)

            if "S" in stages:
                norm_T("n3", S_xn, 6)
                nm, n = "dtT", next_piece()
                t = new_tile(pe, nm)
                for k in range(KT):
                    await_x(k)
                    m = products(t[0:SH, 0:T], wpart(n, k * SH, SH), xpart(k), k == 0, k == KT - 1)
                is_filled(m, nm)
                piece_used(nm)

                def turn_xs(j):
                    n = f"xsT{j}"
                    t = new_tile(pe, n)
                    pe.wait_ge(S("conv_out"), 16 + j + 1)
                    for b in range(NB):
                        m = pe.transpose(t[:, b * P:b * P + P], S_xsT[:, j % 3, b * P:b * P + P], ident)
                    is_filled(m, n)

                for j in range(32):
                    channel_tile(f"xbc{j}")
                    if j == 2:
                        n = "dt"
                        t = new_tile(pe, n)
                        wait_drained(pe, "dtT")
                        for b in range(NB):
                            m = pe.transpose(t[:, b * SH:(b + 1) * SH], S_dtT[:, b * P:b * P + P],
                                             ident[0:SH, 0:SH])
                        is_filled(m, n)
                    if j >= 18:
                        turn_xs(j - 18)
                for c in range(4):
                    if c == 3:
                        n = "acum"
                        t = new_tile(pe, n)
                        pe.wait_ge(S("a_decay"), 5)
                        av = S_dt[:, 1, :]
                        pe.matmul(t[:, 0:64], C("upto"), av, start=True, stop=True)
                        is_filled(pe.matmul(t[:, 64:96], C("ones"), av[:, 0:SH], start=True, stop=True), n)
                        for i in range(2):
                            n = f"Bt{i}"
                            t = new_tile(pe, n)
                            for k in range(4):
                                m = pe.transpose(t[:, k * P:k * P + P], S_BT[:, 4 * i + k, 0:P], ident)
                            is_filled(m, n)
                    token_tiles([f"z{c}_{b}" for b in range(NB)], KT, 2, 512, 0)
                    if c == 0:
                        turn_xs(14)
                        turn_xs(15)
                for i in range(2):
                    wait_drained(pe, f"Bt{i}")
                for j in range(16):
                    wait_drained(pe, f"xsT{j}")

                def decays(i):
                    g, c = divmod(i, 2)
                    n = f"seg{i}"
                    t = new_tile(pe, n)
                    pe.matmul(t[:, :], C16("ident16"), C16("future").unsqueeze(1).to_broadcast([P, SR, P]), start=True,
                              stop=False, skip_group_check=True)
                    hs = slice(c * SH + g * SR, c * SH + (g + 1) * SR)
                    for a in (neg_hi, neg_lo):
                        pe.matmul(t[:, :], upto[:, :], a[:, hs].unsqueeze(2).to_broadcast([P, SR, P]),
                                  start=False, stop=False, skip_group_check=True)
                    for k in range(2):
                        pe.wait_ge(S(("tri_hi", "tri_lo")[k]), i + 1)
                        m = pe.matmul(t[:, :], ones[:, :], S_tri[k][:, i % 2, :], start=False, stop=(k == 1),
                                      skip_group_check=True)
                    is_filled(m, n)
                    n = f"cb{i}"
                    t = new_tile(pe, n)
                    is_filled(pe.matmul(t[:, 0:P], S_BT[:, g, c * P:c * P + P], S_CT[:, g, c * P:c * P + P],
                                        start=True, stop=True), n)

                def mixes(i):
                    g, c = divmod(i, 2)
                    n = f"yd{i}"
                    t = new_tile(pe, n)
                    wait_drained(pe, f"cb{i}")
                    pe.wait_ge(S("xdt_ready"), i + 1)
                    for r in range(SR):
                        m = pe.matmul(t[:, r * SP_:(r + 1) * SP_], S_M[:, i % 2, r * P:r * P + P],
                                      S_xdt[:, i % 2, r * SP_:(r + 1) * SP_], start=True, stop=True)
                    if c == 0:
                        is_filled(m, n)
                        n = f"st{g}"
                        t = new_tile(pe, n)
                        pe.wait_ge(S("xde_ready"), g + 1)
                        m = pe.matmul(t[:, 0:256], S_Bt[:, g, :], S_xde, start=True, stop=True)
                    else:
                        wait_drained(pe, f"st{g}")
                        m = pe.matmul(t[:, 256:512], S_CT[:, g, P:T], S_st[:, g % 2, :], start=True, stop=True)
                    is_filled(m, n)

                for i in range(2 * SG + 1):
                    if i < 2 * SG:
                        decays(i)
                    if i >= 1:
                        mixes(i - 1)
                for i in range(8):
                    n = f"yT{i}"
                    t = new_tile(pe, n)
                    pe.wait_ge(S(("y_even", "y_odd")[i % 2]), i // 2 + 1)
                    for k in range(2):
                        for b in range(NB):
                            m = pe.transpose(t[:, k * T + b * P:k * T + b * P + P],
                                             S_xs[:, b, (2 * i + k) * P:(2 * i + k + 1) * P], ident)
                    is_filled(m, n)
                for i in range(8):
                    made_by(2 * i, f"yT{i}")
                out_tiles("so", 16)

            if "M" in stages:
                norm_T("n4", M_xn, 8)
                token_tiles(["cq0", "cq1"], KT, 2, MQL, 0)
                token_tiles(["ckv0", "ckv1"], KT, 4, MKVL, 0)
                channel_pair("kr")
                for i in range(MH // 2 - 1):
                    channel_pair(f"mz{i}")
                pe.wait_ge(S("lat_norm"), 4)
                n = "ckvT0"
                t = new_tile(pe, n)
                for k in range(2):
                    for b in range(NB):
                        m = pe.transpose(t[:, k * T + b * P:k * T + b * P + P], M_ckv[:, b, k * P:k * P + P], ident)
                is_filled(m, n)
                for i, ks in enumerate(((0, 1), (2,))):
                    n = f"cqT{i}"
                    t = new_tile(pe, n)
                    for j, k in enumerate(ks):
                        for b in range(NB):
                            m = pe.transpose(t[:, j * T + b * P:j * T + b * P + P], M_cq[:, b, k * P:k * P + P], ident)
                    is_filled(m, n)
                channel_pair(f"mz{MH // 2 - 1}")
                made_by(ckv0, "ckvT0")
                for i in range(MH // 4):
                    n = next_piece()
                    for q in range(2):
                        nm = f"kn{2 * i + q}"
                        t = new_tile(pe, nm)
                        channels(t, 0, n, 4 * q * P, P, 2, ckv0)
                        is_filled(channels(t, T, n, (4 * q + 2) * P, P, 2, ckv0), nm)
                    piece_used(nm)
                for j in range(4):
                    token_tiles([f"mv{j}_{b}" for b in range(NB)], 2, 2, 512, ckv0)
                made_by(cq0, "cqT0")
                made_by(cq0 + 2, "cqT1")

                def queries(nm):
                    n = next_piece()
                    t = new_tile(pe, nm)
                    channels(t, 0, n, 0, P, 3, cq0)
                    is_filled(channels(t, T, n, 3 * P, P, 3, cq0), nm)
                    piece_used(nm)

                def m_scores(h):
                    i, lo = h // 2, 64 * (h % 2)
                    if h % 2 == 0:
                        wait_drained(pe, f"qn{i}")
                        pe.wait_ge(S("qrope_ready"), i + 1)
                    n = f"ms{h}"
                    t = new_tile(pe, n)
                    qn, qr = M_qn[:, 2 * (i % 2) + h % 2, :], M_qr[lo:lo + 64, i % 2, :]
                    pe.matmul(t[:, 0:384], C16("ident16"), C16("causal"), start=True, stop=False, skip_group_check=True)
                    pe.matmul(t[:, 0:P], qn[:, 0:P], M_kn[:, h, 0:P], start=False, stop=False, skip_group_check=True)
                    pe.matmul(t[:, P:384], qn[:, P:T], M_kn[:, h, :], start=False, stop=False, skip_group_check=True)
                    pe.matmul(t[:, 0:P], qr[:, 0:P], M_kr[lo:lo + 64, 0:P], start=False, stop=False,
                              skip_group_check=True)
                    is_filled(pe.matmul(t[:, P:384], qr[:, P:T], M_kr[lo:lo + 64, :], start=False, stop=True,
                                        skip_group_check=True), n)

                def m_turn(h):
                    n = f"mpt{h}"
                    t = new_tile(pe, n)
                    pe.wait_ge(S("mp_ready"), 2 * (h + 1))
                    for j in range(3):
                        m = pe.transpose(t[:, j * P:j * P + P], M_p[:, h % 3, j * P:j * P + P], ident)
                    is_filled(m, n)

                def m_values(h):
                    n = f"mo{h}"
                    t = new_tile(pe, n)
                    wait_drained(pe, f"mpt{h}")
                    if h % 4 == 0:
                        for b in range(NB):
                            wait_drained(pe, f"mv{h // 4}_{b}")
                    pT = M_pT[:, h % 2, :]
                    pe.matmul(t[:, 0:T], M_v[:, 0, h * P:h * P + P], pT[:, 0:T], start=True, stop=False,
                              skip_group_check=True)
                    is_filled(pe.matmul(t[:, P:T], M_v[:, 1, h * P:h * P + P], pT[:, T:384], start=False, stop=True,
                                        skip_group_check=True), n)

                queries("qn0")
                queries("qr0")
                for i in range(MH // 2):
                    wait_drained(pe, f"kn{i}")
                pe.wait_ge(S("krope_ready"), 1)
                for h in range(MH + 3):
                    if h % 2 == 1 and h < MH - 2:
                        queries(f"qr{h // 2 + 1}")
                    if h < MH:
                        m_scores(h)
                    if h % 2 == 0 and h < MH - 2:
                        queries(f"qn{h // 2 + 1}")
                    if 2 <= h <= MH + 1:
                        m_turn(h - 2)
                    if h >= 3:
                        m_values(h - 3)
                for h in range(MH):
                    made_by(h, sem=S("g_ready"), count=h + 1)
                out_tiles("mo_out", 16)

        @block.scalar
        def _(act):
            link = chain(act, "act_own")
            limit = [PIECES_A if "1" in stages else 0]

            def split_high(n):
                raw_wait(act, n)
                if n >= WBUFS:
                    act.wait_ge(*last_use[n - WBUFS])
                at = (n % 2) * PIECE
                nc.scalar.activation(w_hi[:, n % WBUFS, :], ring[:, slot_of(n), at:at + PIECE], ACT.Copy)\
                    .then_inc(split_hi, 1)

            until = splitter(act, limit, split_high)

            def await_tile(name, ahead=2):
                until(piece_at[name] + ahead)
                wait_filled(act, name)

            x_count = [0]

            def high(dst, src, **kw):
                nc.scalar.activation(dst, src, ACT.Copy, **kw).then_inc(S("x_high"), 1)
                x_count[0] += 1
                return x_count[0]

            def high_tiles(tag, gain, tiles, n_per, k0, ahead=lambda i: 2):
                for i in range(tiles):
                    n = f"{tag}{i}"
                    await_tile(n, ahead(i))
                    for k in range(n_per if n_per * (i + 1) <= gain.shape[1] else 1):
                        kk = n_per * i + k
                        hi_at[n, k] = high(x_hi[:, k0 + kk, :], tile(n)[:, k * T:(k + 1) * T], scale=gain[:, kk:kk + 1])

            def norm_stats(tag, xn, source, order=((0, 0), (0, 1), (1, 0), (1, 1))):
                nc.scalar.activation(small[:, 112:113], eps, ACT.Sqrt)
                for c, b in order:
                    m = nc.scalar.activation(xn[:, b, c * 512:(c + 1) * 512], source(c, b), ACT.Square,
                                             accum_out=ss[:, 2 * c + b:2 * c + b + 1])
                    if source is summed:
                        m.then_inc(S("sum_squared"), 1)
                    if (c, b) == (0, 1):
                        if source is summed:
                            act.wait_ge(S("sum_squared"), 2)
                        else:
                            link(m)
                        link(nc.scalar.activation(half, ss[:, 0:2], ACT.Identity, scale=1.0 / D, bias=eps))
                if source is summed:
                    act.wait_ge(S("sum_squared"), 4)
                else:
                    link(m)
                for b in range(NB):
                    nc.scalar.activation(rt[:, b:b + 1], ss[:, 2 + b:3 + b], ACT.Sqrt, bias=half[:, b:b + 1],
                                         scale=1.0 / D).then_inc(S(tag + "_rt"), 1)

            def take(name, dst, src, func=ACT.Copy, **kw):
                await_tile(name)
                is_drained(nc.scalar.activation(dst, src, func, **kw), name)

            def half_of(c, b):
                return res[:, b, c * 512:(c + 1) * 512]

            def loaded(c, b):
                act.wait_ge(S(f"loaded_x{b}"), 16)
                return half_of(c, b)

            def added(tag):
                def source(c, b):
                    wait_drained(act, f"{tag}{c}_{b}")
                    return half_of(c, b)
                return source

            def summed(c, b):
                if c == 1:
                    act.wait_ge(S("sum_out"), b + 1)
                return bank[2 * b + c][:, :]

            act.wait_ge(S("loaded_first"), 32)
            if "1" not in stages:
                act.wait_ge(S("loaded_rest"), 32)
            if "1" in stages:
                norm_stats("n1", A_xn, loaded, ((0, 0), (1, 0), (0, 1), (1, 1)))
                high_tiles("n1_T", PR("g1"), 4, 2, 0, at_first)
                for i in range(4):
                    until(2 * i + 3)
                    for j in (2 * i, 2 * i + 1):
                        wait_drained(act, f"qk{j}")
                    nc.scalar.activation(A_sq[:, 2 * i:2 * i + 2, :], A_qk[:, 2 * i:2 * i + 2, :], ACT.Square)\
                        .then_inc(S("sq_ready"), 1)
                for b in range(NB):
                    take(f"v{b}", A_v[:, b, :], tile(f"v{b}")[:, :])
                until(piece_at["v1"] + 2)
                act.wait_ge(S("loaded_rest"), 32)
                act.wait_ge(S("lam_dot"), 1)
                nc.scalar.activation(lamv[:, 2:4], lamv[:, 0:2], ACT.Exp).then_inc(S("lam_exp"), 1)
                act.wait_ge(S("u_zero"), 1)

                def roots(i):
                    n = f"sq{i}"
                    await_tile(n)
                    is_drained(nc.scalar.activation(A_sq[:, 2 * i:2 * i + 2, :], three(tile(n)[:, :], T), ACT.Sqrt,
                                                    bias=eps, scale=1.0 / HD1), n)

                roots(0)
                roots(1)
                for j in range(4):
                    take(f"u{j}", A_u[:, j, UPAD:], tile(f"u{j}")[:, 0:T])
                    if j < 2:
                        roots(2 + j)

                def o_squares(h):
                    until(piece_at[f"o{h}"] + 2)
                    wait_drained(act, f"o{h}")
                    for b in range(NB):
                        m = nc.scalar.activation(A_junk[:, 4 * b + h, :], A_o[:, b, h * P:h * P + P], ACT.Square,
                                                 accum_out=ss[:, b * 4 + h:b * 4 + h + 1])
                    return m

                def exps(h):
                    for m_ in range(2):
                        n = f"s{h}_{m_}"
                        await_tile(n)
                        act.wait_ge(S("max_ready"), 2 * h + m_ + 1)
                        if h >= 2:
                            act.wait_ge(S("a_ready"), h - 1)
                        q = 4 * (h % 2) + 2 * m_
                        nc.scalar.activation(A_p[:, 2 * (h % 2) + m_, 0:P], tile(n)[:, 0:P], ACT.Exp,
                                             bias=mx[:, q:q + 1], accum_out=sm[:, q:q + 1])
                        is_drained(nc.scalar.activation(A_p[:, 2 * (h % 2) + m_, P:384], tile(n)[:, P:384], ACT.Exp,
                                                        bias=mx[:, q + 1:q + 2], accum_out=sm[:, q + 1:q + 2]), n)

                for j in range(16):
                    bare = ATTEND_AT[0] < j <= ATTEND_AT[H1 - 1]
                    take(f"gate{j}", A_sig[:, j % 8, j // 8, :], tile(f"gate{j}")[:, 0:T],
                         ACT.Copy if bare else ACT.Sigmoid)
                    late = j - ATTEND_AT[H1 - 1] - 2
                    if late in (0, 1):
                        first, end = ((ATTEND_AT[0] + 1, KT), (0, ATTEND_AT[H1 - 1] + 1 - KT))[late]
                        if late == 0:
                            for k in range(ATTEND_AT[0] + 1, ATTEND_AT[H1 - 1] + 1):
                                wait_drained(act, f"gate{k}")
                        nc.scalar.activation(A_sig[:, first:end, late, :], A_sig[:, first:end, late, :], ACT.Sigmoid)\
                            .then_inc(S("gates_late"), 1)
                    if j in ATTEND_AT[:H1]:
                        exps(ATTEND_AT.index(j))
                    if j - 1 in ATTEND_AT[3:]:
                        m = o_squares(ATTEND_AT.index(j - 1) - 3)
                link(m)
                nc.scalar.activation(rt[:, 0:8], ss[:, 0:8], ACT.Sqrt, bias=eps, scale=1.0 / P)\
                    .then_inc(S("o_rt"), 1)
                for g in range(4):
                    n = f"pw{g}"
                    await_tile(n)
                    hi_at[n] = high(x_hi[:, 8 + g, :], tile(n)[:, 0:T], scale=PR("pool_scale")[:, g:g + 1])
                for i in range(2):
                    n = f"oT{i}"
                    await_tile(n)
                    hi_at[n] = high(x_hi[:, 12 + 2 * i:14 + 2 * i, :], three(tile(n)[:, :], T), scale=sg08)
                for j in range(KT):
                    await_tile(f"up{j}")
                    until(piece_at[f"up{j}"] + 3)
                    act.wait_ge(S("mix_sum"), j + 1)
                    hi_at["mix", j] = high(x_hi[:, j, :], A_m32[:, j % 4, :])
                until(PIECES_A)
            if "E" in stages:
                norm_stats("n2", E_xn, added("wo") if "1" in stages else loaded)
                act.wait_ge(S("route_gap"), 1)
                gap = buf(E_t, NB, 5)
                nc.scalar.activation(gap, gap, ACT.Exp).then_inc(S("route_exp"), 1)
                act.wait_ge(pairs_known, 1)
                rounds = act.value_load(more32[0:1, 0:1], min_val=0, max_val=MORE) + ROUNDS
                B, Cb, Dk = bank[5], bank[6], bank[7]
                with act.Fori(0, rounds) as it:
                    for two in range(PER_ROUND):
                        i = it * PER_ROUND + two
                        act.wait_ge(units_used, i * PAIR_UNITS + 4)
                        nc.scalar.activation(E_sg, B[:, :], ACT.Silu).then_inc(S("sg_ready"), 1)
                        act.wait_ge(S("hdt_mm"), i + 1)
                        nc.scalar.activation(E_hdT, three(Dk[:, :], P), ACT.Copy).then_inc(S("hdt_out"), 1)
                        act.wait_ge(units_used, i * PAIR_UNITS + 12)
                        nc.scalar.activation(E_y[:, 1, :], Cb[:, :], ACT.Copy).then_inc(S("y1_out"), 1)
                limit[0] = pieces_end
                until(first_b + 1)
                act.wait_ge(S("scattered"), rounds * PER_ROUND)
            if "S" in stages:
                limit[0] = pieces_end
                norm_stats("n3", S_xn, summed if "E" in stages else loaded)
                V = lambda k: S_dt[:, k, :]
                high_tiles("n3_T", PR("gs"), 4, 2, 0, at_first)
                act.wait_ge(S("pad_zero"), 1)
                for j in range(32):
                    n = f"xbc{j}"
                    src = tile(n)[:, 0:T]
                    await_tile(n)
                    if j >= 3:
                        act.wait_ge(S("conv_out"), j - 2)
                    ch = (j + 16) % 32
                    nc.scalar.activation(S_raw[:, j % 3, 3:3 + T], src, ACT.Copy)
                    is_drained(nc.scalar.activation(S_cv[:, j % 3, :], src, ACT.Identity,
                                                    scale=PR("conv_w")[:, ch * CONV + 3:ch * CONV + 4],
                                                    bias=PR("conv_b")[:, ch:ch + 1]), n)
                    if j >= 1:
                        conv_silu(j - 1, act)
                conv_silu(31, act)
                def tri_low(i):
                    g, c = divmod(i, 2)
                    if i >= 2:
                        wait_filled(act, f"seg{i - 2}")
                    for r in range(SR):
                        h = c * SH + g * SR + r
                        m = nc.scalar.activation(S_tri[1][:, i % 2, r * P:r * P + P], C("upto"), ACT.Copy,
                                                 scale=a_lo[:, h:h + 1].bitcast(F32))
                    m.then_inc(S("tri_lo"), 1)

                for c in range(4):
                    for b in range(NB):
                        n = f"z{c}_{b}"
                        take(n, S_z[:, b, c * 512:(c + 1) * 512], tile(n)[:, :], ACT.Silu)
                    if c == 2:
                        act.wait_ge(S("a_decay"), 5)
                        tri_low(0)
                        tri_low(1)
                    if c == 0:
                        until(piece_at["xsT15"] + 2)
                    if c == 1:
                        act.wait_ge(S("dt_abs"), 1)
                        link(nc.scalar.activation(V(3), V(2), ACT.Exp, scale=-1.0))
                        link(nc.scalar.activation(V(11)[:, 0:SH], PR("a_log"), ACT.Exp))
                        nc.scalar.activation(V(4), V(3), ACT.Ln, bias=1.0).then_inc(S("dt_ln"), 1)
                def y_roots(g0, g1):
                    sl = slice(g0, g1)
                    nc.scalar.activation(three(rt, SG)[:, :, sl], three(ss, SG)[:, :, sl], ACT.Sqrt, bias=eps,
                                         scale=1.0 / 256).then_inc(S("y_rt"), 1)

                def square(i):
                    g, c = divmod(i, 2)
                    wait_drained(act, f"yd{i}")
                    junk = (x_hi, x_lo)[i // 8][:, i % 8, :]
                    return nc.scalar.activation(junk, S_xs[:, c, g * 256:(g + 1) * 256], ACT.Square,
                                                accum_out=ss[:, c * SG + g:c * SG + g + 1])

                act.wait_ge(S("acum_out"), 1)
                nc.scalar.activation(V(8), V(5), ACT.Exp).then_inc(S("decay_exp"), 1)
                for i in range(2 * SG):
                    g, c = divmod(i, 2)
                    n = f"seg{i}"
                    await_tile(n, 2 if i > 2 else -1)
                    if i >= 2:
                        wait_drained(act, f"cb{i - 2}")
                    is_drained(nc.scalar.activation(S_E[:, i % 2, :], tile(n)[:, :], ACT.Exp), n)
                    if c == 1:
                        wait_filled(act, f"st{g}")
                        is_drained(nc.scalar.activation(S_st[:, g % 2, :], tile(f"st{g}")[:, 0:256], ACT.Copy), f"st{g}")
                    if i + 2 < 2 * SG:
                        tri_low(i + 2)
                    if i >= 2:
                        m = square(i - 2)
                    if i == 2 * SG - 1:
                        nc.scalar.activation(small[:, 112:113], eps, ACT.Sqrt)
                        link(m)
                        y_roots(0, SG - 1)
                square(2 * SG - 2)
                link(square(2 * SG - 1))
                y_roots(SG - 1, SG)
                high_tiles("yT", PR("ssm_g"), 8, 2, 0)
                until(first_b + PIECES_S + 1)
            if "M" in stages:
                limit[0] = pieces_end
                norm_stats("n4", M_xn, added("so") if "S" in stages else loaded)
                high_tiles("n4_T", PR("gm"), 4, 2, 0, at_first)
                for b in range(NB):
                    n = f"cq{b}"
                    await_tile(n)
                    nc.scalar.activation(M_cq[:, b, :], tile(n)[:, 0:MQL], ACT.Copy)
                    is_drained(nc.scalar.activation(M_junk[:, b, 0:MQL], tile(n)[:, 0:MQL], ACT.Square,
                                                    accum_out=ss[:, b:b + 1]), n)
                for b in range(NB):
                    n = f"ckv{b}"
                    await_tile(n)
                    nc.scalar.activation(M_ckv[:, b, :], tile(n)[:, 0:MKVL], ACT.Copy)
                    is_drained(nc.scalar.activation(M_junk[:, 2 + b, 0:MKVL], tile(n)[:, 0:MKVL], ACT.Square,
                                                    accum_out=ss[:, 2 + b:3 + b]), n)
                wait_drained(act, "ckv1")
                wait_drained(act, "cq1")
                nc.scalar.activation(rt[:, 0:2], ss[:, 0:2], ACT.Sqrt, bias=eps, scale=1.0 / MQL)
                nc.scalar.activation(rt[:, 2:4], ss[:, 2:4], ACT.Sqrt, bias=eps, scale=1.0 / MKVL)\
                    .then_inc(S("lat_rt"), 1)
                for i in range(MH // 2):
                    if i == MH // 2 - 1:
                        high_tiles("ckvT", PR("ckv_g"), 1, 2, ckv0)
                        high_tiles("cqT", PR("cq_g"), 2, 2, cq0)
                    take(f"mz{i}", M_z[:, 2 * i:2 * i + 2, :], three(tile(f"mz{i}")[:, :], T), ACT.Silu)
                for i in range(MH // 2):
                    take(f"kn{i}", M_kn[:, 2 * i:2 * i + 2, :], three(tile(f"kn{i}")[:, :], T))

                def q_copy(i):
                    take(f"qn{i}", M_qn[:, 2 * (i % 2):2 * (i % 2) + 2, :], three(tile(f"qn{i}")[:, :], T))

                def o_high(h):
                    until(piece_at[f"mo{h}"] + 2)
                    wait_drained(act, f"mo{h}")
                    hi_at["g", h] = high(x_hi[:, h, :], M_z[:, h, :])

                def probs_out(h):
                    n = f"mpt{h}"
                    await_tile(n)
                    if h >= 2:
                        wait_filled(act, f"mo{h - 2}")
                    is_drained(nc.scalar.activation(M_pT[:, h % 2, :], tile(n)[:, 0:384], ACT.Copy), n)

                q_copy(0)
                for h in range(MH):
                    n = f"ms{h}"
                    await_tile(n)
                    act.wait_ge(S("mmax_ready"), h + 1)
                    if h >= 3:
                        wait_filled(act, f"mpt{h - 3}")
                    q = 2 * (h % 3)
                    nc.scalar.activation(M_p[:, h % 3, 0:P], tile(n)[:, 0:P], ACT.Exp, scale=MSCALE,
                                         bias=mx[:, q:q + 1], accum_out=sm[:, q:q + 1])
                    is_drained(nc.scalar.activation(M_p[:, h % 3, P:384], tile(n)[:, P:384], ACT.Exp, scale=MSCALE,
                                                    bias=mx[:, q + 1:q + 2], accum_out=sm[:, q + 1:q + 2]), n)
                    if h % 2 == 0 and h // 2 + 1 < MH // 2:
                        if h >= 2:
                            wait_filled(act, f"ms{h - 1}")
                        q_copy(h // 2 + 1)
                    if h >= 2:
                        probs_out(h - 2)
                    if h >= 4:
                        o_high(h - 4)
                for h in range(MH - 4, MH):
                    if h >= MH - 2:
                        probs_out(h)
                    o_high(h)
                until(pieces_end)
            norm_stats("n5", F_out, summed if stages[-1] == "E" else
                       added({"1": "wo", "S": "so", "M": "mo_out"}[stages[-1]]))

        @block.vector
        def _(dve):
            v = nc.vector
            link = chain(dve, "dve_own")
            limit = [PIECES_A if "1" in stages else 0]

            def split_low(n):
                dve.wait_ge(split_hi, n + 1)
                at = (n % 2) * PIECE
                v.tensor_tensor(w_lo[:, n % WBUFS, :], ring[:, slot_of(n), at:at + PIECE],
                                w_hi[:, n % WBUFS, :].bitcast(F32), ALU.subtract).then_inc(split_lo, 1)

            until = splitter(dve, limit, split_low)

            def await_tile(name, ahead=2):
                until(piece_at[name] + ahead)
                wait_filled(dve, name)

            def low(n, dst, src, gain, hi, count):
                dve.wait_ge(S("x_high"), count)
                return v.scalar_tensor_tensor(out=dst, in0=src, scalar=gain, in1=hi.bitcast(F32), op0=ALU.mult,
                                              op1=ALU.subtract)

            def low_tiles(tag, gain, tiles, n_per, k0, ahead=lambda i: 2):
                for i in range(tiles):
                    n = f"{tag}{i}"
                    await_tile(n, ahead(i))
                    ks = range(n_per if n_per * (i + 1) <= gain.shape[1] else 1)
                    dve.wait_ge(S("x_high"), hi_at[n, ks[-1]])
                    for k in ks:
                        kk = n_per * i + k
                        m = low(n, x_lo[:, k0 + kk, :], tile(n)[:, k * T:(k + 1) * T], gain[:, kk:kk + 1],
                                x_hi[:, k0 + kk, :], hi_at[n, k])
                    is_drained(m, n)

            def norm_apply(tag, xn):
                dve.wait_ge(S(tag + "_rt"), NB)
                link(v.reciprocal(rs[:, 0:NB], rt[:, 0:NB]))
                for c in range(2):
                    for b in range(NB):
                        sl = slice(c * 512, (c + 1) * 512)
                        v.tensor_scalar(xn[:, b, sl], res[:, b, sl], rs[:, b:b + 1], None, ALU.mult)\
                            .then_inc(S(tag + "_xn"), 1)

            def norm_out(tag, dst, gain):
                for i in range(KT // 2):
                    n = f"{tag}_T{i}"
                    wait_filled(dve, n)
                    is_drained(v.tensor_tensor(dst[:, 2 * i:2 * i + 2, :], three(tile(n)[:, :], T),
                                               PR(gain)[:, 2 * i:2 * i + 2].unsqueeze(2).to_broadcast([P, 2, T]),
                                               ALU.mult), n)

            def residual(tag):
                for c in range(2):
                    for b in range(NB):
                        n = f"{tag}{c}_{b}"
                        await_tile(n)
                        dst = res[:, b, c * 512:(c + 1) * 512]
                        is_drained(v.tensor_tensor(dst, tile(n)[:, :], dst, ALU.add), n)
                for c in range(2):
                    for b in range(NB):
                        wait_drained(dve, f"{tag}{c}_{b}")

            for b in range(NB):
                dve.wait_ge(S(f"loaded_x{b}"), 16)
            dve.wait_ge(S("loaded_first"), 32)
            if "1" not in stages:
                dve.wait_ge(S("loaded_rest"), 32)
            if "1" in stages:
                v.memset(A_u[:, :, 0:UPAD], 0.0).then_inc(S("u_zero"), 1)
                norm_apply("n1", A_xn)
                low_tiles("n1_T", PR("g1"), 4, 2, 0, at_first)
                until(1)
                for j in range(8):
                    n = f"qk{j}"
                    await_tile(n)
                    is_drained(v.tensor_copy(A_qk[:, j, :], tile(n)[:, 0:T]), n)
                dve.wait_ge(S("loaded_rest"), 32)
                lam = PR("lam")
                for m_ in range(2):
                    m = v.tensor_tensor_reduce(A_lj[:, m_, :], lam[:, 2 * m_ * HD1:(2 * m_ + 1) * HD1],
                                               lam[:, (2 * m_ + 1) * HD1:(2 * m_ + 2) * HD1], 1.0, 0.0, ALU.mult,
                                               ALU.add, lamv[:, m_:m_ + 1])
                m.then_inc(S("lam_dot"), 1)
                link(v.tensor_scalar(qg8, PR("qg"), HD1 ** -0.5, None, ALU.mult))
                v.tensor_scalar(sg08, PR("subln"), 1.0 - LAMBDA_INIT, None, ALU.mult)
                dve.wait_ge(S("sq_ready"), 4)
                for i in range(8):
                    v.tensor_scalar(A_qk[:, i, :], A_qk[:, i, :], qg8 if i < 4 else PR("kg"), None, ALU.mult)\
                        .then_inc(S("qk_gain"), 1)
                until(piece_at["v1"] + 2)
                dve.wait_ge(S("lam_exp"), 1)
                link(v.tensor_tensor(neglam, lamv[:, 3:4], lamv[:, 2:3], ALU.subtract))
                link(v.tensor_scalar(neglam, neglam, -LAMBDA_INIT, None, ALU.add))
                for i in range(8):
                    until(piece_at["v1"] + 2 + i)
                    wait_drained(dve, f"sq{i // 2}")
                    v.reciprocal(A_sq[:, i, :], A_sq[:, i, :]).then_inc(S("qk_recip"), 1)

                def pool_means(g):
                    dve.wait_ge(S("pool_part"), (g + 1) * (g + 2) // 2)
                    s = A_pl[:, g % 2, g * (UPAD + T) + UPAD:(g + 1) * (UPAD + T)]
                    u = A_u[:, g, UPAD:]
                    link(v.tensor_tensor(A_dT[:, g, 0:UPAD], s[:, 0:UPAD], C("count")[:, g * UPAD:(g + 1) * UPAD],
                                         ALU.mult))
                    link(v.tensor_tensor(A_dT[:, g, 0:UPAD], A_dT[:, g, 0:UPAD], u[:, 0:UPAD], ALU.subtract))
                    v.scalar_tensor_tensor(out=A_dT[:, g, UPAD:], in0=s[:, UPAD:], scalar=1.0 / POOL_WINDOWS[g],
                                           in1=u[:, UPAD:], op0=ALU.mult, op1=ALU.subtract).then_inc(S("pool_d"), 1)

                def maxima(h):
                    for m_ in range(2):
                        n = f"s{h}_{m_}"
                        await_tile(n)
                        q = 4 * (h % 2) + 2 * m_
                        v.tensor_reduce(mx[:, q:q + 1], tile(n)[:, 0:P], AX_X, ALU.max)
                        link(v.tensor_reduce(mx[:, q + 1:q + 2], tile(n)[:, P:384], AX_X, ALU.max))
                        v.tensor_scalar(mx[:, q:q + 2], mx[:, q:q + 2], -1.0, None, ALU.mult)\
                            .then_inc(S("max_ready"), 1)

                def combine(h):
                    for m_ in range(2):
                        wait_drained(dve, f"s{h}_{m_}")
                    q = 4 * (h % 2)
                    link(v.reciprocal(sm[:, q:q + 4], sm[:, q:q + 4]))
                    link(v.tensor_scalar(sm[:, q + 2:q + 4], sm[:, q + 2:q + 4], neglam, None, ALU.mult))
                    p0, p1 = A_p[:, 2 * (h % 2), :], A_p[:, 2 * (h % 2) + 1, :]
                    v.tensor_scalar(p0[:, 0:P], p0[:, 0:P], sm[:, q:q + 1], None, ALU.mult)
                    link(v.tensor_scalar(p0[:, P:384], p0[:, P:384], sm[:, q + 1:q + 2], None, ALU.mult))
                    if h >= 2:
                        wait_filled(dve, f"at{h - 2}")
                    v.scalar_tensor_tensor(out=A_a[:, h % 2, 0:P], in0=p1[:, 0:P], scalar=sm[:, q + 2:q + 3],
                                           in1=p0[:, 0:P], op0=ALU.mult, op1=ALU.add)
                    v.scalar_tensor_tensor(out=A_a[:, h % 2, P:384], in0=p1[:, P:384], scalar=sm[:, q + 3:q + 4],
                                           in1=p0[:, P:384], op0=ALU.mult, op1=ALU.add).then_inc(S("a_ready"), 1)

                def probs_out(h):
                    n = f"at{h}"
                    await_tile(n)
                    if h >= 2:
                        wait_filled(dve, f"o{h - 2}")
                    is_drained(v.tensor_copy(A_aT[:, h % 2, :], tile(n)[:, 0:384]), n)

                def o_out(h):
                    n = f"o{h}"
                    await_tile(n)
                    is_drained(v.tensor_copy(A_o[:, :, h * P:h * P + P], three(tile(n)[:, 0:T], P)), n)

                for h in range(H1 + 3):
                    if h < H1:
                        maxima(h)
                        pool_means(h)
                    if 1 <= h <= H1:
                        combine(h - 1)
                    if 2 <= h <= H1 + 1:
                        probs_out(h - 2)
                    if h >= 3:
                        o_out(h - 3)
                until(piece_at["oT0"] + 1)
                dve.wait_ge(S("o_rt"), 1)
                link(v.reciprocal(rs[:, 0:8], rt[:, 0:8]))
                for b in range(NB):
                    o4 = three(A_o[:, b, :], P)
                    v.tensor_tensor(o4, o4, rs[:, 4 * b:4 * b + 4].unsqueeze(2).to_broadcast([P, 4, P]), ALU.mult)\
                        .then_inc(S("o_norm"), 1)
                for g in range(4):
                    n = f"pw{g}"
                    await_tile(n)
                    is_drained(low(n, x_lo[:, 8 + g, :], tile(n)[:, 0:T], PR("pool_scale")[:, g:g + 1],
                                   x_hi[:, 8 + g, :], hi_at[n]), n)
                for i in range(2):
                    n = f"oT{i}"
                    await_tile(n)
                    sl = slice(12 + 2 * i, 14 + 2 * i)
                    is_drained(low(n, x_lo[:, sl, :], three(tile(n)[:, :], T), sg08, x_hi[:, sl, :], hi_at[n]), n)

                def mix_low(j):
                    dve.wait_ge(S("x_high"), hi_at["mix", j])
                    v.tensor_tensor(x_lo[:, j, :], A_m32[:, j % 4, :], x_hi[:, j, :].bitcast(F32), ALU.subtract)\
                        .then_inc(S("mix_ready"), 1)

                dve.wait_ge(S("gates_late"), 2)
                for j in range(KT):
                    n = f"up{j}"
                    await_tile(n)
                    if j >= 2:
                        dve.wait_ge(S("mix_sum"), j - 1)
                    is_drained(v.tensor_tensor(three(A_gt[:, j % 2, :], T), three(tile(n)[:, :], T), A_sig[:, j, :, :],
                                               ALU.mult), n)
                    if j >= 2:
                        mix_low(j - 2)
                mix_low(KT - 2)
                mix_low(KT - 1)
                residual("wo")

            if "E" in stages:
                norm_apply("n2", E_xn)
                norm_out("n2", E_hnT, "g2")
                NL = NG + NE
                lg = buf(E_t + 10, NB, NL)
                gap = buf(E_t, NB, 5)
                f1, g1h = buf(E_t + 100, NB, NG), buf(E_t + 120, NB, NG)
                c1, c2, c3, c4 = (buf(E_t + 140 + 2 * k, NB, 1) for k in range(4))
                le, eq = buf(E_t + 200, NB, NE), buf(E_t + 264, NB, NE)
                e1, e2 = buf(E_t + 328, NB, NE), buf(E_t + 392, NB, NE)
                le2, rk = buf(E_t + 456, NB, NE), buf(E_t + 520, NB, NE)
                mem, wt = buf(E_t + 600, NB, NE), buf(E_t + 664, NB, NE)
                v.memset(E_rank, -1.0)
                v.memset(E_w, 0.0)
                n = "route"
                wait_filled(dve, n)
                is_drained(v.tensor_tensor(lg, three(tile(n)[:, 0:NB * NL], NL),
                                           PR("router_b").unsqueeze(1).to_broadcast([P, NB, NL]), ALU.add), n)
                wait_drained(dve, n)

                def first_max(src, k, width, top, hot, tmp):
                    bc = [P, NB, width]
                    rev = C("rev")[:, NE - width:NE].unsqueeze(1).to_broadcast(bc)
                    link(v.tensor_reduce(top, src, AX_X, ALU.max))
                    link(v.tensor_tensor(tmp, src, top.to_broadcast(bc), ALU.is_equal))
                    link(v.tensor_tensor(tmp, tmp, rev, ALU.mult))
                    link(v.tensor_reduce(c4, tmp, AX_X, ALU.max))
                    link(v.tensor_tensor(hot, tmp, c4.to_broadcast(bc), ALU.is_equal))

                first_max(lg[:, :, 0:NG], 0, NG, c1, g1h, f1)
                link(v.tensor_tensor(gap[:, :, 0:NG], lg[:, :, 0:NG], c1.to_broadcast([P, NB, NG]), ALU.subtract))
                link(v.tensor_scalar(g1h, g1h, 1.0, -NEG, ALU.subtract, ALU.mult))
                link(v.tensor_tensor(le.rearrange("p b (g e) -> p b g e", e=EPG),
                                     lg[:, :, NG:NL].rearrange("p b (g e) -> p b g e", e=EPG),
                                     g1h.unsqueeze(3).to_broadcast([P, NB, NG, EPG]), ALU.add))
                first_max(le, 1, NE, c1, e1, eq)
                link(v.scalar_tensor_tensor(out=le2, in0=e1, scalar=-3e38, in1=le, op0=ALU.mult, op1=ALU.add))
                first_max(le2, 2, NE, c2, e2, eq)
                v.tensor_tensor(mem, e1, e2, ALU.add).then_inc(S("member_ready"), 1)
                v.tensor_tensor(gap[:, :, NG:5], c2, c1, ALU.subtract).then_inc(S("route_gap"), 1)
                n = "rank"
                wait_filled(dve, n)
                link(v.tensor_scalar(rk, three(tile(n)[:, 0:2 * NE], NE), 1.0, None, ALU.add))
                link(v.tensor_tensor(rk, rk, mem, ALU.mult))

                def rank_of_pass(p):
                    return v.tensor_scalar(E_rank[:, :, p * NE:(p + 1) * NE], rk, -1.0 - p * SLOTS, None, ALU.add)

                link(rank_of_pass(0))
                A, B, Cb, Dk = bank[4], bank[5], bank[6], bank[7]
                g2 = PR("g2")

                def picks(e):
                    bc = [P, NB, 2, SLOTS]
                    v.tensor_tensor(E_S.rearrange("p b (j s) -> p b j s", s=SLOTS),
                                    C("slot").unsqueeze(1).unsqueeze(1).to_broadcast(bc),
                                    E_rank[:, :, e].unsqueeze(3).to_broadcast(bc), ALU.is_equal)\
                        .then_inc(S("pick_ready"), 1)

                def weighted(e):
                    bc = [P, NB, 2, SLOTS]
                    v.tensor_tensor(E_SW.rearrange("p b (j s) -> p b j s", s=SLOTS),
                                    E_S.rearrange("p b (j s) -> p b j s", s=SLOTS),
                                    E_w[:, :, e].unsqueeze(3).to_broadcast(bc), ALU.mult)\
                        .then_inc(S("weight_ready"), 1)

                def tokens_out(half, sem, A=A):
                    v.tensor_tensor(E_xe[:, 4 * half:4 * half + 4, :], three(A[:, :], P),
                                    g2[:, 4 * half:4 * half + 4].unsqueeze(2).to_broadcast([P, 4, P]), ALU.mult)\
                        .then_inc(sem, 1)

                picks(slice(0, 2))
                dve.wait_ge(S("route_exp"), 1)
                link(v.tensor_reduce(c1, gap[:, :, 0:NG], AX_X, ALU.add))
                link(v.tensor_scalar(c2, gap[:, :, NG:5], 1.0, None, ALU.add))
                link(v.tensor_tensor(c1, c1, c2, ALU.mult))
                link(v.reciprocal(c3, c1))
                link(v.tensor_tensor(c2, c3, gap[:, :, NG:5], ALU.mult))
                v.tensor_tensor(e1, e1, c3.to_broadcast([P, NB, NE]), ALU.mult)
                link(v.tensor_tensor(e2, e2, c2.to_broadcast([P, NB, NE]), ALU.mult))
                link(v.tensor_tensor(wt, e1, e2, ALU.add))
                for p in range(PASSES):
                    if p > 0:
                        rank_of_pass(p)
                    m = v.tensor_copy(E_w[:, :, p * NE:(p + 1) * NE], wt)
                link(m)
                weighted(slice(0, 2))
                cnt = buf(E_t + 740, NE)
                cm, cf = buf(E_t + 780, 1), buf(E_t + 784, 4)
                link(v.tensor_copy(cnt, tile(n)[:, 2 * NE:3 * NE]))
                is_drained(v.tensor_reduce(cm, cnt, AX_X, ALU.max), n)
                wait_drained(dve, n)
                for k in range(PASSES - 1):
                    m = v.tensor_scalar(cf[:, k:k + 1], cm, float(SLOTS * (k + 1)), float(ROUNDS), ALU.is_gt, ALU.mult)
                link(m)
                link(v.tensor_reduce(cf[:, 3:4], cf[:, 0:3], AX_X, ALU.add))
                v.tensor_copy(more32[:, :], cf[0:1, 3:4]).then_inc(pairs_known, 1)
                dve.wait_ge(pairs_known, 1)
                dve.wait_ge(S("xlo_mm"), 1)
                tokens_out(0, S("xlo_out"))
                dve.wait_ge(S("xhi_mm"), 1)
                tokens_out(1, S("xhi_out"), Dk)
                rounds = dve.value_load(more32[0:1, 0:1], min_val=0, max_val=MORE) + ROUNDS
                with dve.Fori(0, rounds) as it:
                    for two in range(PER_ROUND):
                        i = it * PER_ROUND + two
                        dve.wait_ge(S("swt_mm"), i + 1)
                        v.tensor_copy(E_SWT, A[:, 0:T]).then_inc(S("swt_out"), 1)
                        dve.wait_ge(S("xhi_mm"), i + 1)
                        picks(bass.ds(i * 2 + 2, 2))
                        dve.wait_ge(S("pick_ready"), i + 2)
                        weighted(bass.ds(i * 2 + 2, 2))
                        dve.wait_ge(units_used, i * PAIR_UNITS + 8)
                        dve.wait_ge(S("sg_ready"), i + 1)
                        v.tensor_tensor(E_hd, Cb[:, :], E_sg, ALU.mult).then_inc(S("hd_ready"), 1)
                        dve.wait_ge(S("xlo_mm"), i + 2)
                        tokens_out(0, S("xlo_out"))
                        dve.wait_ge(S("xhi_mm"), i + 2)
                        tokens_out(1, S("xhi_out"))
                        dve.wait_ge(units_used, i * PAIR_UNITS + 10)
                        v.tensor_copy(E_y[:, 0, :], B[:, :]).then_inc(S("y0_out"), 1)
                limit[0] = pieces_end
                until(first_b + 1)
                dve.wait_ge(S("scattered"), rounds * PER_ROUND)
                for c in (1, 0):
                    for b in range(NB):
                        if c == 0:
                            dve.wait_ge(S("sum_squared"), b + 1)
                        v.tensor_copy(res[:, b, c * 512:(c + 1) * 512], bank[2 * b + c][:, :])\
                            .then_inc(S("sum_out"), 1)
                dve.wait_ge(S("sum_out"), 4)

            if "S" in stages:
                limit[0] = pieces_end
                norm_apply("n3", S_xn)
                v.memset(S_raw[:, :, 0:3], 0.0).then_inc(S("pad_zero"), 1)
                v.tensor_copy(upto[:, :], C("upto"))
                v.tensor_copy(ones[:, :], C("ones"))
                low_tiles("n3_T", PR("gs"), 4, 2, 0, at_first)
                V = lambda k: S_dt[:, k, :]
                for j in range(32):
                    ch = (j + 16) % 32
                    until(piece_at[f"xbc{j}"] + 2)
                    wait_drained(dve, f"xbc{j}")
                    for k in range(3):
                        m = v.scalar_tensor_tensor(out=S_cv[:, j % 3, :], in0=S_raw[:, j % 3, k:k + T],
                                                   scalar=PR("conv_w")[:, ch * CONV + k:ch * CONV + k + 1],
                                                   in1=S_cv[:, j % 3, :], op0=ALU.mult, op1=ALU.add)
                        if k < 2:
                            link(m)
                    m.then_inc(S("conv_sum"), 1)
                    if j == 1:
                        n = "dtT"
                        await_tile(n)
                        is_drained(v.tensor_copy(S_dtT, tile(n)[0:SH, 0:T]), n)
                    if j == 3:
                        n = "dt"
                        await_tile(n)
                        is_drained(v.tensor_tensor(three(V(0), SH), three(tile(n)[:, 0:64], SH),
                                                   PR("dt_b").unsqueeze(1).to_broadcast([P, NB, SH]), ALU.add), n)
                    if j >= 18:
                        xs_out(j - 18, await_tile)
                xs_out(14, await_tile)
                xs_out(15, await_tile)
                wait_drained(dve, "dt")
                link(v.tensor_scalar(V(2), V(0), -1.0, None, ALU.mult))
                v.tensor_tensor(V(2), V(2), V(0), ALU.max).then_inc(S("dt_abs"), 1)
                dve.wait_ge(S("dt_abs"), 1)
                link(v.tensor_scalar(V(0), V(0), 0.0, None, ALU.max))
                until(piece_at["z1_1"] + 2)
                dve.wait_ge(S("dt_ln"), 1)
                link(v.tensor_scalar(V(5), V(3), 1.0, None, ALU.add))
                link(v.tensor_scalar(V(5), V(5), 1.0, None, ALU.subtract))
                link(v.tensor_scalar(V(6), V(5), 0.0, None, ALU.is_equal))
                link(v.tensor_tensor(V(5), V(5), V(6), ALU.add))
                link(v.reciprocal(V(5), V(5)))
                until(piece_at["z1_1"] + 3)
                link(v.tensor_tensor(V(5), V(5), V(4), ALU.mult))
                link(v.tensor_tensor(V(5), V(5), V(6), ALU.add))
                link(v.tensor_tensor(V(5), V(5), V(3), ALU.mult))
                link(v.tensor_tensor(V(0), V(0), V(5), ALU.add))
                v.scalar_tensor_tensor(out=three(V(1), SH), in0=three(V(0), SH), scalar=-1.0,
                                       in1=V(11)[:, 0:SH].unsqueeze(1).to_broadcast([P, NB, SH]),
                                       op0=ALU.mult, op1=ALU.mult).then_inc(S("a_decay"), 1)
                dve.wait_ge(S("a_decay"), 1)
                v.tensor_copy(a_hi[:, :], V(1)).then_inc(S("a_decay"), 1)
                dve.wait_ge(S("a_decay"), 2)
                v.tensor_tensor(a_lo[:, :], V(1), a_hi[:, :].bitcast(F32), ALU.subtract).then_inc(S("a_decay"), 1)
                dve.wait_ge(S("a_decay"), 3)
                for a, neg in ((a_hi, neg_hi), (a_lo, neg_lo)):
                    v.tensor_scalar(neg[:, :], a[:, :].bitcast(F32), -1.0, None, ALU.mult).then_inc(S("a_decay"), 1)
                until(piece_at["z2_1"])
                n = "acum"
                await_tile(n)
                ac = tile(n)
                v.tensor_copy(V(5)[:, 0:SH], ac[:, SH:2 * SH])
                link(v.tensor_scalar(V(7), ac[:, 0:64], -1.0, None, ALU.mult))
                is_drained(v.tensor_tensor(V(5)[:, SH:64], ac[:, 64:96], V(7)[:, 0:SH], ALU.add), n)
                dve.wait_ge(drained[where[n][0]], where[n][1])
                v.tensor_copy(V(6), V(5)).then_inc(S("acum_out"), 1)
                for i in range(2):
                    n = f"Bt{i}"
                    wait_filled(dve, n)
                    is_drained(v.tensor_copy(S_Bt[:, 4 * i:4 * i + 4, :], three(tile(n)[:, :], P)), n)

                def m_mul(i):
                    n = f"cb{i}"
                    await_tile(n, 2 if i > 2 else -1)
                    wait_drained(dve, f"seg{i}")
                    if i >= 2:
                        wait_filled(dve, f"yd{i - 2}")
                    m = v.tensor_tensor(three(S_M[:, i % 2, :], P), three(S_E[:, i % 2, :], P),
                                        tile(n)[:, 0:P].unsqueeze(1).to_broadcast([P, SR, P]), ALU.mult)
                    is_drained(m, n)

                def y_add(i):
                    g, c = divmod(i, 2)
                    n = f"yd{i}"
                    wait_filled(dve, n)
                    dst = S_xs[:, c, g * 256:(g + 1) * 256]
                    dve.wait_ge(S("xd_ready"), i + 1)
                    if c == 1:
                        ea = V(8)[:, g * SR:(g + 1) * SR].unsqueeze(2).to_broadcast([P, SR, SP_])
                        link(v.tensor_tensor(three(S_yo, SP_), three(tile(n)[:, 256:512], SP_), ea, ALU.mult))
                        link(v.tensor_tensor(dst, S_yo, S_xd, ALU.add))
                        link(v.tensor_tensor(dst, tile(n)[:, 0:256], dst, ALU.add))
                    else:
                        link(v.tensor_tensor(dst, tile(n)[:, 0:256], S_xd, ALU.add))
                    is_drained(v.tensor_tensor(dst, dst, S_z[:, c, g * 256:(g + 1) * 256], ALU.mult), n)

                def y_inverse(g0, g1, n):
                    dve.wait_ge(S("y_rt"), n)
                    v.reciprocal(three(rs, SG)[:, :, g0:g1], three(rt, SG)[:, :, g0:g1]).then_inc(S("y_rs"), 1)
                    dve.wait_ge(S("y_rs"), n)

                for i in range(2 * SG + 1):
                    if i < 2 * SG:
                        m_mul(i)
                    if i == 2 * SG:
                        y_inverse(0, SG - 1, 1)
                        y_scale(v, 0).then_inc(S("y_even"), 1)
                    if i >= 1:
                        y_add(i - 1)
                for g in range(2, SG, 2):
                    y_scale(v, g).then_inc(S("y_even"), 1)
                y_inverse(SG - 1, SG, 2)
                low_tiles("yT", PR("ssm_g"), 8, 2, 0)
                residual("so")

            if "M" in stages:
                limit[0] = pieces_end
                norm_apply("n4", M_xn)
                low_tiles("n4_T", PR("gm"), 4, 2, 0, at_first)
                rope = three(C("rope"), T)

                def rotate(n, k):
                    await_tile(n)
                    is_drained(v.tensor_tensor(three(M_rt[:, k, :], T), three(tile(n)[:, :], T), rope, ALU.mult), n)

                def rotate_queries(i):
                    if i == 1:
                        dve.wait_ge(S("krope_ready"), 1)
                    if i >= 2:
                        dve.wait_ge(S("qrope_ready"), i - 1)
                    rotate(f"qr{i}", i % 2)

                until(piece_at["cq0"] + 1)
                until(piece_at["ckv0"] + 2)
                dve.wait_ge(S("lat_rt"), 1)
                rotate("kr", 1)
                link(v.reciprocal(rs[:, 0:4], rt[:, 0:4]))
                for b in range(NB):
                    v.tensor_scalar(M_ckv[:, b, :], M_ckv[:, b, :], rs[:, 2 + b:3 + b], None, ALU.mult)\
                        .then_inc(S("lat_norm"), 1)
                    v.tensor_scalar(M_cq[:, b, :], M_cq[:, b, :], rs[:, b:b + 1], None, ALU.mult)\
                        .then_inc(S("lat_norm"), 1)
                for i in range(MH // 2 - 1):
                    until(piece_at[f"mz{i}"] + 2)
                low_tiles("ckvT", PR("ckv_g"), 1, 2, ckv0)
                low_tiles("cqT", PR("cq_g"), 2, 2, cq0)
                for j in range(4):
                    for b in range(NB):
                        n = f"mv{j}_{b}"
                        await_tile(n)
                        is_drained(v.tensor_copy(M_v[:, b, j * 512:(j + 1) * 512], tile(n)[:, :]), n)

                def m_max(h):
                    n = f"ms{h}"
                    await_tile(n)
                    q = 2 * (h % 3)
                    v.tensor_reduce(mx[:, q:q + 1], tile(n)[:, 0:P], AX_X, ALU.max)
                    link(v.tensor_reduce(mx[:, q + 1:q + 2], tile(n)[:, P:384], AX_X, ALU.max))
                    v.tensor_scalar(mx[:, q:q + 2], mx[:, q:q + 2], -MSCALE, None, ALU.mult)\
                        .then_inc(S("mmax_ready"), 1)

                def m_probs(h):
                    wait_drained(dve, f"ms{h}")
                    q = 2 * (h % 3)
                    link(v.reciprocal(sm[:, q:q + 2], sm[:, q:q + 2]))
                    p = M_p[:, h % 3, :]
                    v.tensor_scalar(p[:, 0:P], p[:, 0:P], sm[:, q:q + 1], None, ALU.mult).then_inc(S("mp_ready"), 1)
                    v.tensor_scalar(p[:, P:384], p[:, P:384], sm[:, q + 1:q + 2], None, ALU.mult)\
                        .then_inc(S("mp_ready"), 1)

                def m_o(h):
                    n = f"mo{h}"
                    await_tile(n)
                    is_drained(v.tensor_tensor(M_z[:, h, :], tile(n)[:, 0:T], M_z[:, h, :], ALU.mult), n)

                def g_low(h):
                    dve.wait_ge(S("x_high"), hi_at["g", h])
                    v.tensor_tensor(x_lo[:, h, :], M_z[:, h, :], x_hi[:, h, :].bitcast(F32), ALU.subtract)\
                        .then_inc(S("g_ready"), 1)

                for i in range(MH // 2):
                    wait_drained(dve, f"mz{i}")
                rotate_queries(0)
                for h in range(MH + 3):
                    if h % 2 == 1 and h < MH - 2:
                        rotate_queries(h // 2 + 1)
                    if h < MH:
                        m_max(h)
                    if 1 <= h <= MH:
                        m_probs(h - 1)
                    if h >= 3:
                        m_o(h - 3)
                    if h >= 5:
                        g_low(h - 5)
                for h in range(MH - 2, MH):
                    g_low(h)
                residual("mo_out")
            dve.wait_ge(S("n5_rt"), NB)
            dve.wait_ge(S("loaded_g"), 16)
            link(v.reciprocal(rs[:, 0:NB], rt[:, 0:NB]))
            for b in range(NB):
                v.scalar_tensor_tensor(out=F_out[:, b, :], in0=res[:, b, :], scalar=rs[:, b:b + 1], in1=F_g,
                                       op0=ALU.mult, op1=ALU.mult).then_inc(S("out_ready"), 1)

        @block.gpsimd
        def _(pool):
            g_ = nc.gpsimd
            if "1" in stages:
                W = UPAD + T
                for g, w in enumerate(POOL_WINDOWS):
                    wait_drained(pool, f"u{g}")
                    src, d = A_u[:, g, :], 1
                    for k in range(g + 1):
                        dst = A_pl[:, k % 2, g * W:(g + 1) * W]
                        if k > 0:
                            pool.wait_ge(S("pool_part"), g * (g + 1) // 2 + k)
                        else:
                            pool.wait_ge(S("u_zero"), 1)
                        lo = 2 * d - 1
                        m = g_.tensor_tensor(dst[:, lo:W], src[:, lo:W], src[:, lo - d:W - d], ALU.add)
                        m.then_inc(S("pool_part"), 1)
                        src, d = dst, 2 * d
                pool.wait_ge(S("qk_gain"), 8)
                for i in range(8):
                    pool.wait_ge(S("qk_recip"), i + 1)
                    g_.tensor_tensor(A_qk[:, i, :], A_qk[:, i, :], A_sq[:, i, :], ALU.mult)\
                        .then_inc(S("qk_ready"), 1)
                for j in range(KT):
                    wait_drained(pool, f"up{j}")
                    if j >= 4:
                        pool.wait_ge(S("mix_ready"), j - 3)
                    g_.tensor_tensor(A_m32[:, j % 4, :], A_gt[:, j % 2, 0:T], A_gt[:, j % 2, T:2 * T], ALU.add)\
                        .then_inc(S("mix_sum"), 1)
            if "S" in stages:
                pool.wait_ge(S("a_decay"), 5)
                for j in range(16):
                    wait_drained(pool, f"xsT{j}")
                bc = [P, SR, SP_]

                def tri_high(i):
                    g, c = divmod(i, 2)
                    if i >= 2:
                        wait_filled(pool, f"seg{i - 2}")
                    hs = slice(c * SH + g * SR, c * SH + (g + 1) * SR)
                    g_.tensor_tensor(three(S_tri[0][:, i % 2, :], P), C("upto").unsqueeze(1).to_broadcast([P, SR, P]),
                                     a_hi[:, hs].bitcast(F32).unsqueeze(2).to_broadcast([P, SR, P]), ALU.mult)\
                        .then_inc(S("tri_hi"), 1)

                tri_high(0)
                tri_high(1)
                for i in range(2 * SG):
                    g, c = divmod(i, 2)
                    xs = three(S_xs[:, c, g * 256:(g + 1) * 256], SP_)
                    if i >= 2:
                        wait_filled(pool, f"yd{i - 2}")
                    hs = slice(c * SH + g * SR, c * SH + (g + 1) * SR)
                    g_.tensor_tensor(three(S_xdt[:, i % 2, :], SP_), xs,
                                     S_dt[:, 0, hs].unsqueeze(2).to_broadcast(bc), ALU.mult)\
                        .then_inc(S("xdt_ready"), 1)
                    if c == 0:
                        pool.wait_ge(S("xdt_ready"), i + 1)
                        if g >= 1:
                            wait_filled(pool, f"st{g - 1}")
                        else:
                            pool.wait_ge(S("decay_exp"), 1)
                        g_.tensor_tensor(three(S_xde, SP_), three(S_xdt[:, i % 2, :], SP_),
                                         S_dt[:, 8, SH + g * SR:SH + (g + 1) * SR].unsqueeze(2).to_broadcast(bc),
                                         ALU.mult).then_inc(S("xde_ready"), 1)
                    if i >= 1:
                        wait_drained(pool, f"yd{i - 1}")
                    g_.tensor_tensor(three(S_xd, SP_), xs,
                                     PR("d_skip")[:, g * SR:(g + 1) * SR].unsqueeze(2).to_broadcast(bc), ALU.mult)\
                        .then_inc(S("xd_ready"), 1)
                    if i + 2 < 2 * SG:
                        tri_high(i + 2)
                pool.wait_ge(S("y_rs"), 1)
                for g in range(1, SG, 2):
                    if g == SG - 1:
                        pool.wait_ge(S("y_rs"), 2)
                    y_scale(g_, g).then_inc(S("y_odd"), 1)
            if "M" in stages:
                wait_drained(pool, "kr")
                g_.tensor_tensor(M_kr, M_rt[:, 1, 0:T], M_rt[:, 1, T:512], ALU.add).then_inc(S("krope_ready"), 1)
                for i in range(MH // 2):
                    wait_drained(pool, f"qr{i}")
                    if i >= 2:
                        wait_filled(pool, f"ms{2 * i - 3}")
                    g_.tensor_tensor(M_qr[:, i % 2, :], M_rt[:, i % 2, 0:T], M_rt[:, i % 2, T:512], ALU.add)\
                        .then_inc(S("qrope_ready"), 1)

        @block.sync
        def _(sp):
            sp.dma_start(con[:, 0:P + 1], consts[:, 0:P + 1]).then_inc(S("loaded_first"), 16)
            sp.dma_start(par[:, 0:KT], params[:, 0:KT]).then_inc(S("loaded_first"), 16)
            for b in range(NB):
                sp.dma_start(res[:, b, :], x[b * P:(b + 1) * P, :]).then_inc(S(f"loaded_x{b}"), 16)

            def load(slot, u, sem):
                sp.dma_start(ring[:, slot, :], weights[u, :, :]).then_inc(sem, 16)

            def load_e(s, u):
                sp.dma_start(slot_e(s).unsqueeze(1), weights[bass.ds(u, 1), :, :].rearrange("u p n -> p u n"))\
                    .then_inc(raw_e[s], 16)

            def slot_split(n):
                sp.wait_ge(split_lo, n)

            if "1" in stages:
                for u in range(2):
                    load(u, u, raw_a[u])
            sp.dma_start(con[:, P + 1:], consts[:, P + 1:]).then_inc(S("loaded_rest"), 16)
            sp.dma_start(par[:, KT:], params[:, KT:]).then_inc(S("loaded_rest"), 16)
            if "1" in stages:
                for u in range(2, UNITS_A):
                    if u >= RING:
                        slot_split(2 * (u - RING + 1))
                    load(u % RING, u, raw_a[u % RING])
            R2 = PER_ROUND * PAIR_UNITS
            if "E" in stages:
                for k in range(R2):
                    if k < RING and "1" in stages:
                        slot_split(2 * (UNITS_A - RING + k + 1))
                    if k == RING and "1" in stages:
                        sp.wait_ge(S("mix_ready"), KT)
                    if k == 12 and "1" in stages:
                        wait_filled(sp, "wo1_1")
                    if k >= RING_E:
                        sp.wait_ge(units_used, k - RING_E + 1)
                    s = k % RING_E
                    sp.dma_start(slot_e(s), weights[UNITS_A + k, :, :]).then_inc(raw_e[s], 16)
                with sp.Fori(0, ROUNDS - 1) as it:
                    for k in range(R2):
                        sp.wait_ge(units_used, it * R2 + (R2 + k - RING_E + 1))
                        load_e(k % RING_E, it * R2 + (UNITS_A + R2 + k))
                sp.wait_ge(pairs_known, 1)
                rounds = sp.value_load(more32[0:1, 0:1], min_val=0, max_val=MORE) + ROUNDS
                with sp.If(rounds > ROUNDS):
                    with sp.Fori(ROUNDS, rounds, ROUNDS) as first:
                        with sp.Fori(0, ROUNDS) as it:
                            for k in range(R2):
                                sp.wait_ge(units_used, (first + it) * R2 + (k - RING_E + 1))
                                load_e(k % RING_E, it * R2 + (UNITS_A + k))
            pieces_b = (PIECES_S if "S" in stages else 0) + (PIECES_M if "M" in stages else 0)
            off = UNITS_A + UNITS_E
            for u in range((pieces_b + 1) // 2):
                if u < RING and "E" in stages:
                    sp.wait_ge(units_used, rounds * R2 + (u - RING_E + 1))
                if u >= RING:
                    slot_split(first_b + 2 * (u - RING + 1))
                load(u % RING, off + u, raw_b[u % RING])
            if "M" in stages or "S" in stages:
                wait_filled(sp, "n4_T0" if "M" in stages else "yT7")
            elif "E" in stages:
                sp.wait_ge(S("sum_out"), 4)
            sp.dma_start(F_g, final_g.partition_broadcast(P)).then_inc(S("loaded_g"), 16)
            for b in range(NB):
                sp.wait_ge(S("out_ready"), b + 1)
                sp.dma_start(out[b * P:(b + 1) * P, :], F_out[:, b, :]).then_inc(S("stored"), 16)
            sp.wait_ge(S("stored"), 16 * NB)
    return nc


def pack(inp):
    f = lambda n: np.asarray(inp[n], dtype=np.float32)
    pieces = []

    def rows(w):
        return w.reshape(w.shape[0] // P, P, -1).transpose(1, 0, 2).reshape(P, -1)

    def piece(a):
        if a.shape[1] < PIECE:
            a = np.concatenate([a, np.zeros((P, PIECE - a.shape[1]), np.float32)], axis=1)
        pieces.append(a)

    def channel_pieces(w):
        for j in range(0, w.shape[1], P):
            piece(rows(w[:, j:j + P]))

    def token_pieces(w, kts):
        for k in range(0, w.shape[0], kts * P):
            piece(rows(w[k:k + kts * P]))

    w = f("w_in")[0]
    channel_pieces(w[:, 512:1536])
    token_pieces(w[:, 1536:2048], 2)
    channel_pieces(w[:, 0:512])
    channel_pieces(w[:, 2048:])
    wp, wa = f("w_pool_up")[0], f("w_attn_up")[0]
    for j in range(0, D, P):
        piece(np.concatenate([rows(wp[:, j:j + P]), rows(wa[:, j:j + P])], axis=1))
    for c in range(2):
        token_pieces(f("w_out")[0][:, c * 512:(c + 1) * 512], 2)
    before = np.stack(pieces)
    wg, wu, wd = f("w_expert_gate")[0], f("w_expert_up")[0], f("w_expert_down")[0]
    pair = [w.reshape(PAIRS, 2, D // (2 * P), 2, P, 512) for w in (wg, wu)]
    down = wd.reshape(PAIRS, 2, 2, 2, P, 2, 512)
    units = [w.transpose(0, 2, 4, 1, 3, 5).reshape(PAIRS, 4, P, UNIT) for w in pair]
    units.append(down.transpose(0, 5, 2, 4, 1, 3, 6).reshape(PAIRS, 4, P, UNIT))
    experts = np.concatenate(units, axis=1).reshape(UNITS_E, P, UNIT)

    pieces = []
    w = f("ssm_in_w_2")[0]
    piece(rows(w[:, 6144:6176]))
    channel_pieces(w[:, 4096:6144])
    channel_pieces(w[:, 2048:4096])
    for c in range(4):
        token_pieces(w[:, c * 512:(c + 1) * 512], 2)
    for c in range(2):
        token_pieces(f("ssm_out_w_2")[0][:, c * 512:(c + 1) * 512], 2)
    w = f("mla_in_w_2")[0]
    token_pieces(w[:, 0:MQL], 2)
    o = MQL + MKVL
    token_pieces(w[:, MQL:o], 4)
    kr = w[:, o:o + MR]
    swap = lambda r: np.concatenate([r[:, MR // 2:], r[:, :MR // 2]], axis=1)
    channel_pieces(np.concatenate([kr, kr, swap(kr), swap(kr)], axis=1))
    channel_pieces(w[:, o + MR:])
    w = f("mla_ukv_w_2")[0].reshape(MKVL, MH, 2, P)
    for h in range(0, MH, 4):
        piece(np.concatenate([rows(w[:, h + a, 0]) for a in range(4)], axis=1))
    for h in range(0, MH, 4):
        piece(rows(w[:, h:h + 4, 1].reshape(MKVL, -1)))
    w = f("mla_uq_w_2")[0].reshape(MQL, MH, P + MR)
    for h in range(0, MH, 2):
        r0, r1 = w[:, h, P:], w[:, h + 1, P:]
        piece(np.concatenate([rows(w[:, h, :P]), rows(w[:, h + 1, :P])], axis=1))
        piece(np.concatenate([rows(np.concatenate([r0, r1], axis=1)),
                              rows(np.concatenate([swap(r0), swap(r1)], axis=1))], axis=1))
    for c in range(2):
        token_pieces(f("mla_out_w_2")[0][:, c * 512:(c + 1) * 512], 2)
    if len(pieces) % 2:
        piece(np.zeros((P, PIECE), np.float32))
    after = np.stack(pieces)
    joined = lambda a: a.reshape(-1, 2, P, PIECE).transpose(0, 2, 1, 3).reshape(-1, P, UNIT)
    weights = np.concatenate([joined(before), experts, joined(after)])

    tiles = lambda v: v.reshape(-1, P).T
    wide = lambda v: np.broadcast_to(v.reshape(1, -1), (P, v.size))
    parts = dict(
        g1=tiles(f("norm1_g")[0]), g2=tiles(f("norm2_g")[0]), gs=tiles(f("norm_w_2")[0]), gm=tiles(f("norm_w_2")[1]),
        pool_scale=tiles(f("pool_scale")[0]), qg=np.tile(f("q_norm_g")[0], 2)[:, None],
        kg=np.tile(f("k_norm_g")[0], 2)[:, None], subln=f("subln_g")[0][:, None],
        lam=wide(np.concatenate([f(n)[0] for n in ("lambda_q1", "lambda_k1", "lambda_q2", "lambda_k2")])),
        router_b=wide(np.concatenate([f("b_router_group")[0], f("b_router_expert")[0]])),
        conv_w=f("ssm_conv_w_2")[0].T.reshape(32, P, CONV).transpose(1, 0, 2).reshape(P, -1),
        conv_b=tiles(f("ssm_conv_b_2")[0]), dt_b=wide(f("ssm_dt_bias_2")[0]), a_log=wide(f("ssm_A_log_2")[0]),
        d_skip=wide(f("ssm_D_2")[0]), ssm_g=tiles(f("ssm_norm_w_2")[0]), cq_g=tiles(f("mla_q_norm_w_2")[0]),
        ckv_g=tiles(f("mla_kv_norm_w_2")[0]),
        router_w=rows(np.concatenate([f("w_router_group")[0], f("w_router_expert")[0]], axis=1)),
        pool_w=f("pool_w")[0].transpose(1, 0, 2).reshape(P, -1))
    params = np.concatenate([parts[n].reshape(P, -1) for n in PARAM_WIDTHS], axis=1)
    assert params.shape[1] == NPARAM
    return weights, np.ascontiguousarray(params)


def kernel(**inputs):
    import concourse.bacc as bacc
    from concourse.bass_utils import run_bass_kernel_spmd

    nc = bacc.Bacc("TRN2", target_bir_lowering=False, num_devices=1, dynamic_dma_scratch_size=1024)
    weights, params = pack(inputs)
    cmap, consts = constants()
    arrays = {"weights_dram": weights, "params_dram": params, "consts_dram": consts,
              "x_dram": np.ascontiguousarray(np.asarray(inputs["x"], dtype=np.float32)[0]),
              "final_g_dram": np.asarray(inputs["final_norm_w_2"], dtype=np.float32)}
    aps = [nc.dram_tensor(n, a.shape, F32, kind="ExternalInput").ap() for n, a in arrays.items()]
    out = nc.dram_tensor("out_dram", (T, D), F32, kind="ExternalOutput").ap()
    program(nc, *aps, out, cmap)
    r = run_bass_kernel_spmd(nc, [arrays], core_ids=[0])
    return np.asarray(r.results[0]["out_dram"]).reshape(1, T, D)
```
